# Optimizing a Trainium2 kernel written in Bass

```python
import jax, jax.numpy as jnp
from jax import lax
import numpy as np

D_MODEL = 2048
BATCH = 1
SEQ = 256
DEPTH = 2

N_HEADS_MLA = 8
QK_NOPE_DIM = 128
QK_ROPE_DIM = 64
V_HEAD_DIM = 128
Q_LORA_RANK = 512
KV_LORA_RANK = 256
D_MLA = N_HEADS_MLA * V_HEAD_DIM
ROPE_THETA = 10000.0
Q_BLOCK = 128
POOL_WINDOWS = (2, 4, 8, 16)
N_POOL_GROUPS = 4
POOL_GROUP_DIM = 128
D_POOL = N_POOL_GROUPS * POOL_GROUP_DIM
N_CONV_HEADS = 4
CONV_HEAD_DIM = 128
D_CONV = N_CONV_HEADS * CONV_HEAD_DIM
CONV_WIDTH = 3
D_MIX = D_MLA + D_POOL + D_CONV
SPLIT_SIZES = (Q_LORA_RANK, KV_LORA_RANK, QK_ROPE_DIM, D_MLA, D_POOL, D_POOL, D_CONV, D_CONV, D_CONV, D_CONV)
D_IN_PROJ = sum(SPLIT_SIZES)
LN_EPS = 1e-5
RMS_EPS = 1e-6
DEEPNORM_ALPHA = (2 * DEPTH) ** 0.25
DEEPNORM_BETA = (8 * DEPTH) ** -0.25


def layernorm(x, g, b):
    xf = x.astype(jnp.float32)
    mu = jnp.mean(xf, axis=-1, keepdims=True)
    var = jnp.mean(jnp.square(xf - mu), axis=-1, keepdims=True)
    y = (xf - mu) * lax.rsqrt(var + LN_EPS) * g.astype(jnp.float32) + b.astype(jnp.float32)
    return y.astype(x.dtype)

def rmsnorm(x, g):
    xf = x.astype(jnp.float32)
    y = xf * lax.rsqrt(jnp.mean(jnp.square(xf), axis=-1, keepdims=True) + RMS_EPS) * g.astype(jnp.float32)
    return y.astype(x.dtype)

def apply_rope(x, cos, sin):
    half = QK_ROPE_DIM // 2
    xf = x.astype(jnp.float32)
    x1, x2 = xf[..., :half], xf[..., half:]
    return jnp.concatenate([x1 * cos - x2 * sin, x2 * cos + x1 * sin], axis=-1).astype(x.dtype)

def mla_mixer(q_lat, kv_lat, k_rope, positions, q_norm_g, kv_norm_g, w_uq, w_ukv):
    Bn, S, _ = q_lat.shape
    H = N_HEADS_MLA
    q = (rmsnorm(q_lat, q_norm_g) @ w_uq).reshape(Bn, S, H, QK_NOPE_DIM + QK_ROPE_DIM)
    q_nope, q_rope = q[..., :QK_NOPE_DIM], q[..., QK_NOPE_DIM:]
    kv = (rmsnorm(kv_lat, kv_norm_g) @ w_ukv).reshape(Bn, S, H, QK_NOPE_DIM + V_HEAD_DIM)
    k_nope, v = kv[..., :QK_NOPE_DIM], kv[..., QK_NOPE_DIM:]
    half = QK_ROPE_DIM // 2
    inv_freq = ROPE_THETA ** (-jnp.arange(half, dtype=jnp.float32) / half)
    ang = positions.astype(jnp.float32)[..., None] * inv_freq
    cos, sin = jnp.cos(ang), jnp.sin(ang)
    q_rope = apply_rope(q_rope, cos[:, :, None, :], sin[:, :, None, :])
    k_rope = apply_rope(k_rope, cos, sin)
    scale = (QK_NOPE_DIM + QK_ROPE_DIM) ** -0.5
    nb = S // Q_BLOCK
    qn_blocks = q_nope.reshape(Bn, nb, Q_BLOCK, H, QK_NOPE_DIM).transpose(1, 0, 2, 3, 4)
    qr_blocks = q_rope.reshape(Bn, nb, Q_BLOCK, H, QK_ROPE_DIM).transpose(1, 0, 2, 3, 4)
    key_idx = jnp.arange(S)

    def attend(args):
        qn, qr, blk = args
        s = (jnp.einsum('bqhd,bkhd->bhqk', qn, k_nope).astype(jnp.float32)
             + jnp.einsum('bqhr,bkr->bhqk', qr, k_rope).astype(jnp.float32)) * scale
        q_idx = blk * Q_BLOCK + jnp.arange(Q_BLOCK)
        causal = key_idx[None, :] <= q_idx[:, None]
        s = jnp.where(causal[None, None], s, -jnp.inf)
        p = jax.nn.softmax(s, axis=-1).astype(v.dtype)
        return jnp.einsum('bhqk,bkhd->bqhd', p, v)

    out = lax.map(attend, (qn_blocks, qr_blocks, jnp.arange(nb)))
    return out.transpose(1, 0, 2, 3, 4).reshape(Bn, S, D_MLA)

def pool_mixer(h, w_pool, pool_scale):
    Bn, S, _ = h.shape
    hg = h.reshape(Bn, S, N_POOL_GROUPS, POOL_GROUP_DIM).astype(jnp.float32)
    cs = jnp.cumsum(hg, axis=1)
    t1 = jnp.arange(1, S + 1, dtype=jnp.float32)
    means = []
    for g, w in enumerate(POOL_WINDOWS):
        c = cs[:, :, g]
        lag = jnp.pad(c, ((0, 0), (w, 0), (0, 0)))[:, :S]
        means.append((c - lag) / jnp.minimum(t1, float(w))[None, :, None])
    pooled = (jnp.stack(means, axis=2) - hg).astype(h.dtype)
    y = jnp.einsum('bsgc,gcd->bsgd', pooled, w_pool).reshape(Bn, S, D_POOL)
    return y * pool_scale

def conv_mixer(h, b_gate, c_gate, conv_w):
    u = c_gate * h
    y = lax.conv_general_dilated(u, conv_w[:, None, :], window_strides=(1,),
                                 padding=((CONV_WIDTH - 1, 0),),
                                 dimension_numbers=('NWC', 'WIO', 'NWC'),
                                 feature_group_count=D_CONV)
    return b_gate * y

def hybrid_layer(x, positions, w_in, q_norm_g, kv_norm_g, w_uq, w_ukv, w_pool, pool_scale,
                 conv_w, w_out, b_out, ln_g, ln_b):
    split_idx = np.cumsum(SPLIT_SIZES)[:-1].tolist()
    proj = x @ w_in
    (q_lat, kv_lat, k_rope, g_mla, p_in, g_pool, c_h, c_b, c_c, g_conv) = jnp.split(proj, split_idx, axis=-1)
    y_mla = mla_mixer(q_lat, kv_lat, k_rope, positions, q_norm_g, kv_norm_g, w_uq, w_ukv) * jax.nn.silu(g_mla)
    y_pool = pool_mixer(p_in, w_pool, pool_scale) * jax.nn.silu(g_pool)
    y_conv = conv_mixer(c_h, c_b, c_c, conv_w) * jax.nn.silu(g_conv)
    mix = jnp.concatenate([y_mla, y_pool, y_conv], axis=-1)
    out = mix @ w_out + b_out
    return layernorm(DEEPNORM_ALPHA * x + out, ln_g, ln_b)

def first_inputs(seed: int = 0) -> dict:
    key = jax.random.key(seed)
    ks = jax.random.split(key, 16)
    f32 = jnp.float32
    nrm = lambda k, shape, s: jax.random.normal(k, shape, f32) * s
    x = jax.random.normal(ks[0], (BATCH, SEQ, D_MODEL), f32)
    positions = jnp.broadcast_to(jnp.arange(SEQ, dtype=jnp.int32), (BATCH, SEQ))
    return {
        "x": x,
        "positions": positions,
        "emb_ln_g": 1.0 + nrm(ks[1], (D_MODEL,), 0.01),
        "emb_ln_b": nrm(ks[2], (D_MODEL,), 0.01),
        "w_in": nrm(ks[3], (DEPTH, D_MODEL, D_IN_PROJ), D_MODEL ** -0.5),
        "q_norm_g": 1.0 + nrm(ks[4], (DEPTH, Q_LORA_RANK), 0.01),
        "kv_norm_g": 1.0 + nrm(ks[5], (DEPTH, KV_LORA_RANK), 0.01),
        "w_uq": nrm(ks[6], (DEPTH, Q_LORA_RANK, N_HEADS_MLA * (QK_NOPE_DIM + QK_ROPE_DIM)), Q_LORA_RANK ** -0.5),
        "w_ukv": nrm(ks[7], (DEPTH, KV_LORA_RANK, N_HEADS_MLA * (QK_NOPE_DIM + V_HEAD_DIM)), KV_LORA_RANK ** -0.5),
        "w_pool": nrm(ks[8], (DEPTH, N_POOL_GROUPS, POOL_GROUP_DIM, POOL_GROUP_DIM), POOL_GROUP_DIM ** -0.5),
        "pool_scale": 1.0 + nrm(ks[9], (DEPTH, D_POOL), 0.1),
        "conv_w": nrm(ks[10], (DEPTH, CONV_WIDTH, D_CONV), CONV_WIDTH ** -0.5),
        "w_out": nrm(ks[11], (DEPTH, D_MIX, D_MODEL), DEEPNORM_BETA * D_MIX ** -0.5),
        "b_out": nrm(ks[12], (DEPTH, D_MODEL), 0.01),
        "ln_g": 1.0 + nrm(ks[13], (DEPTH, D_MODEL), 0.01),
        "ln_b": nrm(ks[14], (DEPTH, D_MODEL), 0.01),
    }

def first_block(x, positions, emb_ln_g, emb_ln_b, w_in, q_norm_g, kv_norm_g, w_uq, w_ukv, w_pool,
              pool_scale, conv_w, w_out, b_out, ln_g, ln_b):
    h = layernorm(x, emb_ln_g, emb_ln_b)
    for l in range(DEPTH):
        h = hybrid_layer(h, positions, w_in[l], q_norm_g[l], kv_norm_g[l], w_uq[l], w_ukv[l], w_pool[l],
                         pool_scale[l], conv_w[l], w_out[l], b_out[l], ln_g[l], ln_b[l])
    return h


DEPTH_2 = 1

HEAD_DIM = D_MODEL // 16
FOX_HEADS = 6
SWA_HEADS = 6
SWA_KV_HEADS = 2
MEM_HEADS = 4
MEM_LEN = 256
WINDOW = 128
D_FF = 5632
EPS = 1e-6
NEG_INF = -1e30

FOX_W = FOX_HEADS * HEAD_DIM
SWA_Q_W = SWA_HEADS * HEAD_DIM
SWA_KV_W = SWA_KV_HEADS * HEAD_DIM
MEM_W = MEM_HEADS * HEAD_DIM
MIX_WIDTH = FOX_W + SWA_Q_W + MEM_W
IN_SPLITS = [FOX_W, FOX_W, FOX_W, FOX_HEADS, SWA_Q_W, SWA_KV_W, SWA_KV_W, MEM_W]
IN_WIDTH = int(sum(IN_SPLITS))
IN_CUTS = [int(c) for c in np.cumsum(IN_SPLITS)[:-1]]


def rms_norm(x, g):
    xf = x.astype(jnp.float32)
    y = xf * lax.rsqrt(jnp.mean(xf * xf, axis=-1, keepdims=True) + EPS)
    return (y * g.astype(jnp.float32)).astype(x.dtype)

def swiglu(x, w_gate, w_up, w_down):
    return (jax.nn.silu(x @ w_gate) * (x @ w_up)) @ w_down

def alibi_slopes(n):
    return jnp.asarray(2.0 ** (-8.0 * np.arange(1, n + 1) / n), dtype=jnp.float32)

def forgetting_attention(q, k, v, log_f):
    B, S, H, D = q.shape
    nb = S // Q_BLOCK
    scale = D ** -0.5
    c = jnp.cumsum(log_f, axis=1)
    c_k = c.transpose(0, 2, 1)
    kf = k.astype(jnp.float32)
    vf = v.astype(jnp.float32)
    qb = q.astype(jnp.float32).reshape(B, nb, Q_BLOCK, H, D).transpose(1, 0, 2, 3, 4)
    cb = c.reshape(B, nb, Q_BLOCK, H).transpose(1, 0, 3, 2)
    kpos = jnp.arange(S)

    def block(args):
        qi, ci, i = args
        qpos = i * Q_BLOCK + jnp.arange(Q_BLOCK)
        s = jnp.einsum('bqhd,bkhd->bhqk', qi, kf) * scale
        s = s + ci[..., None] - c_k[:, :, None, :]
        causal = kpos[None, :] <= qpos[:, None]
        s = jnp.where(causal, s, NEG_INF)
        p = jax.nn.softmax(s, axis=-1)
        return jnp.einsum('bhqk,bkhd->bqhd', p, vf)

    out = lax.map(block, (qb, cb, jnp.arange(nb)))
    return out.transpose(1, 0, 2, 3, 4).reshape(B, S, H, D).astype(q.dtype)

def sliding_window_sink_attention(q, k, v, sinks, slopes):
    B, S, Hq, D = q.shape
    Hkv = k.shape[2]
    G = Hq // Hkv
    nb = S // WINDOW
    scale = D ** -0.5
    qb = q.astype(jnp.float32).reshape(B, nb, WINDOW, Hkv, G, D)

    def band(t):
        tb = t.astype(jnp.float32).reshape(B, nb, WINDOW, Hkv, D)
        prev = jnp.pad(tb[:, :-1], ((0, 0), (1, 0), (0, 0), (0, 0), (0, 0)))
        return jnp.concatenate([prev, tb], axis=2)

    kb, vb = band(k), band(v)
    s = jnp.einsum('bnqhgd,bnkhd->bnhgqk', qb, kb) * scale
    r = jnp.arange(WINDOW)[:, None]
    j = jnp.arange(2 * WINDOW)[None, :]
    dist = WINDOW + r - j
    in_window = (dist >= 0) & (dist < WINDOW)
    valid = in_window[None] & ((jnp.arange(nb)[:, None, None] > 0) | (j[None] >= WINDOW))
    alibi = -slopes.astype(jnp.float32).reshape(Hkv, G)[:, :, None, None] * dist.astype(jnp.float32)
    s = s + alibi[None, None]
    s = jnp.where(valid[None, :, None, None], s, NEG_INF)
    sink = jnp.broadcast_to(
        sinks.astype(jnp.float32).reshape(Hkv, G)[None, None, :, :, None, None],
        s.shape[:-1] + (1,))
    p = jax.nn.softmax(jnp.concatenate([s, sink], axis=-1), axis=-1)[..., :-1]
    out = jnp.einsum('bnhgqk,bnkhd->bnqhgd', p, vb)
    return out.reshape(B, S, Hq, D).astype(q.dtype)

def memory_attention(q, mk, mv):
    scale = q.shape[-1] ** -0.5
    s = jnp.einsum('bqhd,bmhd->bhqm', q.astype(jnp.float32), mk.astype(jnp.float32)) * scale
    p = jax.nn.softmax(s, axis=-1)
    return jnp.einsum('bhqm,bmhd->bqhd', p, mv.astype(jnp.float32)).astype(q.dtype)

def second_inputs(seed: int = 0) -> dict:
    key = jax.random.key(seed)
    ks = jax.random.split(key, 32)
    f32 = jnp.float32

    def w(k, shape, fan_in):
        return jax.random.normal(k, shape, f32) * (fan_in ** -0.5)

    def gain(k, shape):
        return 1.0 + 0.02 * jax.random.normal(k, shape, f32)

    L = DEPTH_2
    return {
        "x": jax.random.normal(ks[0], (BATCH, SEQ, D_MODEL), f32),
        "mem": jax.random.normal(ks[1], (BATCH, MEM_LEN, D_MODEL), f32),
        "ffn1_norm": gain(ks[2], (L, D_MODEL)),
        "ffn1_gate": w(ks[3], (L, D_MODEL, D_FF), D_MODEL),
        "ffn1_up": w(ks[4], (L, D_MODEL, D_FF), D_MODEL),
        "ffn1_down": w(ks[5], (L, D_FF, D_MODEL), D_FF),
        "mix_norm": gain(ks[6], (L, D_MODEL)),
        "mem_norm": gain(ks[7], (L, D_MODEL)),
        "w_in": w(ks[8], (L, D_MODEL, IN_WIDTH), D_MODEL),
        "forget_bias": jax.random.uniform(ks[9], (L, FOX_HEADS), f32, 1.0, 4.0),
        "w_mem_k": w(ks[10], (L, D_MODEL, MEM_W), D_MODEL),
        "w_mem_v": w(ks[11], (L, D_MODEL, MEM_W), D_MODEL),
        "fox_q_gain": gain(ks[12], (L, HEAD_DIM)),
        "fox_k_gain": gain(ks[13], (L, HEAD_DIM)),
        "swa_q_gain": gain(ks[14], (L, HEAD_DIM)),
        "swa_k_gain": gain(ks[15], (L, HEAD_DIM)),
        "swa_sinks": jax.random.normal(ks[16], (L, SWA_HEADS), f32),
        "mem_q_gain": gain(ks[17], (L, HEAD_DIM)),
        "mem_k_gain": gain(ks[18], (L, HEAD_DIM)),
        "w_out": w(ks[19], (L, MIX_WIDTH, D_MODEL), MIX_WIDTH),
        "ffn2_norm": gain(ks[20], (L, D_MODEL)),
        "ffn2_gate": w(ks[21], (L, D_MODEL, D_FF), D_MODEL),
        "ffn2_up": w(ks[22], (L, D_MODEL, D_FF), D_MODEL),
        "ffn2_down": w(ks[23], (L, D_FF, D_MODEL), D_FF),
    }

def second_block(x, mem, ffn1_norm, ffn1_gate, ffn1_up, ffn1_down, mix_norm, mem_norm, w_in,
              forget_bias, w_mem_k, w_mem_v, fox_q_gain, fox_k_gain, swa_q_gain, swa_k_gain,
              swa_sinks, mem_q_gain, mem_k_gain, w_out, ffn2_norm, ffn2_gate, ffn2_up, ffn2_down):
    B, S, _ = x.shape
    M = mem.shape[1]
    slopes = alibi_slopes(SWA_HEADS).astype(x.dtype)
    for l in range(DEPTH_2):
        x = x + 0.5 * swiglu(rms_norm(x, ffn1_norm[l]), ffn1_gate[l], ffn1_up[l], ffn1_down[l])

        h = rms_norm(x, mix_norm[l])
        proj = h @ w_in[l]
        fq, fk, fv, f_logit, sq, sk, sv, mq = jnp.split(proj, IN_CUTS, axis=-1)

        fq = rms_norm(fq.reshape(B, S, FOX_HEADS, HEAD_DIM), fox_q_gain[l])
        fk = rms_norm(fk.reshape(B, S, FOX_HEADS, HEAD_DIM), fox_k_gain[l])
        fv = fv.reshape(B, S, FOX_HEADS, HEAD_DIM)
        log_f = jax.nn.log_sigmoid(f_logit.astype(jnp.float32) + forget_bias[l].astype(jnp.float32))
        out_a = forgetting_attention(fq, fk, fv, log_f)

        sq = rms_norm(sq.reshape(B, S, SWA_HEADS, HEAD_DIM), swa_q_gain[l])
        sk = rms_norm(sk.reshape(B, S, SWA_KV_HEADS, HEAD_DIM), swa_k_gain[l])
        sv = sv.reshape(B, S, SWA_KV_HEADS, HEAD_DIM)
        out_b = sliding_window_sink_attention(sq, sk, sv, swa_sinks[l], slopes)

        mn = rms_norm(mem, mem_norm[l])
        mk = rms_norm((mn @ w_mem_k[l]).reshape(B, M, MEM_HEADS, HEAD_DIM), mem_k_gain[l])
        mv = (mn @ w_mem_v[l]).reshape(B, M, MEM_HEADS, HEAD_DIM)
        mq = rms_norm(mq.reshape(B, S, MEM_HEADS, HEAD_DIM), mem_q_gain[l])
        out_c = memory_attention(mq, mk, mv)

        mixed = jnp.concatenate([out_a.reshape(B, S, FOX_W), out_b.reshape(B, S, SWA_Q_W),
                                 out_c.reshape(B, S, MEM_W)], axis=-1)
        x = x + mixed @ w_out[l]

        x = x + 0.5 * swiglu(rms_norm(x, ffn2_norm[l]), ffn2_gate[l], ffn2_up[l], ffn2_down[l])
    return x


def setup_inputs(seed=0):
    out = dict(first_inputs(seed))
    for name, value in second_inputs(seed + 1).items():
        if name != "x":
            out[name + "_2"] = value
    return out


def reference(
    x, positions, emb_ln_g, emb_ln_b, w_in, q_norm_g, kv_norm_g, w_uq, w_ukv, w_pool,
    pool_scale, conv_w, w_out, b_out, ln_g, ln_b, mem_2, ffn1_norm_2, ffn1_gate_2, ffn1_up_2,
    ffn1_down_2, mix_norm_2, mem_norm_2, w_in_2, forget_bias_2, w_mem_k_2, w_mem_v_2,
    fox_q_gain_2, fox_k_gain_2, swa_q_gain_2, swa_k_gain_2, swa_sinks_2, mem_q_gain_2,
    mem_k_gain_2, w_out_2, ffn2_norm_2, ffn2_gate_2, ffn2_up_2, ffn2_down_2,
):
    x = first_block(
        x, positions, emb_ln_g, emb_ln_b, w_in, q_norm_g, kv_norm_g, w_uq, w_ukv, w_pool,
        pool_scale, conv_w, w_out, b_out, ln_g, ln_b,
    )
    return second_block(
        x, mem_2, ffn1_norm_2, ffn1_gate_2, ffn1_up_2, ffn1_down_2, mix_norm_2, mem_norm_2,
        w_in_2, forget_bias_2, w_mem_k_2, w_mem_v_2, fox_q_gain_2, fox_k_gain_2, swa_q_gain_2,
        swa_k_gain_2, swa_sinks_2, mem_q_gain_2, mem_k_gain_2, w_out_2, ffn2_norm_2,
        ffn2_gate_2, ffn2_up_2, ffn2_down_2,
    )


_drawn_inputs = setup_inputs


def setup_inputs(seed=0):
    import zlib

    import numpy as np

    out = dict(_drawn_inputs(seed))
    spreads = {}
    factors = {'emb_ln_g': 4.604,
     'emb_ln_b': 4.037,
     'q_norm_g': 8.0,
     'kv_norm_g': 8.0,
     'pool_scale': 3.94,
     'b_out': 18.048,
     'ln_g': 3.582,
     'ln_b': 2.944,
     'ffn1_norm_2': 6.46,
     'mix_norm_2': 6.278,
     'mem_norm_2': 8.0,
     'fox_q_gain_2': 8.0,
     'fox_k_gain_2': 8.0,
     'swa_q_gain_2': 8.0,
     'swa_k_gain_2': 8.0,
     'swa_sinks_2': 31.352,
     'mem_q_gain_2': 8.0,
     'mem_k_gain_2': 8.0,
     'ffn2_norm_2': 7.394}
    for name, (base, spread) in spreads.items():
        noise = np.random.default_rng([zlib.crc32(name.encode()), seed]).standard_normal(out[name].shape)
        drawn = base * np.exp(spread * noise) if base else spread * noise
        out[name] = __import__('jax').numpy.asarray(drawn.astype(out[name].dtype))
    for name, factor in factors.items():
        out[name] = (out[name] * factor).astype(out[name].dtype)
    return out
```

```python
from contextlib import ExitStack

import numpy as np

import concourse.bass as bass
from concourse import mybir

F32 = mybir.dt.float32
F32R = mybir.dt.float32r
I32 = mybir.dt.int32
ALU = mybir.AluOpType
ACT = mybir.ActivationFunctionType
AX = mybir.AxisListType

P = 128
D = 2048
S = 256
KT = D // P
TB = S // P
DEPTH = 2
HEADS = 8
ROPE = 64
QLAT, KVLAT = 512, 256
KQ, KKV = QLAT // P, KVLAT // P
GROUPS = 4
WINDOWS = (2, 4, 8, 16)
FOX, SWA, SWA_KV, MEM = 6, 6, 2, 4
SWA_WINDOW = 128
FF = 5632
FT = FF // P
CHUNKS = 2
CT = FT // CHUNKS
HALF = CT // 2
LN_EPS, RMS_EPS = 1e-5, 1e-6
ALPHA = (2 * DEPTH) ** 0.25
MLA_SCALE = (128 + ROPE) ** -0.5
HEAD_SCALE = 128 ** -0.5
NEG = -1e30
FAR = 1e32
INV_2PI = float(1 / (2 * np.pi))
MAGIC = 1.5 * 2.0 ** 23
PI_A = 6.28125
PI_B = float(np.float32(np.round((2 * np.pi - PI_A) * 2 ** 20) / 2 ** 20))
PI_C = float(2 * np.pi - PI_A - PI_B)
PI_IN = float(np.nextafter(np.float32(np.pi), np.float32(0)))

COLUMNS, AT = [], {}


def _column(name, width):
    AT[name] = (sum(w for _, w in COLUMNS), width)
    COLUMNS.append((name, width))


for _name, _width in (
        ("emb_g", KT), ("emb_b", KT), ("ffn1_g", KT), ("mix_g", KT), ("mem_g", KT), ("ffn2_g", KT),
        ("ln_g", DEPTH * KT), ("ln_b", DEPTH * KT), ("b_out", DEPTH * KT),
        ("q_g", DEPTH * KQ), ("kv_g", DEPTH * KKV), ("pool_s", DEPTH * GROUPS), ("conv", DEPTH * 3 * GROUPS),
        ("fox_q", 1), ("fox_k", 1), ("swa_q", 1), ("swa_k", 1), ("mem_q", 1), ("mem_k", 1),
        ("forget", FOX), ("sinks", SWA), ("inv_freq", 1), ("count", max(WINDOWS)),
        ("ident", P), ("ones", P), ("upto", TB * S), ("causal", TB * S), ("dist", TB * S)):
    _column(_name, _width)
NPAR = sum(w for _, w in COLUMNS)


class Region:
    def __init__(self, name, slabs, pieces, tiles, groups):
        self.name, self.n, self.pieces, self.tiles, self.groups = name, slabs, pieces, tiles, groups
        self.blocks = sum(pieces)


def plan():
    regions = [Region("mem_k", 4, (8, 8), 4, 2), Region("mem_v", 4, (8, 8), TB, 2)]
    for layer in range(DEPTH):
        regions += [
            Region(f"in_a{layer}", 16, (8, 8), 16, 2), Region(f"uq{layer}", 4, (4, 8), 12, 3),
            Region(f"uk{layer}", 1, (8, 8), 8, 8), Region(f"uv{layer}", 2, (4, 4), 2 * TB, 2),
            Region(f"in_b{layer}", 24, (8, 8), 24, 2), Region(f"pool{layer}", 1, (2, 2), 4, 4),
            Region(f"out{layer}", KT, (8, 8), KT, 2)]
    for part in (1, 2):
        if part == 2:
            regions += [Region("nat", 8, (8, 8), 2 * TB, 2), Region("heads", 24, (8, 8), 24, 2),
                        Region("mixout", KT, (8, 8), KT, 2)]
        for c in range(CHUNKS):
            regions += [Region(f"up{part}{c}", 2 * CT, (8, 8), 2 * CT, 2),
                        Region(f"down{part}{c}", 2 * KT, (6, 5), KT, 2)]
    s = t = g = pairs = 0
    used = {}
    for r in regions:
        r.s0, r.t0, r.g0 = s, t, g
        s, t, g = s + r.n, t + r.tiles, g + r.n * r.groups
        r.kind = next((k for n, k in (("up", "tile"), ("down", "down"), ("uq", "uq"), ("uk", "uk"), ("uv", "uv"),
                                      ("pool", "pool"), ("mem_v", "natural"), ("nat", "natural"))
                       if r.name.startswith(n)), "tile")
        r.layer = int(r.name[-1]) if r.name[-1].isdigit() else 0
        r.array = {"in_": "w_in", "uq": "w_uq", "uk": "w_uk", "uv": "w_uv", "pool": "w_pool", "out": "w_out",
                   "mem_k": "w_memk", "mem_v": "w_memv", "nat": "w_nat", "heads": "w_heads", "mixout": "w_mixout",
                   "up1": "w_up1", "up2": "w_up2", "down1": "w_down1", "down2": "w_down2"}[
                       next(n for n in ("in_", "uq", "uk", "uv", "pool", "out", "mem_k", "mem_v", "nat", "heads",
                                        "mixout", "up1", "up2", "down1", "down2") if r.name.startswith(n))]
        r.a0 = used.get(r.array, 0)
        used[r.array] = r.a0 + r.n
        r.looped = r.name.startswith(("up", "down"))
        r.first = 4 if r.name in ("up10", "up20") else 0
        if r.looped:
            assert r.s0 % 4 == 0 and r.t0 % 2 == 0
        r.pair0 = pairs
        if r.name.startswith("up"):
            pairs += r.n // 2
        r.hidden0 = pairs - CT
    return regions


REGIONS = plan()
REG = {r.name: r for r in REGIONS}
ORDER = [r.name for r in REGIONS]
SLABS = REGIONS[-1].s0 + REGIONS[-1].n
GROUPS_ALL = REGIONS[-1].g0 + REGIONS[-1].n * REGIONS[-1].groups
RAW = 4
SPLIT = 2


def region_of(s):
    return next(r for r in REGIONS if r.s0 <= s < r.s0 + r.n)


def released(s, piece):
    r = region_of(s)
    at = r.g0 + (s - r.s0) * r.groups
    if r.name[:2] == "uv" or piece == 1:
        return at + r.groups
    return at + {2: 1, 3: 1, 8: 4, 4: 2}[r.groups]


NORMS = ([("mem", False, True), ("emb", True, True)]
         + [(f"ln{layer}", True, layer < DEPTH - 1) for layer in range(DEPTH)]
         + [("ffn1", False, True), ("mix", False, True), ("ffn2", False, True)])
NORM = {}
for _i, (_n, _m, _s) in enumerate(NORMS):
    NORM[_n] = dict(i=_i, mean=_m, split=_s, means=sum(x[1] for x in NORMS[:_i]), splits=sum(x[2] for x in NORMS[:_i]))

MEM_STEPS = {("mem_k", 2): [("square", 0)], ("mem_k", 3): [("headnorm", 0)],
             ("mem_v", 0): [("square", 1)], ("mem_v", 1): [("headnorm", 1)]}


def layer_steps(layer):
    steps = {}

    def put(slot, *step):
        for name, first in (("in_a", 0), ("uq", 16), ("uk", 20), ("uv", 21), ("in_b", 23), ("pool", 47)):
            r = REG[f"{name}{layer}"]
            if first <= slot < first + r.n:
                steps.setdefault((r.name, slot - first), []).append(step)

    put(8, "lat_square", layer)
    put(9, "lat_scale", layer)
    put(10, "lat_split", layer)
    put(11, "rope_k", layer)
    put(20, "rope_q", layer)
    for j in range(HEADS):
        put(9 + j, "silu", 16 * layer + j, j)
    for h in range(HEADS):
        put(23 + 3 * h, "scores", layer * HEADS + h)
        put(24 + 3 * h, "turn", layer * HEADS + h)
        put(25 + 3 * h, "mixv", layer * HEADS + h)
    for g in range(GROUPS):
        put(27 + 6 * g, "silu", 16 * layer + 8 + 2 * g, 12 + g)
        put(27 + 6 * g, "conv", layer, g)
        put(28 + 6 * g, "pool", layer, g)
        put(29 + 6 * g, "silu", 16 * layer + 9 + 2 * g, 8 + g)
    return steps


MLA_ALL = DEPTH * HEADS
FOX0, SWA0, MEM0 = 4, 10, 0
PAIRS = ["mem_q", "mem_q", "fox_k", "fox_q", "fox_k", "fox_q", "fox_k", "fox_q", "swa_k", "swa_q", "swa_q", "swa_q"]


def mix_steps():
    steps = {}

    def put(slot, *step):
        where = ("nat", slot) if slot < 8 else ("heads", slot - 8) if slot < 32 else ("after", slot - 32)
        steps.setdefault(where, []).append(step)

    def head(slot, n):
        put(slot, "scores", MLA_ALL + n)
        put(slot + 1, "turn", MLA_ALL + n)
        put(slot + 2, "mixv", MLA_ALL + n)

    put(0, "forget")
    for h in range(FOX):
        put(1 + h, "decay", h)
    for n in range(4):
        head(12 + n, n)
    for n in range(FOX):
        head(18 + 4 * (n // 2) + n % 2, 4 + n)
    for n in range(SWA):
        head(30 + n, 10 + n)
    for p in range(len(PAIRS)):
        put(8 + 2 * p + 2, "square", 2 + p)
        put(8 + 2 * p + 3, "headnorm", 2 + p)
    return steps


def in_order(steps):
    rank = {"mixv": 0, "turn": 1, "silu": 2, "square": 3, "headnorm": 3}
    return {k: sorted(v, key=lambda x: rank.get(x[0], 4)) for k, v in steps.items()}


STEPS = dict(MEM_STEPS)
for _l in range(DEPTH):
    STEPS.update(layer_steps(_l))
STEPS.update(mix_steps())
STEPS = in_order(STEPS)
AFTER = max(k[1] for k in STEPS if k[0] == "after") + 1


def build(nc, t):
    with ExitStack() as ctx:
        cursor = [(nc.sbuf_base + 31) // 32 * 32]

        def at(name, shape, dt, offset=None):
            size = int(np.prod(shape[1:])) * 4
            if offset is None:
                offset = cursor[0]
                cursor[0] += (size + 31) // 32 * 32
            return nc.alloc_sbuf_tensor_at(name, shape, dt, offset=offset)

        raw = at("raw", [P, RAW, 16 * P], F32)
        high = at("high", [P, SPLIT, 16 * P], F32R)
        low = at("low", [P, SPLIT, 16 * P], F32R)
        xs = at("xs", [P, KT, 2 * S], F32R)
        x = at("x", [P, KT, S], F32)
        memk = at("memk", [P, MEM, S], F32)
        memv = at("memv", [P, TB, MEM * P], F32)
        work = cursor[0]
        cursor[0] += 63488
        KB = 1024
        square = at("square", [P, KT, S], F32, work)
        normed = at("normed", [P, KT, S], F32, work + 16 * KB)
        memx = at("memx", [P, KT, S], F32, work + 32 * KB)
        hidden = at("hidden", [P, CT, 2 * S], F32R, work)
        lat = at("lat", [P, 8, S], F32, work)
        v_mla = at("v_mla", [P, TB, HEADS * P], F32, work)
        lats = at("lats", [P, KQ + KKV, 2 * S], F32R, work + 8 * KB)
        pooled = at("pooled", [P, GROUPS, 2 * S], F32R, work + 8 * KB)
        rope_t = at("rope_t", [P, 4, TB, S], F32, work + 8 * KB)
        branch = at("branch", [P, 8, S], F32, work + 16 * KB)
        q = at("q", [P, 12, S], F32, work + 24 * KB)
        lat_sq = at("lat_sq", [P, 6, S], F32, work + 24 * KB)
        rope_u = at("rope_u", [P, 4, S], F32, work + 30 * KB)
        kn = at("kn", [P, HEADS, S], F32, work + 36 * KB)
        kr = at("kr", [P, 2, S], F32, work + 44 * KB)
        mix = at("mix", [P, KT, S], F32, work + 46 * KB)
        feat = at("feat", [P, 24, S], F32, work)
        v_nat = at("v_nat", [P, TB, (FOX + SWA_KV) * P], F32, work + 24 * KB)
        decay = at("decay", [P, FOX, S], F32, work + 32 * KB)
        lf_rows = at("lf_rows", [P, FOX, TB, P], F32, work + 38 * KB)
        lowsum = at("lowsum", [P, 2, S], F32)
        gate = at("gate", [P, S], F32)
        silu_g = at("silu_g", [P, S], F32)
        up = at("up", [P, S], F32)
        prod = at("prod", [P, S], F32)
        prob = at("prob", [P, 2, TB, S], F32)
        turned = at("turned", [P, TB, S], F32)
        scale_a = at("scale_a", [P, 2 * S], F32)
        scale_b = at("scale_b", [P, 2 * S], F32)
        mean = at("mean", [P, S], F32)
        cos = at("cos", [P, S], F32)
        sin = at("sin", [P, S], F32)
        par = at("par", [P, NPAR], F32)
        stat = at("stat", [P, 2, 8], F32)
        wf = at("wf", [P, KT * FOX], F32)
        wfh = at("wfh", [P, KT, FOX], F32R)
        wfl = at("wfl", [P, KT, FOX], F32R)
        fz = at("fz", [P, 4, TB, FOX], F32)
        cum = at("cum", [P, TB, FOX], F32)
        neg_sink = at("neg_sink", [P, SWA], F32)
        scale_c = at("scale_c", [P, 2 * S], F32)
        pos = at("pos", [P, S], I32, work + 48 * KB)
        ang = at("ang", [P, 5, S], F32, work + 49 * KB)
        assert cursor[0] <= nc.sbuf_usable_end

        def bank(name, shape):
            return ctx.enter_context(nc.psum_tensor(name, shape, F32))

        acc = [bank(f"acc{i}", [P, 2 * S]) for i in range(2)]
        score = [bank(f"score{i}", [P, TB, S]) for i in range(2)]
        turn_ps = bank("turn_ps", [P, TB, S])
        head_ps = bank("head_ps", [P, 2 * S])
        sums = bank("sums", [P, 2 * S])

        def sem(name):
            return ctx.enter_context(nc.semaphore(name))

        loaded = [sem(f"loaded{i}") for i in range(RAW)]
        highs = sem("highs")
        lows_a = sem("lows_a")
        lows_b = sem("lows_b")
        products = sem("products")
        low_ready = sem("low_ready")
        stored = sem("stored")
        dve_order, act_order = sem("dve_order"), sem("act_order")
        par_in, x_in, mem_in, pos_in, wf_in = (sem(n) for n in ("par_in", "x_in", "mem_in", "pos_in", "wf_in"))
        out_done = sem("out_done")
        mean_sum, centered, squares, sumsq, variance, root, normed_t, split_h, split_l = (
            sem(n) for n in ("mean_sum", "centered", "squares", "sumsq", "variance", "root", "normed_t",
                             "split_h", "split_l"))
        angles, tables = sem("angles"), sem("tables")
        silu_done, hidden_done = sem("silu_done"), sem("hidden_done")
        lat_sq_done, lat_sums, lat_var, lat_root, lat_ready = (
            sem(n) for n in ("lat_sq_done", "lat_sums", "lat_var", "lat_root", "lat_ready"))
        roped = sem("roped")
        gate_exp, gated = sem("gate_exp"), sem("gated")
        pool_ready = sem("pool_ready")
        negmax = sem("negmax")
        scores_done, shifted, exps, probs, turns, turned_s, mixed, head_out = (
            sem(n) for n in ("scores_done", "shifted", "exps", "probs", "turns", "turned_s", "mixed", "head_out"))
        sink_exp = sem("sink_exp")
        pair_sq, pair_sum, pair_var, pair_ln, pair_exp, pair_done = (
            sem(n) for n in ("pair_sq", "pair_sum", "pair_var", "pair_ln", "pair_exp", "pair_done"))
        wf_split, logits, logit_in, soft_exp, soft_ln, logf, cum_sum, cum_done, decay_sum, decay_done = (
            sem(n) for n in ("wf_split", "logits", "logit_in", "soft_exp", "soft_ln", "logf", "cum_sum", "cum_done",
                             "decay_sum", "decay_done"))
        mix_final, mix_h, mix_l = sem("mix_final"), sem("mix_h"), sem("mix_l")

        def p_(name, i=0, n=1):
            o, w = AT[name]
            assert i + n <= w
            return par[:, o + i:o + i + n]

        ident = p_("ident", 0, P)
        ones = p_("ones", 0, P)

        def blocks_of(name):
            return p_(name, 0, TB * S).rearrange("p (b s) -> p b s", b=TB)

        upto, causal, dist = blocks_of("upto"), blocks_of("causal"), blocks_of("dist")

        def walk(eng, slot, between, chain=None):
            for name in ORDER:
                r = REG[name]
                between(name)
                if r.looped:
                    first = r.first
                    for k in range(first):
                        slot(r, k, None)
                    runs = (r.n - first) // 4 - 1
                    with eng.Fori(0, runs) as i:
                        if chain:
                            chain.enter(i, r)
                        for k in range(first, first + 4):
                            slot(r, k, i)
                        if chain:
                            chain.leave(runs, r)
                    for k in range(first + 4 * runs, r.n):
                        slot(r, k, None)
                else:
                    for k in range(r.n):
                        slot(r, k, None)
            between("end")

        def val(base, per, i):
            return base if i is None else i * per + base

        def following(r, k, i):
            if i is not None or k + 1 < r.n:
                return r, k + 1, i
            at_ = ORDER.index(r.name) + 1
            return (REG[ORDER[at_]], 0, None) if at_ < len(ORDER) else None

        def free_after(r, k, i, piece):
            if i is not None:
                return val(r.g0 + (k - 2) * r.groups + piece + 1, 4 * r.groups, i)
            s = r.s0 + k - SPLIT
            return released(s, piece) if s >= 0 else None

        def wait_slot_free(eng, r, k, i, piece):
            v = free_after(r, k, i, piece)
            if v is not None:
                eng.wait_ge(products, v)

        def steps_at(r, k, i):
            return STEPS.get((r.name, k), []) if i is None else []

        def after_steps(name):
            return [x for k in range(AFTER) for x in STEPS.get(("after", k), [])] if name == "mixout" else []

        def norms_before(name):
            return {"mem_k": ["mem"], "in_a0": ["emb"], "in_a1": ["ln0"], "up10": ["ln1", "ffn1"],
                    "nat": ["mix"], "up20": ["ffn2"]}.get(name, [])

        def mix_split(name):
            return {"out0": 0, "out1": 1, "mixout": 2}.get(name)

        def tiles_done(r, k, i):
            T = r.t0
            if r.kind == "tile":
                return [(k, 4, r.g0 + 2 * k + 2, 8)]
            if r.kind == "down":
                return [(k // 2, 2, r.g0 + 2 * k + 2, 8)] if k % 2 else []
            at_ = r.g0 + r.groups * k
            if r.kind == "uq":
                return [(3 * k + m, 0, at_ + 1 + m, 0) for m in range(3)]
            if r.kind in ("uk", "pool"):
                return [(m, 0, at_ + 1 + m, 0) for m in range(r.groups)]
            if r.kind == "uv":
                return [(TB * k + m, 0, at_ + 1 + m, 0) for m in range(TB)]
            return [(TB * (k // 4) + m, 0, at_ + 2, 0) for m in range(TB)] if k % 4 == 3 else []

        def natural_dest(r, tile):
            dest = {"mem_v": memv, "nat": v_nat}.get(r.name, v_mla)
            c = tile // TB
            return dest[:, tile % TB, 512 * c:512 * (c + 1)]

        def tile_dest(r, tile):
            if r.name == "mem_k":
                return memk[:, tile, :]
            if r.name[:4] == "in_a":
                return lat[:, tile, :] if tile < 8 else mix[:, tile - 8, :]
            if r.kind == "uq":
                return q[:, tile, :]
            if r.kind == "uk":
                return kn[:, tile, :]
            if r.name[:4] == "in_b":
                g, e = tile // 6, tile % 6
                return [branch[:, 0, :], branch[:, 1, :], branch[:, 2, :], mix[:, 12 + g, :], branch[:, 3, :],
                        mix[:, 8 + g, :]][e]
            assert r.name == "heads"
            return feat[:, tile, :]

        def head_spec(n):
            if n < MLA_ALL:
                h = n % HEADS
                a = 32 * (h % 4)
                qk = [(q[:, h, :], kn[:, h, :])] + [
                    (q[a:a + 32, 8 + 2 * e + h // 4, :], kr[a:a + 32, e, :]) for e in range(2)]
                return "mla", h, qk, [v_mla[:, b, h * P:(h + 1) * P] for b in range(TB)], h
            m = n - MLA_ALL
            if m < FOX0:
                return "mem", m, [(feat[:, m, :], memk[:, m, :])], [
                    memv[:, b, m * P:(m + 1) * P] for b in range(TB)], FOX + SWA + m
            if m < SWA0:
                h = m - FOX0
                base = MEM + 4 * (h // 2) + h % 2
                return "fox", h, [(feat[:, base + 2, :], feat[:, base, :])], [
                    v_nat[:, b, h * P:(h + 1) * P] for b in range(TB)], h
            h = m - SWA0
            kv = h // (SWA // SWA_KV)
            return "swa", h, [(feat[:, 18 + h, :], feat[:, 16 + kv, :])], [
                v_nat[:, b, (FOX + kv) * P:(FOX + kv + 1) * P] for b in range(TB)], FOX + h

        def blocks_seen(kind):
            return [(b, c) for b in range(TB) for c in range(TB) if kind == "mem" or c <= b]

        def pair_of(p):
            if p < 2:
                return memk[:, 2 * p:2 * p + 2, :], "mem_k"
            return feat[:, 2 * (p - 2):2 * (p - 2) + 2, :], PAIRS[p - 2]

        def pair_stored(p):
            return REG["mem_k"].t0 + 2 * p + 2 if p < 2 else REG["heads"].t0 + 2 * (p - 2) + 2

        def flat(a):
            return a.rearrange("p b s -> p (b s)")

        def norm_ready(name):
            return {"ffn1": (normed_t, KT * (NORM["ln1"]["i"] + 1)),
                    "mix": (stored, REG["nat"].t0), "ffn2": (stored, REG["up20"].t0), "mem": (mem_in, 16),
                    "emb": (x_in, 16), "ln0": (stored, REG["in_a1"].t0), "ln1": (stored, REG["up10"].t0)}[name]

        def gate_stored(n):
            layer, m = n // 16, n % 16
            if m < 8:
                return REG[f"in_a{layer}"].t0 + 8 + m + 1
            g, e = (m - 8) // 2, (m - 8) % 2
            return REG[f"in_b{layer}"].t0 + 6 * g + (4 if e == 0 else 6)

        block = ctx.enter_context(nc.Block())

        @block.sync
        def _(eng):
            eng.dma_start(memx[:, :, :], t["mem"]).then_inc(mem_in, 16)
            eng.dma_start(par[:, :], t["par"]).then_inc(par_in, 16)
            eng.dma_start(pos[:, :], t["positions"]).then_inc(pos_in, 16)

            def slot(r, k, i):
                s = r.s0 + k
                if i is not None or s >= RAW:
                    eng.wait_ge(lows_a, val(s - RAW + 1, 4, i))
                    eng.wait_ge(lows_b, val(s - RAW + 1, 4, i))
                eng.dma_start(raw[:, s % RAW, 0:r.blocks * P],
                              t[r.array][val(r.a0 + k, 4, i), :, :]).then_inc(loaded[s % RAW], 16)
                if r.name == "mem_k" and k == 3:
                    eng.dma_start(x[:, :, :], t["x"]).then_inc(x_in, 16)
                    eng.dma_start(wf[:, :], t["wf"]).then_inc(wf_in, 16)

            def between(name):
                if name == "end":
                    eng.wait_ge(stored, REGIONS[-1].t0 + REGIONS[-1].tiles)
                    eng.dma_start(t["out"], x[:, :, :]).then_inc(out_done, 16)
                    eng.wait_ge(out_done, 16)

            walk(eng, slot, between)

        @block.tensor
        def _(eng):
            def product(bank_, hi, lo, moving, start, stop):
                eng.matmul(bank_[:, :], hi, moving, start=start, stop=False)
                return eng.matmul(bank_[:, S:2 * S], lo, moving[:, 0:S], start=False, stop=stop)

            def product_natural(bank_, still, hi, lo, b, start, stop):
                xh, xl = still[:, b * P:(b + 1) * P], still[:, S + b * P:S + (b + 1) * P]
                eng.matmul(bank_[:, :], xh, hi, start=start, stop=False)
                eng.matmul(bank_[:, :], xl, hi, start=False, stop=False)
                return eng.matmul(bank_[:, :], xh, lo, start=False, stop=stop)

            def sum_over_features(out, tiles):
                for n, a in enumerate(tiles):
                    last = eng.matmul(out, ones, a, start=(n == 0), stop=(n == len(tiles) - 1))
                return last

            def slot(r, k, i):
                for step in steps_at(r, k, i):
                    do(*step)
                s = r.s0 + k
                pos_ = s % SPLIT

                def piece_ready(piece):
                    eng.wait_ge((lows_a, lows_b)[piece], val(s + 1, 4, i))

                def bank_free(tile, per):
                    if r.t0 + tile >= 2:
                        eng.wait_ge(stored, val(r.t0 + tile - 1, per, i))
                    return acc[(r.t0 + tile) % 2]

                def hl(b):
                    b += (8 - r.pieces[0]) * (b >= r.pieces[0])
                    return high[:, pos_, b * P:(b + 1) * P], low[:, pos_, b * P:(b + 1) * P]

                if r.kind == "tile":
                    a = bank_free(k, 4)
                    for b in range(KT):
                        if b % 8 == 0:
                            piece_ready(b // 8)
                        if k == 0 and mix_split(r.name) is not None and b % 4 == 0:
                            eng.wait_ge(mix_l, 4 * mix_split(r.name) + b // 4 + 1)
                        if k == 0 and norms_before(r.name):
                            eng.wait_ge(split_l, KT * NORM[norms_before(r.name)[-1]]["splits"] + b + 1)
                        last = product(a, *hl(b), xs[:, b, :], b == 0, b == KT - 1)
                        if b % 8 == 7:
                            last.then_inc(products, 1)
                elif r.kind == "down":
                    half = k % 2
                    eng.wait_ge(hidden_done, r.hidden0 + HALF * (half + 1))
                    a = bank_free(k // 2, 2) if not half else acc[(r.t0 + k // 2) % 2]
                    for b in range(HALF):
                        if b in (0, r.pieces[0]):
                            piece_ready(int(b > 0))
                        last = product(a, *hl(b), hidden[:, HALF * half + b, :], half == 0 and b == 0,
                                       half == 1 and b == HALF - 1)
                        if b in (r.pieces[0] - 1, HALF - 1):
                            last.then_inc(products, 1)
                elif r.kind in ("uq", "uk"):
                    eng.wait_ge(lat_ready, r.layer + 1)
                    per, src = (KQ, 0) if r.kind == "uq" else (KKV, KQ)
                    for m in range(r.groups):
                        a = bank_free(k * r.groups + m, 0)
                        for b in range(per):
                            if m * per + b in (0, r.pieces[0]):
                                piece_ready(int(m * per + b > 0))
                            last = product(a, *hl(m * per + b), lats[:, src + b, :], b == 0, b == per - 1)
                        last.then_inc(products, 1)
                elif r.kind == "pool":
                    piece_ready(0)
                    piece_ready(1)
                    for g in range(GROUPS):
                        a = bank_free(g, 0)
                        eng.wait_ge(pool_ready, GROUPS * r.layer + g + 1)
                        product(a, *hl(g), pooled[:, g, :], True, True).then_inc(products, 1)
                elif r.kind == "uv":
                    piece_ready(0)
                    piece_ready(1)
                    for b in range(TB):
                        a = bank_free(TB * k + b, 0)
                        for c in range(KKV):
                            w = slice(c * 8 * P, c * 8 * P + 512)
                            last = product_natural(a, lats[:, KQ + c, :], high[:, pos_, w], low[:, pos_, w], b,
                                                   c == 0, c == KKV - 1)
                        last.then_inc(products, 1)
                else:
                    if k == 0 and norms_before(r.name):
                        eng.wait_ge(split_l, KT * (NORM[norms_before(r.name)[-1]]["splits"] + 1))
                    for piece in range(2):
                        piece_ready(piece)
                        for b in range(TB):
                            tile = TB * (k // 4) + b
                            a = bank_free(tile, 0) if k % 4 == 0 and piece == 0 else acc[(r.t0 + tile) % 2]
                            for c in range(2 * piece, 2 * piece + 2):
                                w = slice(c * 512, (c + 1) * 512)
                                kt = 4 * (k % 4) + c
                                last = product_natural(a, xs[:, kt, :], high[:, pos_, w], low[:, pos_, w], b,
                                                       kt == 0, kt == KT - 1)
                        last.then_inc(products, 1)

            def do(kind, *a):
                if kind == "lat_scale":
                    eng.wait_ge(lat_sq_done, a[0] + 1)
                    sum_over_features(sums[:, 0:S], [lat_sq[:, n, :] for n in range(KQ)])
                    sum_over_features(sums[:, S:2 * S], [lat_sq[:, n, :] for n in range(KQ, KQ + KKV)])\
                        .then_inc(lat_sums, 1)
                elif kind == "headnorm":
                    p = a[0]
                    eng.wait_ge(pair_sq, p + 1)
                    if p:
                        eng.wait_ge(pair_var, p)
                    if p == 2:
                        eng.wait_ge(decay_done, FOX)
                    eng.matmul(sums[:, :], ones, scale_a[:, :], start=True, stop=True).then_inc(pair_sum, 1)
                elif kind == "forget":
                    eng.wait_ge(split_l, KT * (NORM["mix"]["splits"] + 1))
                    eng.wait_ge(wf_split, 1)
                    for b in range(TB):
                        out_ = sums[:, 8 * b:8 * b + FOX]
                        for kt in range(KT):
                            xh, xl = xs[:, kt, b * P:(b + 1) * P], xs[:, kt, S + b * P:S + (b + 1) * P]
                            eng.matmul(out_, xh, wfh[:, kt, :], start=(kt == 0), stop=False)
                            eng.matmul(out_, xl, wfh[:, kt, :], start=False, stop=False)
                            last = eng.matmul(out_, xh, wfl[:, kt, :], start=False, stop=(kt == KT - 1))
                    last.then_inc(logits, 1)
                elif kind == "decay":
                    h = a[0]
                    eng.wait_ge(logf, 1)
                    if h == 0:
                        for b in range(TB):
                            for c in range(TB):
                                last = eng.matmul(sums[:, 8 * b:8 * b + FOX], upto[:, c, b * P:(b + 1) * P],
                                                  fz[:, 0, c, :], start=(c == 0), stop=(c == TB - 1))
                        last.then_inc(cum_sum, 1)
                        eng.wait_ge(cum_done, 1)
                    else:
                        eng.wait_ge(decay_done, h)
                    for c in range(TB):
                        last = eng.matmul(sums[:, 0:S], lf_rows[:, h, c, :], upto[:, c, :],
                                          start=(c == 0), stop=(c == TB - 1))
                    last.then_inc(decay_sum, 1)
                elif kind == "scores":
                    n = a[0]
                    what, h, qk, _, _ = head_spec(n)
                    if n >= 2:
                        eng.wait_ge(shifted, n - 1)
                    if what == "mla":
                        layer = n // HEADS
                        eng.wait_ge(stored, REG[f"in_b{layer}"].t0)
                        eng.wait_ge(roped, 2 * layer + 2)
                    else:
                        eng.wait_ge(stored, REG["heads"].t0)
                        p = {"mem": h // 2, "fox": 3 + 2 * (h // 2), "swa": 9 + h // 2}[what]
                        eng.wait_ge(pair_done, 2 + p + 1)
                    for b in range(TB):
                        for m, (qc, kc) in enumerate(qk):
                            last = eng.matmul(score[n % 2][:, b, :], qc[:, b * P:(b + 1) * P], kc,
                                              start=(m == 0), stop=(m == len(qk) - 1))
                    last.then_inc(scores_done, 1)
                elif kind == "turn":
                    n = a[0]
                    eng.wait_ge(probs, 2 * n + 2)
                    if n:
                        eng.wait_ge(turned_s, n)
                    for b, c in blocks_seen(head_spec(n)[0]):
                        last = eng.transpose(turn_ps[:, c, b * P:(b + 1) * P], prob[:, n % 2, b, c * P:(c + 1) * P], ident)
                    last.then_inc(turns, 1)
                elif kind == "mixv":
                    n = a[0]
                    what, _, _, v, _ = head_spec(n)
                    eng.wait_ge(turned_s, n + 1)
                    if n:
                        eng.wait_ge(head_out, n)
                    o_ = 0 if what == "mem" else P
                    eng.matmul(head_ps[:, 0:S], v[0], turned[:, 0, :], start=True, stop=False)
                    eng.matmul(head_ps[:, o_:S], v[1], turned[:, 1, o_:S], start=False, stop=True).then_inc(mixed, 1)

            def norm(name):
                c = NORM[name]
                if c["mean"]:
                    eng.wait_ge(*norm_ready(name))
                    if name == "emb":
                        eng.wait_ge(pair_var, 2)
                    sum_over_features(sums[:, 0:S], [x[:, kt, :] for kt in range(KT)]).then_inc(mean_sum, 1)
                for kt in range(KT):
                    if kt % 4 == 0:
                        eng.wait_ge(squares, 4 * c["i"] + kt // 4 + 1)
                    last = eng.matmul(sums[:, S:2 * S], ones, square[:, kt, :], start=(kt == 0), stop=(kt == KT - 1))
                last.then_inc(sumsq, 1)

            def between(name):
                if name == "mem_k":
                    eng.wait_ge(par_in, 16)
                for step in after_steps(name):
                    do(*step)
                for n in norms_before(name):
                    norm(n)

            walk(eng, slot, between)

        @block.scalar
        def _(eng):
            def split_high(r, k, i):
                s = r.s0 + k
                eng.wait_ge(loaded[s % RAW], val(16 * (s // RAW + 1), 16, i))
                for piece, n in enumerate(r.pieces):
                    wait_slot_free(eng, r, k, i, piece)
                    at_ = piece * r.pieces[0] * P
                    eng.activation(high[:, s % SPLIT, piece * 8 * P:(8 * piece + n) * P],
                                   raw[:, s % RAW, at_:at_ + n * P], ACT.Copy).then_inc(highs, 1)

            def slot(r, k, i):
                nxt = following(r, k, i)
                if nxt:
                    split_high(*nxt)
                for step in steps_at(r, k, i):
                    do(*step)
                for tile, per, prod_, pper in tiles_done(r, k, i):
                    T = r.t0 + tile
                    eng.wait_ge(products, val(prod_, pper, i))
                    if r.kind in ("natural", "uv"):
                        eng.activation(natural_dest(r, tile)[:, 0:S], acc[T % 2][:, 0:S], ACT.Copy)\
                            .then_inc(low_ready, 1)
                        continue
                    if T >= 2:
                        eng.wait_ge(stored, val(T - 1, per, i))
                    eng.activation(lowsum[:, T % 2, :], acc[T % 2][:, S:2 * S], ACT.Copy,
                                   scale=0.5 if r.kind == "down" else 1.0).then_inc(low_ready, 1)
                    if r.name[:2] == "up" and k % 2 == 0:
                        pair = r.pair0 + k // 2
                        eng.wait_ge(stored, val(T + 1, per, i))
                        if i is not None or pair:
                            eng.wait_ge(hidden_done, val(pair, 2, i))
                        eng.activation(silu_g[:, :], gate[:, :], ACT.Silu).then_inc(silu_done, 1)

            def do(kind, *a):
                if kind == "lat_square":
                    eng.wait_ge(stored, REG[f"in_a{a[0]}"].t0 + KQ + KKV)
                    eng.activation(lat_sq[:, :, :], lat[:, 0:KQ + KKV, :], ACT.Square).then_inc(lat_sq_done, 1)
                elif kind == "lat_scale":
                    eng.wait_ge(lat_var, a[0] + 1)
                    eng.activation(scale_b[:, :], scale_a[:, :], ACT.Sqrt).then_inc(lat_root, 1)
                elif kind == "silu":
                    n, dest = a
                    eng.wait_ge(stored, gate_stored(n))
                    if n:
                        eng.wait_ge(gated, n)
                    eng.activation(up[:, :], mix[:, dest, :], ACT.Exp, scale=-1.0).then_inc(gate_exp, 1)
                elif kind == "square":
                    p = a[0]
                    eng.wait_ge(stored, pair_stored(p))
                    if p:
                        eng.wait_ge(pair_done, p)
                    eng.activation(scale_a[:, :], flat(pair_of(p)[0]), ACT.Square).then_inc(pair_sq, 1)
                elif kind == "headnorm":
                    p = a[0]
                    eng.wait_ge(pair_var, p + 1)
                    eng.activation(scale_a[:, :], scale_b[:, :], ACT.Ln).then_inc(pair_ln, 1)
                    eng.wait_ge(pair_ln, p + 1)
                    eng.activation(scale_a[:, :], scale_a[:, :], ACT.Exp, scale=-0.5).then_inc(pair_exp, 1)
                elif kind == "forget":
                    eng.wait_ge(logit_in, 1)
                    eng.activation(fz[:, 2, :, :], fz[:, 1, :, :], ACT.Exp).then_inc(soft_exp, 1)
                    eng.wait_ge(soft_exp, 1)
                    eng.activation(fz[:, 3, :, :], fz[:, 2, :, :], ACT.Ln, bias=1.0).then_inc(soft_ln, 1)
                elif kind == "scores":
                    n = a[0]
                    what, h, _, _, _ = head_spec(n)
                    eng.wait_ge(negmax, n + 1)
                    for b in range(TB):
                        eng.activation(prob[:, n % 2, b, :], prob[:, n % 2, b, :], ACT.Exp,
                                       bias=stat[:, n % 2, b:b + 1], accum_out=stat[:, n % 2, 2 + b:3 + b])\
                            .then_inc(exps, 1)
                    if what == "swa":
                        eng.activation(stat[:, n % 2, 4:6], stat[:, n % 2, 0:2], ACT.Exp, bias=p_("sinks", h))\
                            .then_inc(sink_exp, 1)
                elif kind == "turn":
                    n = a[0]
                    eng.wait_ge(turns, n + 1)
                    if n:
                        eng.wait_ge(mixed, n)
                    if head_spec(n)[0] == "mem":
                        eng.activation(flat(turned[:, :, :]), flat(turn_ps[:, :, :]), ACT.Copy).then_inc(turned_s, 1)
                    else:
                        eng.activation(turned[:, 0, :], turn_ps[:, 0, :], ACT.Copy)
                        eng.activation(turned[:, 1, P:S], turn_ps[:, 1, P:S], ACT.Copy).then_inc(turned_s, 1)

            def norm(name):
                c = NORM[name]
                src = memx if name == "mem" else normed if c["mean"] else x
                y = x if c["mean"] else normed
                if not c["mean"]:
                    eng.wait_ge(*norm_ready(name))
                for n in range(4):
                    if c["mean"]:
                        eng.wait_ge(centered, 4 * c["means"] + n + 1)
                    eng.activation(square[:, 4 * n:4 * n + 4, :], src[:, 4 * n:4 * n + 4, :], ACT.Square)\
                        .then_inc(squares, 1)
                eng.wait_ge(variance, c["i"] + 1)
                eng.activation(scale_b[:, 0:S], scale_a[:, 0:S], ACT.Sqrt).then_inc(root, 1)
                if c["split"]:
                    for kt in range(KT):
                        eng.wait_ge(normed_t, KT * c["i"] + kt + 1)
                        eng.activation(xs[:, kt, 0:S], y[:, kt, :], ACT.Copy).then_inc(split_h, 1)

            def between(name):
                if name == "mem_k":
                    eng.wait_ge(par_in, 16)
                    split_high(REG[name], 0, None)
                    eng.wait_ge(angles, 1)
                    eng.activation(sin[:, :], ang[:, 0, :], ACT.Sin)
                    eng.activation(cos[:, :], ang[:, 1, :], ACT.Sin).then_inc(tables, 1)
                for step in after_steps(name):
                    do(*step)
                if mix_split(name) is not None:
                    n = mix_split(name)
                    if n < DEPTH:
                        eng.wait_ge(head_out, HEADS * (n + 1))
                        eng.wait_ge(mix_final, n + 1)
                    else:
                        eng.wait_ge(head_out, MLA_ALL + FOX + SWA + MEM)
                    eng.wait_ge(products, REG[name].g0)
                    for c in range(4):
                        eng.activation(xs[:, 4 * c:4 * c + 4, 0:S], mix[:, 4 * c:4 * c + 4, :], ACT.Copy)\
                            .then_inc(mix_h, 1)
                for n in norms_before(name):
                    norm(n)

            walk(eng, slot, between)

        @block.vector
        def _(eng):
            chain = Chain(eng, dve_order)
            step_ = chain.step

            def split_low(r, k, i):
                s = r.s0 + k
                w = slice(8 * P, (8 + r.pieces[1]) * P)
                eng.wait_ge(highs, val(2 * s + 2, 8, i))
                eng.tensor_tensor(low[:, s % SPLIT, w], raw[:, s % RAW, r.pieces[0] * P:r.blocks * P], high[:, s % SPLIT, w].bitcast(F32),
                                  ALU.subtract).then_inc(lows_b, 1)

            def slot(r, k, i):
                nxt = following(r, k, i)
                if nxt:
                    split_low(*nxt)
                for step in steps_at(r, k, i):
                    do(*step)
                for tile, per, prod_, pper in tiles_done(r, k, i):
                    store(r, k, i, tile, per)

            def store(r, k, i, tile, per):
                T = r.t0 + tile
                first, second = acc[T % 2][:, 0:S], lowsum[:, T % 2, :]
                eng.wait_ge(low_ready, val(T + 1, per, i))

                def done(ins, and_wait=False):
                    ins.then_inc(stored, 1)
                    if and_wait:
                        eng.wait_ge(stored, val(T + 1, per, i))

                if r.kind in ("natural", "uv"):
                    done(eng.tensor_copy(natural_dest(r, tile)[:, S:2 * S], acc[T % 2][:, S:2 * S]))
                elif r.name[:2] == "up":
                    if k % 2 == 0:
                        done(eng.tensor_tensor(gate[:, :], first, second, ALU.add))
                        return
                    hid = val(k // 2, 2, i)
                    done(eng.tensor_tensor(up[:, :], first, second, ALU.add), True)
                    eng.wait_ge(silu_done, val(r.pair0 + k // 2 + 1, 2, i))
                    step_(eng.tensor_tensor(hidden[:, hid, 0:S], silu_g[:, :], up[:, :], ALU.mult))
                    step_(eng.tensor_tensor(prod[:, :], silu_g[:, :], up[:, :], ALU.mult))
                    eng.tensor_tensor(hidden[:, hid, S:2 * S], prod[:, :], hidden[:, hid, 0:S].bitcast(F32),
                                      ALU.subtract).then_inc(hidden_done, 1)
                    eng.wait_ge(hidden_done, val(r.pair0 + k // 2 + 1, 2, i))
                elif r.kind == "down":
                    xt = x[:, val(tile, per, i), :]
                    step_(eng.scalar_tensor_tensor(out=xt, in0=first, scalar=0.5, in1=xt, op0=ALU.mult, op1=ALU.add))
                    done(eng.tensor_tensor(xt, xt, second, ALU.add))
                elif r.name[:3] == "out":
                    xt = x[:, tile, :]
                    step_(eng.scalar_tensor_tensor(out=xt, in0=xt, scalar=ALPHA, in1=first, op0=ALU.mult, op1=ALU.add))
                    done(eng.scalar_tensor_tensor(out=xt, in0=second, scalar=p_("b_out", KT * r.layer + tile), in1=xt,
                                                  op0=ALU.add, op1=ALU.add))
                elif r.name == "mixout":
                    xt = x[:, tile, :]
                    step_(eng.tensor_tensor(xt, first, xt, ALU.add))
                    done(eng.tensor_tensor(xt, xt, second, ALU.add))
                elif r.kind == "pool":
                    done(eng.tensor_tensor(gate[:, :], first, second, ALU.add), True)
                    ins = eng.scalar_tensor_tensor(out=mix[:, 8 + tile, :], in0=gate[:, :],
                                                   scalar=p_("pool_s", GROUPS * r.layer + tile),
                                                   in1=mix[:, 8 + tile, :], op0=ALU.mult, op1=ALU.mult)
                    if tile == GROUPS - 1:
                        ins.then_inc(mix_final, 1)
                    else:
                        step_(ins)
                else:
                    done(eng.tensor_tensor(tile_dest(r, tile), first, second, ALU.add))

            def rotate(x1, x2, c, s_, tmp, out1, out2, last):
                step_(eng.tensor_tensor(tmp[0], x1, c, ALU.mult))
                step_(eng.tensor_tensor(tmp[1], x2, s_, ALU.mult))
                step_(eng.tensor_tensor(tmp[2], x2, c, ALU.mult))
                step_(eng.tensor_tensor(tmp[3], x1, s_, ALU.mult))
                step_(eng.tensor_tensor(out1, tmp[0], tmp[1], ALU.subtract))
                eng.tensor_tensor(out2, tmp[2], tmp[3], ALU.add).then_inc(roped, 1)
                eng.wait_ge(roped, last)

            def do(kind, *a):
                if kind == "lat_scale":
                    layer = a[0]
                    eng.wait_ge(lat_sums, layer + 1)
                    step_(eng.tensor_scalar(scale_a[:, 0:S], sums[:, 0:S], 1.0 / QLAT, RMS_EPS, ALU.mult, ALU.add))
                    eng.tensor_scalar(scale_a[:, S:2 * S], sums[:, S:2 * S], 1.0 / KVLAT, RMS_EPS, ALU.mult, ALU.add)\
                        .then_inc(lat_var, 1)
                    eng.wait_ge(lat_root, layer + 1)
                    step_(eng.reciprocal(scale_a[:, :], scale_b[:, :]))
                    for n in range(KQ + KKV):
                        g, o_ = (p_("q_g", KQ * layer + n), 0) if n < KQ else (p_("kv_g", KKV * layer + n - KQ), S)
                        step_(eng.scalar_tensor_tensor(out=lat[:, n, :], in0=lat[:, n, :], scalar=g,
                                                       in1=scale_a[:, o_:o_ + S], op0=ALU.mult, op1=ALU.mult))
                elif kind == "lat_split":
                    n = KQ + KKV
                    step_(eng.tensor_copy(lats[:, :, 0:S], lat[:, 0:n, :]))
                    eng.tensor_tensor(lats[:, :, S:2 * S], lat[:, 0:n, :], lats[:, :, 0:S].bitcast(F32), ALU.subtract)\
                        .then_inc(lat_ready, 1)
                elif kind == "rope_k":
                    layer = a[0]
                    eng.wait_ge(tables, 1)
                    eng.wait_ge(stored, REG[f"in_a{layer}"].t0 + 8)
                    rotate(lat[:, 6, :], lat[:, 7, :], cos[:, :], sin[:, :], [rope_u[:, n, :] for n in range(4)],
                           kr[:, 0, :], kr[:, 1, :], 2 * layer + 1)
                elif kind == "rope_q":
                    layer = a[0]
                    wide = [tt[:, :].unsqueeze(1).to_broadcast([P, 2, S]) for tt in (cos, sin)]
                    eng.wait_ge(stored, REG[f"uk{layer}"].t0)
                    rotate(q[:, 8:10, :], q[:, 10:12, :], *wide, [rope_t[:, n, :, :] for n in range(4)],
                           q[:, 8:10, :], q[:, 10:12, :], 2 * layer + 2)
                elif kind == "silu":
                    n, dest = a
                    eng.wait_ge(gate_exp, n + 1)
                    step_(eng.tensor_scalar(prod[:, :], up[:, :], 1.0, None, ALU.add))
                    step_(eng.reciprocal(gate[:, :], prod[:, :]))
                    eng.tensor_tensor(mix[:, dest, :], mix[:, dest, :], gate[:, :], ALU.mult).then_inc(gated, 1)
                    eng.wait_ge(gated, n + 1)
                elif kind == "conv":
                    layer, g = a

                    def tap(w):
                        return p_("conv", (3 * layer + w) * GROUPS + g)

                    eng.wait_ge(stored, REG[f"in_b{layer}"].t0 + 6 * g + 3)
                    u, y = branch[:, 4, :], branch[:, 5, :]
                    step_(eng.tensor_tensor(u, branch[:, 0, :], branch[:, 1, :], ALU.mult))
                    step_(eng.tensor_scalar(y, u, tap(2), None, ALU.mult))
                    for back in (1, 2):
                        step_(eng.scalar_tensor_tensor(out=y[:, back:S], in0=u[:, 0:S - back], scalar=tap(2 - back),
                                                       in1=y[:, back:S], op0=ALU.mult, op1=ALU.add))
                    step_(eng.tensor_tensor(y, y, branch[:, 2, :], ALU.mult))
                    step_(eng.tensor_tensor(mix[:, 12 + g, :], mix[:, 12 + g, :], y, ALU.mult))
                elif kind == "pool":
                    layer, g = a
                    w = WINDOWS[g]
                    src = branch[:, 3, :]
                    eng.wait_ge(stored, REG[f"in_b{layer}"].t0 + 6 * g + 5)
                    cur, back, n = src, 1, 0
                    while back < w:
                        nxt = branch[:, 6 + n % 2, :]
                        step_(eng.tensor_tensor(nxt[:, back:S], cur[:, back:S], cur[:, 0:S - back], ALU.add))
                        step_(eng.tensor_copy(nxt[:, 0:back], cur[:, 0:back]))
                        cur, back, n = nxt, back * 2, n + 1
                    y = branch[:, 6 + n % 2, :]
                    step_(eng.scalar_tensor_tensor(out=y[:, w:S], in0=cur[:, w:S], scalar=1.0 / w, in1=src[:, w:S],
                                                   op0=ALU.mult, op1=ALU.subtract))
                    step_(eng.tensor_tensor(y[:, 0:w], cur[:, 0:w], p_("count", 0, w), ALU.mult))
                    step_(eng.tensor_tensor(y[:, 0:w], y[:, 0:w], src[:, 0:w], ALU.subtract))
                    step_(eng.tensor_copy(pooled[:, g, 0:S], y))
                    eng.tensor_tensor(pooled[:, g, S:2 * S], y, pooled[:, g, 0:S].bitcast(F32), ALU.subtract)\
                        .then_inc(pool_ready, 1)
                    eng.wait_ge(pool_ready, GROUPS * layer + g + 1)
                elif kind == "headnorm":
                    p = a[0]
                    pair, gain = pair_of(p)
                    eng.wait_ge(pair_sum, p + 1)
                    eng.tensor_scalar(scale_b[:, :], sums[:, :], 1.0 / P, RMS_EPS, ALU.mult, ALU.add)\
                        .then_inc(pair_var, 1)
                    eng.wait_ge(pair_exp, p + 1)
                    step_(eng.scalar_tensor_tensor(out=scale_c[:, :], in0=scale_a[:, :], scalar=-0.5, in1=scale_a[:, :],
                                                   op0=ALU.mult, op1=ALU.mult))
                    step_(eng.tensor_tensor(scale_c[:, :], scale_c[:, :], scale_b[:, :], ALU.mult))
                    step_(eng.scalar_tensor_tensor(out=scale_c[:, :], in0=scale_c[:, :], scalar=1.5, in1=scale_a[:, :],
                                                   op0=ALU.add, op1=ALU.mult))
                    eng.scalar_tensor_tensor(out=flat(pair), in0=flat(pair), scalar=p_(gain), in1=scale_c[:, :],
                                             op0=ALU.mult, op1=ALU.mult).then_inc(pair_done, 1)
                    eng.wait_ge(pair_done, p + 1)
                elif kind == "forget":
                    eng.wait_ge(logits, 1)
                    for b in range(TB):
                        step_(eng.tensor_tensor(fz[:, 0, b, :], sums[:, 8 * b:8 * b + FOX], p_("forget", 0, FOX), ALU.add))
                    step_(eng.tensor_scalar(fz[:, 1, :, :], fz[:, 0, :, :], -1.0, None, ALU.mult))
                    eng.tensor_tensor(fz[:, 1, :, :], fz[:, 1, :, :], fz[:, 0, :, :], ALU.min).then_inc(logit_in, 1)
                    eng.wait_ge(soft_ln, 1)
                    step_(eng.scalar_tensor_tensor(out=fz[:, 0, :, :], in0=fz[:, 0, :, :], scalar=0.0, in1=fz[:, 3, :, :],
                                                   op0=ALU.min, op1=ALU.subtract))
                    for h in range(FOX):
                        for b in range(TB):
                            ins = eng.tensor_scalar(lf_rows[:, h, b, :], ones, fz[:, 0, b, h:h + 1], -1.0,
                                                    ALU.mult, ALU.mult)
                    ins.then_inc(logf, 1)
                elif kind == "decay":
                    h = a[0]
                    if h == 0:
                        eng.wait_ge(cum_sum, 1)
                        for b in range(TB):
                            ins = eng.tensor_copy(cum[:, b, :], sums[:, 8 * b:8 * b + FOX])
                        ins.then_inc(cum_done, 1)
                    eng.wait_ge(decay_sum, h + 1)
                    eng.tensor_copy(decay[:, h, :], sums[:, 0:S]).then_inc(decay_done, 1)
                elif kind == "scores":
                    softmax(a[0])
                elif kind == "mixv":
                    n = a[0]
                    what, h, _, _, dest = head_spec(n)
                    eng.wait_ge(mixed, n + 1)
                    if what == "mla":
                        eng.tensor_tensor(mix[:, dest, :], head_ps[:, 0:S], mix[:, dest, :], ALU.mult)\
                            .then_inc(head_out, 1)
                    else:
                        eng.tensor_copy(mix[:, dest, :], head_ps[:, 0:S]).then_inc(head_out, 1)

            def softmax(n):
                what, h, _, _, _ = head_spec(n)
                pr, sc = prob[:, n % 2, :, :], score[n % 2]
                neg, total, inv = stat[:, n % 2, 0:2], stat[:, n % 2, 2:4], stat[:, n % 2, 6:8]
                eng.wait_ge(scores_done, n + 1)
                if n >= 2:
                    eng.wait_ge(turns, n - 1)
                if what == "mla":
                    ins = eng.scalar_tensor_tensor(out=flat(pr), in0=flat(sc[:, :, :]), scalar=MLA_SCALE,
                                                   in1=flat(causal), op0=ALU.mult, op1=ALU.add)
                elif what == "mem":
                    ins = eng.tensor_copy(flat(pr), flat(sc[:, :, :]))
                elif what == "fox":
                    eng.wait_ge(decay_done, FOX)
                    for b in range(TB):
                        step_(eng.scalar_tensor_tensor(out=pr[:, b, :], in0=sc[:, b, :], scalar=cum[:, b, h:h + 1],
                                                       in1=decay[:, h, :], op0=ALU.add, op1=ALU.add))
                    ins = eng.tensor_tensor(flat(pr), flat(pr), flat(causal), ALU.add)
                else:
                    slope = float(np.float32(2.0 ** (-8.0 * (h + 1) / SWA)))
                    ins = eng.scalar_tensor_tensor(out=flat(pr), in0=flat(dist), scalar=-slope,
                                                   in1=flat(sc[:, :, :]), op0=ALU.mult, op1=ALU.add)
                ins.then_inc(shifted, 1)
                eng.wait_ge(shifted, n + 1)
                ins = eng.tensor_reduce(neg, pr, AX.X, ALU.max, negate=True)
                if what == "swa":
                    step_(ins)
                    ins = eng.tensor_scalar(neg, neg, neg_sink[:, h:h + 1], None, ALU.min)
                ins.then_inc(negmax, 1)
                eng.wait_ge(exps, 2 * n + 2)
                if what == "swa":
                    eng.wait_ge(sink_exp, h + 1)
                    step_(eng.tensor_tensor(total, total, stat[:, n % 2, 4:6], ALU.add))
                step_(eng.reciprocal(inv, total))
                for b in range(TB):
                    eng.tensor_scalar(pr[:, b, :], pr[:, b, :], stat[:, n % 2, 6 + b:7 + b], None, ALU.mult)\
                        .then_inc(probs, 1)

            def norm(name):
                c = NORM[name]
                eng.wait_ge(*norm_ready(name))
                eps = LN_EPS if c["mean"] else RMS_EPS
                if c["mean"]:
                    eng.wait_ge(mean_sum, c["means"] + 1)
                    step_(eng.tensor_scalar(mean[:, :], sums[:, 0:S], 1.0 / D, None, ALU.mult))
                    for n in range(4):
                        eng.tensor_tensor(normed[:, 4 * n:4 * n + 4, :], x[:, 4 * n:4 * n + 4, :],
                                          mean[:, :].unsqueeze(1).to_broadcast([P, 4, S]), ALU.subtract)\
                            .then_inc(centered, 1)
                eng.wait_ge(sumsq, c["i"] + 1)
                eng.tensor_scalar(scale_a[:, 0:S], sums[:, S:2 * S], 1.0 / D, eps, ALU.mult, ALU.add)\
                    .then_inc(variance, 1)
                eng.wait_ge(root, c["i"] + 1)
                step_(eng.reciprocal(scale_a[:, 0:S], scale_b[:, 0:S]))
                src = normed if c["mean"] else memx if name == "mem" else x
                gain, bias, o_ = {"mem": ("mem_g", None, 0), "emb": ("emb_g", "emb_b", 0), "ln0": ("ln_g", "ln_b", 0),
                                  "ln1": ("ln_g", "ln_b", KT), "ffn1": ("ffn1_g", None, 0), "mix": ("mix_g", None, 0),
                                  "ffn2": ("ffn2_g", None, 0)}[name]
                for kt in range(KT):
                    ins = eng.scalar_tensor_tensor(out=normed[:, kt, :], in0=src[:, kt, :], scalar=p_(gain, o_ + kt),
                                                   in1=scale_a[:, 0:S], op0=ALU.mult, op1=ALU.mult)
                    if bias:
                        step_(ins)
                        ins = eng.tensor_scalar(x[:, kt, :], normed[:, kt, :], p_(bias, o_ + kt), None, ALU.add)
                    ins.then_inc(normed_t, 1)
                eng.wait_ge(normed_t, KT * (c["i"] + 1))

            def rope_angles():
                eng.wait_ge(pos_in, 16)
                eng.wait_ge(par_in, 16)
                a0, a1, turns_, r, m = (ang[:, n, :] for n in range(5))
                step_(eng.tensor_copy(r, pos[:, :]))
                step_(eng.tensor_scalar(a0, r, p_("inv_freq"), None, ALU.mult))
                step_(eng.tensor_scalar(turns_, a0, INV_2PI, MAGIC, ALU.mult, ALU.add))
                step_(eng.tensor_scalar(turns_, turns_, -MAGIC, None, ALU.add))
                for part in (PI_A, PI_B, PI_C):
                    step_(eng.scalar_tensor_tensor(out=a0, in0=turns_, scalar=-part, in1=a0, op0=ALU.mult, op1=ALU.add))
                step_(eng.tensor_scalar(a1, a0, float(np.pi / 2), None, ALU.add))
                step_(eng.tensor_scalar(m, a1, PI_IN, -2 * float(np.pi), ALU.is_gt, ALU.mult))
                step_(eng.tensor_tensor(a1, a1, m, ALU.add))
                step_(eng.tensor_scalar(a0, a0, PI_IN, -PI_IN, ALU.min, ALU.max))
                eng.tensor_scalar(a1, a1, PI_IN, -PI_IN, ALU.min, ALU.max).then_inc(angles, 1)

            def between(name):
                if name == "mem_k":
                    split_low(REG[name], 0, None)
                    rope_angles()
                    for g in ("fox_q", "swa_q", "mem_q"):
                        step_(eng.tensor_scalar(p_(g), p_(g), HEAD_SCALE, None, ALU.mult))
                    step_(eng.tensor_scalar(neg_sink[:, :], p_("sinks", 0, SWA), -1.0, None, ALU.mult))
                if name == "in_a0":
                    eng.wait_ge(wf_in, 16)
                    flat_h = wfh[:, :, :].rearrange("p k f -> p (k f)")
                    step_(eng.tensor_copy(flat_h, wf[:, :]))
                    eng.tensor_tensor(wfl[:, :, :].rearrange("p k f -> p (k f)"), wf[:, :], flat_h.bitcast(F32),
                                      ALU.subtract).then_inc(wf_split, 1)
                for step in after_steps(name):
                    do(*step)
                if mix_split(name) is not None:
                    n = mix_split(name)
                    for c in range(4):
                        eng.wait_ge(mix_h, 4 * n + c + 1)
                        w = slice(4 * c, 4 * c + 4)
                        eng.tensor_tensor(xs[:, w, S:2 * S], mix[:, w, :], xs[:, w, 0:S].bitcast(F32), ALU.subtract)\
                            .then_inc(mix_l, 1)
                for n in norms_before(name):
                    norm(n)

            walk(eng, slot, between, chain)

        @block.gpsimd
        def _(eng):
            def split_low(r, k, i):
                s = r.s0 + k
                w = slice(0, r.pieces[0] * P)
                eng.wait_ge(highs, val(2 * s + 1, 8, i))
                eng.tensor_tensor(low[:, s % SPLIT, w], raw[:, s % RAW, w], high[:, s % SPLIT, w].bitcast(F32),
                                  ALU.subtract).then_inc(lows_a, 1)

            def slot(r, k, i):
                nxt = following(r, k, i)
                if nxt:
                    split_low(*nxt)

            def between(name):
                if name == "mem_k":
                    split_low(REG[name], 0, None)
                for n in norms_before(name):
                    c = NORM[n]
                    y = x if c["mean"] else normed
                    for kt in range(KT if c["split"] else 0):
                        eng.wait_ge(split_h, KT * c["splits"] + kt + 1)
                        eng.tensor_tensor(xs[:, kt, S:2 * S], y[:, kt, :], xs[:, kt, 0:S].bitcast(F32), ALU.subtract)\
                            .then_inc(split_l, 1)

            walk(eng, slot, between)


class Chain:

    def __init__(self, eng, sem):
        self.eng, self.sem, self.n, self.i, self.per = eng, sem, 0, None, 0

    def enter(self, i, r):
        self.i, self.per, self.start = i, 4 if r.kind == "tile" else 2, self.n

    def leave(self, runs, r):
        assert self.n - self.start == self.per, (r.name, self.n - self.start)
        self.n, self.i = self.start + runs * self.per, None

    def step(self, ins):
        ins.then_inc(self.sem, 1)
        self.n += 1
        self.eng.wait_ge(self.sem, self.n if self.i is None else self.i * self.per + self.n)


def _tiles(w, columns=None):
    w = w if columns is None else w[:, columns]
    k, n = w.shape
    return np.ascontiguousarray(w.reshape(k // P, P, n // P, P).transpose(2, 1, 0, 3)).reshape(n // P, P, k)


def _rows(w, per, width):
    k, n = w.shape
    a = w.reshape(k // P // per, per, P, n // width, width).transpose(3, 0, 2, 1, 4)
    return np.ascontiguousarray(a).reshape(-1, P, per * width)


def _cols(v):
    return np.asarray(v).reshape(-1, P).T


def _all(v):
    return np.broadcast_to(np.asarray(v).reshape(1, -1), (P, np.size(v)))


def layout(inp):
    a = {k: np.asarray(v) for k, v in inp.items()}
    arange = np.arange
    out = {}
    starts = dict(zip(("q", "kv", "kr", "g", "p", "gp", "ch", "cb", "cc", "gc"),
                      np.cumsum([0, QLAT, KVLAT, ROPE, 1024, 512, 512, 512, 512, 512])))
    half = ROPE // 2
    first = [arange(QLAT + KVLAT), starts["kr"] + arange(P) % half, starts["kr"] + half + arange(P) % half,
             starts["g"] + arange(1024)]
    rest = [starts[n] + g * P + arange(P) for g in range(GROUPS) for n in ("ch", "cc", "cb", "gc", "p", "gp")]
    columns = np.concatenate(first + rest)
    out["w_in"] = np.concatenate([_tiles(a["w_in"][l], columns) for l in range(DEPTH)])
    per = P + ROPE
    nope = (arange(HEADS)[:, None] * per + arange(P)).ravel()
    x1 = (arange(HEADS)[:, None] * per + P + arange(half)).ravel()
    uq = [_tiles(a["w_uq"][l], np.concatenate([nope, x1, x1 + half])) for l in range(DEPTH)]
    out["w_uq"] = np.concatenate([u.reshape(4, 3, P, QLAT).transpose(0, 2, 1, 3).reshape(4, P, 3 * QLAT) for u in uq])
    kcols = (arange(HEADS)[:, None] * 2 * P + arange(P)).ravel()
    out["w_uk"] = np.stack([_tiles(a["w_ukv"][l], kcols).transpose(1, 0, 2).reshape(P, -1) for l in range(DEPTH)])
    out["w_uv"] = np.concatenate([_rows(a["w_ukv"][l][:, kcols + P], KKV, 512) for l in range(DEPTH)])
    out["w_pool"] = np.ascontiguousarray(a["w_pool"].transpose(0, 2, 1, 3)).reshape(DEPTH, P, GROUPS * P)
    out["w_out"] = np.concatenate([_tiles(a["w_out"][l]) for l in range(DEPTH)])
    for part in ("1", "2"):
        up = np.stack([_tiles(a[f"ffn{part}_{n}_2"][0]) for n in ("gate", "up")], 1)
        out["w_up" + part] = up.reshape(2 * FT, P, D)
        down = a[f"ffn{part}_down_2"][0].reshape(CHUNKS, 2, HALF, P, KT, P).transpose(0, 4, 1, 3, 2, 5)
        out["w_down" + part] = np.ascontiguousarray(down).reshape(CHUNKS * KT * 2, P, HALF * P)
    w = a["w_in_2"][0]
    cuts = np.cumsum([0, FOX * P, FOX * P, FOX * P, FOX, SWA * P, SWA_KV * P, SWA_KV * P, MEM * P])
    fq, fk, fv, fl, sq, sk, sv, mq = (arange(cuts[n], cuts[n + 1]) for n in range(8))
    out["w_nat"] = _rows(w[:, np.concatenate([fv, sv])], 4, 512)
    order = [mq]
    for n in range(FOX // 2):
        order += [fk[2 * P * n:2 * P * (n + 1)], fq[2 * P * n:2 * P * (n + 1)]]
    out["w_heads"] = _tiles(w, np.concatenate(order + [sk, sq]))
    out["wf"] = np.ascontiguousarray(w[:, fl].reshape(KT, P, FOX).transpose(1, 0, 2)).reshape(P, KT * FOX)
    out["w_mixout"] = _tiles(a["w_out_2"][0])
    out["w_memk"] = _tiles(a["w_mem_k_2"][0])
    out["w_memv"] = _rows(a["w_mem_v_2"][0], 4, 512)
    for name, src in (("x", "x"), ("mem", "mem_2")):
        out[name] = np.ascontiguousarray(a[src][0].T.reshape(KT, P, S).transpose(1, 0, 2))
    out["positions"] = np.ascontiguousarray(np.broadcast_to(a["positions"], (P, S)))
    tok = arange(S)
    upto = (tok[:, None] <= tok[None, :]).astype(np.float32).reshape(TB, P, S).transpose(1, 0, 2).reshape(P, -1)
    gap = tok[:, None] - tok[None, :]
    causal = np.where(gap >= 0, 0.0, NEG)
    far = np.where((gap >= 0) & (gap < SWA_WINDOW), gap, FAR)
    causal, far = (m.astype(np.float32).reshape(TB, P, S).transpose(1, 0, 2).reshape(P, -1) for m in (causal, far))
    inv_freq = np.float32(10000.0) ** (-(arange(P) % half).astype(np.float32) / np.float32(half))
    values = dict(
        emb_g=_cols(a["emb_ln_g"]), emb_b=_cols(a["emb_ln_b"]), ffn1_g=_cols(a["ffn1_norm_2"]),
        mix_g=_cols(a["mix_norm_2"]), mem_g=_cols(a["mem_norm_2"]), ffn2_g=_cols(a["ffn2_norm_2"]),
        ln_g=_cols(a["ln_g"]), ln_b=_cols(a["ln_b"]), b_out=_cols(a["b_out"]), q_g=_cols(a["q_norm_g"]),
        kv_g=_cols(a["kv_norm_g"]), pool_s=_cols(a["pool_scale"]), conv=_cols(a["conv_w"]),
        fox_q=_cols(a["fox_q_gain_2"]), fox_k=_cols(a["fox_k_gain_2"]), swa_q=_cols(a["swa_q_gain_2"]),
        swa_k=_cols(a["swa_k_gain_2"]), mem_q=_cols(a["mem_q_gain_2"]), mem_k=_cols(a["mem_k_gain_2"]),
        forget=_all(a["forget_bias_2"]), sinks=_all(a["swa_sinks_2"]),
        inv_freq=inv_freq.reshape(P, 1).astype(np.float32),
        count=_all(1 / np.arange(1, max(WINDOWS) + 1, dtype=np.float32)),
        ident=np.eye(P, dtype=np.float32), ones=np.ones((P, P), np.float32), upto=upto, causal=causal, dist=far)
    out["par"] = np.ascontiguousarray(np.concatenate([values[n] for n, _ in COLUMNS], 1))
    return out


def kernel(**inputs):
    import concourse.bacc as bacc
    from concourse.bass_utils import run_bass_kernel_spmd

    arrays = layout(inputs)
    nc = bacc.Bacc("TRN2", target_bir_lowering=False, num_devices=1, dynamic_dma_scratch_size=1024)
    t = {n: nc.dram_tensor(n + "_dram", v.shape, mybir.dt.from_np(v.dtype), kind="ExternalInput").ap()
         for n, v in arrays.items()}
    t["out"] = nc.dram_tensor("out_dram", (P, KT, S), F32, kind="ExternalOutput").ap()
    build(nc, t)
    r = run_bass_kernel_spmd(nc, [{n + "_dram": v for n, v in arrays.items()}], core_ids=[0])
    out = np.asarray(r.results[0]["out_dram"])
    return np.ascontiguousarray(out.transpose(2, 1, 0)).reshape(1, S, D)
```

```python
from contextlib import ExitStack

import numpy as np

import concourse.bass as bass
from concourse import mybir

F32 = mybir.dt.float32
F32R = mybir.dt.float32r
I32 = mybir.dt.int32
ALU = mybir.AluOpType
ACT = mybir.ActivationFunctionType
AX = mybir.AxisListType

P = 128
D = 2048
S = 256
KT = D // P
TB = S // P
DEPTH = 2
HEADS = 8
ROPE = 64
QLAT, KVLAT = 512, 256
KQ, KKV = QLAT // P, KVLAT // P
GROUPS = 4
WINDOWS = (2, 4, 8, 16)
FOX, SWA, SWA_KV, MEM = 6, 6, 2, 4
SWA_WINDOW = 128
FF = 5632
FT = FF // P
CHUNKS = 2
CT = FT // CHUNKS
HALF = CT // 2
LN_EPS, RMS_EPS = 1e-5, 1e-6
ALPHA = (2 * DEPTH) ** 0.25
MLA_SCALE = (128 + ROPE) ** -0.5
HEAD_SCALE = 128 ** -0.5
NEG = -1e30
FAR = 1e32
INV_2PI = float(1 / (2 * np.pi))
MAGIC = 1.5 * 2.0 ** 23
PI_A = 6.28125
PI_B = float(np.float32(np.round((2 * np.pi - PI_A) * 2 ** 20) / 2 ** 20))
PI_C = float(2 * np.pi - PI_A - PI_B)
PI_IN = float(np.nextafter(np.float32(np.pi), np.float32(0)))

COLUMNS, AT = [], {}


def _column(name, width):
    AT[name] = (sum(w for _, w in COLUMNS), width)
    COLUMNS.append((name, width))


for _name, _width in (
        ("emb_g", KT), ("emb_b", KT), ("ffn1_g", KT), ("mix_g", KT), ("mem_g", KT), ("ffn2_g", KT),
        ("ln_g", DEPTH * KT), ("ln_b", DEPTH * KT), ("b_out", DEPTH * KT),
        ("q_g", DEPTH * KQ), ("kv_g", DEPTH * KKV), ("pool_s", DEPTH * GROUPS), ("conv", DEPTH * 3 * GROUPS),
        ("fox_q", 1), ("fox_k", 1), ("swa_q", 1), ("swa_k", 1), ("mem_q", 1), ("mem_k", 1),
        ("forget", FOX), ("sinks", SWA), ("inv_freq", 1), ("count", max(WINDOWS)),
        ("ident", P), ("ones", P), ("upto", TB * S), ("causal", TB * S), ("dist", TB * S)):
    _column(_name, _width)
NPAR = sum(w for _, w in COLUMNS)


class Region:
    def __init__(self, name, slabs, pieces, tiles, groups):
        self.name, self.n, self.pieces, self.tiles, self.groups = name, slabs, pieces, tiles, groups
        self.blocks = sum(pieces)


def plan():
    regions = [Region("mem_k", 4, (8, 8), 4, 2), Region("mem_v", 4, (8, 8), TB, 2)]
    for layer in range(DEPTH):
        regions += [
            Region(f"in_a{layer}", 16, (8, 8), 16, 2), Region(f"uq{layer}", 4, (4, 8), 12, 3),
            Region(f"uk{layer}", 1, (8, 8), 8, 8), Region(f"uv{layer}", 2, (4, 4), 2 * TB, 2),
            Region(f"in_b{layer}", 8, (8, 8), 8, 2), Region(f"pool{layer}", 1, (2, 2), 4, 4),
            Region(f"in_c{layer}", 16, (8, 8), 16, 2),
            Region(f"out{layer}", KT, (8, 8), KT, 2)]
    for part in (1, 2):
        if part == 2:
            regions += [Region("nat0", 4, (8, 8), TB, 2), Region("heads", 24, (8, 8), 24, 2),
                        Region("nat1", 4, (8, 8), TB, 2), Region("mixout", KT, (8, 8), KT, 2)]
        for c in range(CHUNKS):
            regions += [Region(f"up{part}{c}", 2 * CT, (8, 8), 2 * CT, 2),
                        Region(f"down{part}{c}", 2 * KT, (6, 5), KT, 2)]
    s = t = g = pairs = 0
    used = {}
    for r in regions:
        r.s0, r.t0, r.g0 = s, t, g
        s, t, g = s + r.n, t + r.tiles, g + r.n * r.groups
        r.kind = next((k for n, k in (("up", "tile"), ("down", "down"), ("uq", "uq"), ("uk", "uk"), ("uv", "uv"),
                                      ("pool", "pool"), ("mem_v", "natural"), ("nat", "natural"))
                       if r.name.startswith(n)), "tile")
        r.layer = int(r.name[-1]) if r.name[-1].isdigit() else 0
        r.array = {"in_": "w_in", "uq": "w_uq", "uk": "w_uk", "uv": "w_uv", "pool": "w_pool", "out": "w_out",
                   "mem_k": "w_memk", "mem_v": "w_memv", "nat": "w_nat", "heads": "w_heads", "mixout": "w_mixout",
                   "up1": "w_up1", "up2": "w_up2", "down1": "w_down1", "down2": "w_down2"}[
                       next(n for n in ("in_", "uq", "uk", "uv", "pool", "out", "mem_k", "mem_v", "nat", "heads",
                                        "mixout", "up1", "up2", "down1", "down2") if r.name.startswith(n))]
        r.a0 = used.get(r.array, 0)
        used[r.array] = r.a0 + r.n
        r.looped = r.name.startswith(("up", "down"))
        r.first = 4 if r.name in ("up10", "up20") else 0
        if r.looped:
            assert r.s0 % 4 == 0 and r.t0 % 2 == 0
        r.pair0 = pairs
        if r.name.startswith("up"):
            pairs += r.n // 2
        r.hidden0 = pairs - CT
    return regions


REGIONS = plan()
REG = {r.name: r for r in REGIONS}
ORDER = [r.name for r in REGIONS]
SLABS = REGIONS[-1].s0 + REGIONS[-1].n
GROUPS_ALL = REGIONS[-1].g0 + REGIONS[-1].n * REGIONS[-1].groups
RAW = 4
TURNED = 4
SPLIT = 2


def region_of(s):
    return next(r for r in REGIONS if r.s0 <= s < r.s0 + r.n)


def released(s, piece):
    r = region_of(s)
    at = r.g0 + (s - r.s0) * r.groups
    if r.name[:2] == "uv" or piece == 1:
        return at + r.groups
    return at + {2: 1, 3: 1, 8: 4, 4: 2}[r.groups]


NORMS = ("mem", "emb", "ln0", "ln1", "ffn1", "mix", "ffn2")
N_OF = {n: i for i, n in enumerate(NORMS)}
LAYER_NORMS = ("emb", "ln0", "ln1")
SHIFT_TILES = 4
CUTS = ((0, 1), (1, 4), (4, 8), (8, 12), (12, 16))
FILLS = {"mem": "gv", "emb": "gg", "ln0": "gg", "ln1": "vv", "mix": "gv", "ffn2": "vv"}
NORMED_T = {}
_n = 0
for _name in NORMS:
    NORMED_T[_name] = _n
    _n += {"mem": KT, "mix": KT}.get(_name, len(CUTS) if _name in LAYER_NORMS else 0)


def high_count(name, kt):
    return KT * list(FILLS).index(name) + kt + 1


def low_count(name, kt):
    who, n = FILLS[name][kt % 2], 0
    for other, engines in FILLS.items():
        for k in range(KT if other != name else kt + 1):
            n += engines[k % 2] == who
        if other == name:
            return who, n


MEM_STEPS = {("mem_k", 1): [("first_sum", "emb")], ("mem_k", 2): [("shift", "emb"), ("square", 0)],
             ("mem_k", 3): [("headnorm", 0), ("moments", "emb", 0, 1, 2)],
             ("mem_v", 0): [("square", 1), ("moments", "emb", 3, 4, 5)],
             ("mem_v", 1): [("headnorm", 1), ("moments", "emb", 6, 7, 8)],
             ("mem_v", 2): [("moments", "emb", 9, 10, 11)],
             ("mem_v", 3): [("moments", "emb", 12, 13, 14, 15)]}


def head_steps(put, n, slot, last):
    put(slot, "scores", n)
    put(slot + 1, "exps", n)
    put(slot + 2, "turn", n)
    put(last, "mixv", n)


MLA_ALL = DEPTH * HEADS
SWA0, FOX0 = 4, 10
PAIRS = ["mem_q", "mem_q", "swa_k", "swa_q", "swa_q", "swa_q", "fox_k", "fox_q", "fox_k", "fox_q", "fox_k", "fox_q"]
MIX_ORDER = [(2, 0, 1, 3)] * DEPTH + [(0, 1, 2, 3)]


def layer_steps(layer):
    steps = {}

    def put(slot, *step):
        for name, first in (("in_a", 0), ("uq", 16), ("uk", 20), ("uv", 21), ("in_b", 23), ("pool", 31),
                            ("in_c", 32), ("out", 48)):
            r = REG[f"{name}{layer}"]
            if first <= slot < first + r.n:
                steps.setdefault((r.name, slot - first), []).append(step)

    put(8, "lat_square", layer)
    put(9, "lat_scale", layer)
    put(10, "lat_split", layer)
    put(11, "rope_k", layer)
    put(23, "rope_q", layer)
    for j in range(HEADS):
        put(9 + j if j < 7 else 23, "silu", 16 * layer + j, j)
    for h, slot in enumerate((24, 26, 28, 30, 33, 35, 38, 40)):
        head_steps(put, layer * HEADS + h, slot, slot + 3)
    for g in range(GROUPS):
        put(24 + 2 * g, "pool", layer, g)
        put(25 + 2 * g, "silu", 16 * layer + 8 + g, 8 + g)
        put(33 + 4 * g, "silu", 16 * layer + 12 + g, 12 + g)
        put(35 + 4 * g, "conv", layer, g)
    for slot, c in zip((44, 45, 46), MIX_ORDER[layer]):
        put(slot, "mix_split", layer, c)
    ln = f"ln{layer}"
    put(48 + 4, "first_sum", ln)
    put(48 + 5, "shift", ln)
    put(48 + 5, "moments", ln, 0)
    for k in range(6, KT):
        put(48 + k, "moments", ln, *([k - 5, k - 1] if k < 10 else [k - 1]))
    return steps


def mix_steps():
    steps = {}

    def put(slot, *step):
        where = (("nat0", slot) if slot < 4 else ("heads", slot - 4) if slot < 28 else ("nat1", slot - 28)
                 if slot < 32 else ("after", slot - 32))
        steps.setdefault(where, []).append(step)

    put(1, "forget")
    put(2, "forget_turn")
    for h in range(FOX):
        put(3 + h // 2, "decay", h)
    for n, slot in enumerate((8, 9, 10, 12, 14, 15, 16, 17, 18, 20, 22, 24, 26, 28, 30, 30)):
        head_steps(put, MLA_ALL + n, slot, slot + 3 if n < FOX0 + 2 else max(32, slot + 3))
    for p in range(len(PAIRS)):
        put(6 + 2 * p, "square", 2 + p)
        put(7 + 2 * p, "headnorm", 2 + p)
    return steps


def ffn_steps():
    steps = {}
    for k in range(1, KT):
        steps[("mixout", k)] = [("gain", "ffn2", k - 1)]
    for part in (1, 2):
        steps[(f"up{part}0", 0)] = [("factor", f"ffn{part}")]
        steps[(f"up{part}0", 1)] = [("factor_sum", f"ffn{part}")]
    return steps


def in_order(steps):
    rank = {"mixv": 0, "turn": 1, "silu": 2, "exps": 2, "shift": 2, "square": 3, "headnorm": 3, "scores": 5}
    return {k: sorted(v, key=lambda x: rank.get(x[0], 4)) for k, v in steps.items()}


STEPS = dict(MEM_STEPS)
for _l in range(DEPTH):
    STEPS.update(layer_steps(_l))
STEPS.update(mix_steps())
STEPS.update(ffn_steps())
STEPS = in_order(STEPS)
AFTER = max(k[1] for k in STEPS if k[0] == "after") + 1


def build(nc, t):
    with ExitStack() as ctx:
        cursor = [(nc.sbuf_base + 31) // 32 * 32]

        def at(name, shape, dt, offset=None):
            size = int(np.prod(shape[1:])) * 4
            if offset is None:
                offset = cursor[0]
                cursor[0] += (size + 31) // 32 * 32
            return nc.alloc_sbuf_tensor_at(name, shape, dt, offset=offset)

        raw = at("raw", [P, RAW, 16 * P], F32)
        high = at("high", [P, SPLIT, 16 * P], F32R)
        low = at("low", [P, SPLIT, 16 * P], F32R)
        xs = at("xs", [P, KT, 2 * S], F32R)
        x = at("x", [P, KT, S], F32)
        memk = at("memk", [P, MEM, S], F32)
        memv = at("memv", [P, TB, MEM * P], F32)
        work = cursor[0]
        cursor[0] += 63488
        KB = 1024
        memx = at("memx", [P, KT, S], F32, work)
        square = at("square", [P, KT, S], F32, work + 16 * KB)
        mixs = at("mixs", [P, KT, 2 * S], F32R, work)
        moment = at("moment", [P, 2 * S], F32, work + 32 * KB)
        moment_sq = at("moment_sq", [P, S], F32, work + 34 * KB)
        shift = at("shift", [P, S], F32, work + 35 * KB)
        factor = at("factor", [P, S], F32, work + 44 * KB)
        late_moment = at("late_moment", [P, 2 * S], F32, work + 46 * KB)
        normed = at("normed", [P, KT, S], F32, work + 46 * KB)
        hidden = at("hidden", [P, CT, 2 * S], F32R, work)
        lat = at("lat", [P, 8, S], F32, work)
        v_mla = at("v_mla", [P, TB, HEADS * P], F32, work)
        lats = at("lats", [P, KQ + KKV, 2 * S], F32R, work + 8 * KB)
        pooled = at("pooled", [P, GROUPS, 2 * S], F32R, work + 8 * KB)
        rope_t = at("rope_t", [P, 4, TB, S], F32, work + 8 * KB)
        branch = at("branch", [P, 4, S], F32, work + 32 * KB)
        q = at("q", [P, 12, S], F32, work + 20 * KB)
        lat_sq = at("lat_sq", [P, 6, S], F32, work + 24 * KB)
        rope_u = at("rope_u", [P, 4, S], F32, work + 30 * KB)
        kn = at("kn", [P, HEADS, S], F32, work + 36 * KB)
        kr = at("kr", [P, 2, S], F32, work + 44 * KB)
        mix = at("mix", [P, KT, S], F32, work + 46 * KB)
        feat = at("feat", [P, 24, S], F32, work)
        v_nat = at("v_nat", [P, TB, (FOX + SWA_KV) * P], F32, work + 24 * KB)
        decay = at("decay", [P, FOX, S], F32, work + 32 * KB)
        lf_rows = at("lf_rows", [P, FOX, TB, P], F32, work + 38 * KB)
        lowsum = at("lowsum", [P, 2, S], F32)
        gate = at("gate", [P, S], F32)
        silu_g = at("silu_g", [P, S], F32)
        up = at("up", [P, S], F32)
        prod = at("prod", [P, S], F32)
        prob = at("prob", [P, 2, TB, S], F32)
        turned = at("turned", [P, TURNED, TB, S], F32)
        scale_a = at("scale_a", [P, 2 * S], F32)
        scale_b = at("scale_b", [P, 2 * S], F32)
        mean = at("mean", [P, S], F32)
        dummy = at("dummy", [P, 1], F32)
        cos = at("cos", [P, S], F32)
        sin = at("sin", [P, S], F32)
        par = at("par", [P, NPAR], F32)
        stat = at("stat", [P, 2, 8], F32)
        wf = at("wf", [P, KT * FOX], F32)
        wfh = at("wfh", [P, KT, FOX], F32R)
        wfl = at("wfl", [P, KT, FOX], F32R)
        fz = at("fz", [P, 4, TB, FOX], F32)
        cum = at("cum", [P, TB, FOX], F32)
        neg_sink = at("neg_sink", [P, SWA], F32)
        scale_c = at("scale_c", [P, 2 * S], F32)
        pos = at("pos", [P, S], I32, work + 36 * KB)
        ang = at("ang", [P, 5, S], F32, work + 37 * KB)
        assert cursor[0] <= nc.sbuf_usable_end

        def bank(name, shape):
            return ctx.enter_context(nc.psum_tensor(name, shape, F32))

        acc = [bank(f"acc{i}", [P, 2 * S]) for i in range(2)]
        score = [bank(f"score{i}", [P, TB, S]) for i in range(2)]
        turn_ps = bank("turn_ps", [P, TB, S])
        head_ps = [bank(f"head_ps{i}", [P, 2 * S]) for i in range(2)]
        sums = bank("sums", [P, 2 * S])

        def sem(name):
            return ctx.enter_context(nc.semaphore(name))

        loaded = [sem(f"loaded{i}") for i in range(RAW)]
        highs = sem("highs")
        lows_a = sem("lows_a")
        lows_b = sem("lows_b")
        products = sem("products")
        low_ready = sem("low_ready")
        stored = sem("stored")
        dve_order, act_order = sem("dve_order"), sem("act_order")
        par_in, masks_in, x_in, pos_in, wf_in = (sem(n) for n in ("par_in", "masks_in", "x_in", "pos_in", "wf_in"))
        mem_in = [sem(f"mem_in{n}") for n in range(4)]
        out_done = sem("out_done")
        first_in, first_sum, shifted_by, moments_in, squares, sumsq, variance, root, normed_t = (
            sem(n) for n in ("first_in", "first_sum", "shifted_by", "moments_in", "squares", "sumsq", "variance",
                             "root", "normed_t"))
        split_h = sem("split_h")
        split_l = {"g": sem("split_l_g"), "v": sem("split_l_v")}
        ffn_squares = sem("ffn_squares")
        embedded = sem("embedded")
        angles, tables = sem("angles"), sem("tables")
        silu_done, hidden_done = sem("silu_done"), sem("hidden_done")
        lat_sq_done, lat_sums, lat_var, lat_root, lat_ready = (
            sem(n) for n in ("lat_sq_done", "lat_sums", "lat_var", "lat_root", "lat_ready"))
        roped = sem("roped")
        gate_exp, gated = sem("gate_exp"), sem("gated")
        pool_ready = sem("pool_ready")
        negmax = sem("negmax")
        scores_done, shifted, exps, probs, turns, turned_s, mixed, head_out = (
            sem(n) for n in ("scores_done", "shifted", "exps", "probs", "turns", "turned_s", "mixed", "head_out"))
        sink_exp = sem("sink_exp")
        pair_sq, pair_sum, pair_var, pair_ln, pair_exp, pair_done = (
            sem(n) for n in ("pair_sq", "pair_sum", "pair_var", "pair_ln", "pair_exp", "pair_done"))
        logit_rows = sem("logit_rows")
        wf_split, logits, logit_in, soft_exp, soft_ln, logf, cum_sum, cum_done, decay_sum, decay_done = (
            sem(n) for n in ("wf_split", "logits", "logit_in", "soft_exp", "soft_ln", "logf", "cum_sum", "cum_done",
                             "decay_sum", "decay_done"))
        mix_final, mix_h, mix_l = sem("mix_final"), sem("mix_h"), sem("mix_l")

        def p_(name, i=0, n=1):
            o, w = AT[name]
            assert i + n <= w
            return par[:, o + i:o + i + n]

        ident = p_("ident", 0, P)
        ones = p_("ones", 0, P)

        def blocks_of(name):
            return p_(name, 0, TB * S).rearrange("p (b s) -> p b s", b=TB)

        upto, causal, dist = blocks_of("upto"), blocks_of("causal"), blocks_of("dist")

        def walk(eng, slot, between, chain=None):
            for name in ORDER:
                r = REG[name]
                between(name)
                if r.looped:
                    first = r.first
                    for k in range(first):
                        slot(r, k, None)
                    runs = (r.n - first) // 4 - 1
                    with eng.Fori(0, runs) as i:
                        if chain:
                            chain.enter(i, r)
                        for k in range(first, first + 4):
                            slot(r, k, i)
                        if chain:
                            chain.leave(runs, r)
                    for k in range(first + 4 * runs, r.n):
                        slot(r, k, None)
                else:
                    for k in range(r.n):
                        slot(r, k, None)
            between("end")

        def val(base, per, i):
            return base if i is None else i * per + base

        def following(r, k, i):
            if i is not None or k + 1 < r.n:
                return r, k + 1, i
            at_ = ORDER.index(r.name) + 1
            return (REG[ORDER[at_]], 0, None) if at_ < len(ORDER) else None

        def free_after(r, k, i, piece):
            if i is not None:
                return val(r.g0 + (k - 2) * r.groups + piece + 1, 4 * r.groups, i)
            s = r.s0 + k - SPLIT
            return released(s, piece) if s >= 0 else None

        def wait_slot_free(eng, r, k, i, piece):
            v = free_after(r, k, i, piece)
            if v is not None:
                eng.wait_ge(products, v)

        def steps_at(r, k, i):
            return STEPS.get((r.name, k), []) if i is None else []

        def after_steps(name):
            return [x for k in range(AFTER) for x in STEPS.get(("after", k), [])] if name == "mixout" else []

        def norms_before(name):
            return {"mem_k": ["mem"], "in_a0": ["emb"], "in_a1": ["ln0"], "up10": ["ln1"],
                    "nat0": ["mix"], "up20": ["ffn2"]}.get(name, [])

        def wait_split(eng, name, kt):
            who, n = low_count(name, kt)
            eng.wait_ge(split_l[who], n)

        def input_region(ln):
            return REG["out" + ln[2:]] if ln != "emb" else None

        def in_mix(r):
            return mixs if r.name[:3] == "out" or r.name == "mixout" else xs

        def mix_split(name):
            return {"out0": 0, "out1": 1, "mixout": 2}.get(name)

        def tiles_done(r, k, i):
            T = r.t0
            if r.kind == "tile":
                return [(k, 4, r.g0 + 2 * k + 2, 8)]
            if r.kind == "down":
                return [(k // 2, 2, r.g0 + 2 * k + 2, 8)] if k % 2 else []
            at_ = r.g0 + r.groups * k
            if r.kind == "uq":
                return [(3 * k + m, 0, at_ + 1 + m, 0) for m in range(3)]
            if r.kind in ("uk", "pool"):
                return [(m, 0, at_ + 1 + m, 0) for m in range(r.groups)]
            if r.kind == "uv":
                return [(TB * k + m, 0, at_ + 1 + m, 0) for m in range(TB)]
            return [(TB * (k // 4) + m, 0, at_ + 2, 0) for m in range(TB)] if k % 4 == 3 else []

        def natural_dest(r, tile):
            dest = {"mem_v": memv, "nat0": v_nat, "nat1": v_nat}.get(r.name, v_mla)
            c = tile // TB if r.name != "nat1" else 1
            return dest[:, tile % TB, 512 * c:512 * (c + 1)]

        def tile_dest(r, tile):
            if r.name == "mem_k":
                return memk[:, tile, :]
            if r.name[:4] == "in_a":
                return lat[:, tile, :] if tile < 8 else mix[:, tile - 8, :]
            if r.kind == "uq":
                return q[:, tile, :]
            if r.kind == "uk":
                return kn[:, tile, :]
            if r.name[:4] == "in_b":
                return branch[:, 3, :] if tile % 2 == 0 else mix[:, 8 + tile // 2, :]
            if r.name[:4] == "in_c":
                g, e = tile // 4, tile % 4
                return mix[:, 12 + g, :] if e == 0 else branch[:, e - 1, :]
            assert r.name == "heads"
            return feat[:, tile, :]

        def head_spec(n):
            if n < MLA_ALL:
                h = n % HEADS
                a = 32 * (h % 4)
                qk = [(q[:, h, :], kn[:, h, :])] + [
                    (q[a:a + 32, 8 + 2 * e + h // 4, :], kr[a:a + 32, e, :]) for e in range(2)]
                return "mla", h, qk, [v_mla[:, b, h * P:(h + 1) * P] for b in range(TB)], h
            m = n - MLA_ALL
            if m < SWA0:
                return "mem", m, [(feat[:, m, :], memk[:, m, :])], [
                    memv[:, b, m * P:(m + 1) * P] for b in range(TB)], FOX + SWA + m
            if m < FOX0:
                h = m - SWA0
                kv = h // (SWA // SWA_KV)
                return "swa", h, [(feat[:, MEM + SWA_KV + h, :], feat[:, MEM + kv, :])], [
                    v_nat[:, b, kv * P:(kv + 1) * P] for b in range(TB)], FOX + h
            h = m - FOX0
            k_at = MEM + SWA_KV + SWA + 4 * (h // 2) + h % 2
            return "fox", h, [(feat[:, k_at + 2, :], feat[:, k_at, :])], [
                v_nat[:, b, (SWA_KV + h) * P:(SWA_KV + h + 1) * P] for b in range(TB)], h

        def keys_seen(kind, b):
            return S if kind == "mem" else (b + 1) * P

        def blocks_seen(kind):
            return [(b, c) for b in range(TB) for c in range(TB) if kind == "mem" or c <= b]

        def pair_of(p):
            if p < 2:
                return memk[:, 2 * p:2 * p + 2, :], "mem_k"
            return feat[:, 2 * (p - 2):2 * (p - 2) + 2, :], PAIRS[p - 2]

        def pair_stored(p):
            return REG["mem_k"].t0 + 2 * p + 2 if p < 2 else REG["heads"].t0 + 2 * (p - 2) + 2

        def flat(a):
            return a.rearrange("p b s -> p (b s)")

        def gate_stored(n):
            layer, m = n // 16, n % 16
            if m < 8:
                return REG[f"in_a{layer}"].t0 + 8 + m + 1
            if m < 12:
                return REG[f"in_b{layer}"].t0 + 2 * (m - 8) + 2
            return REG[f"in_c{layer}"].t0 + 4 * (m - 12) + 1

        block = ctx.enter_context(nc.Block())

        @block.sync
        def _(eng):
            cut = AT["upto"][0]
            eng.dma_start(memx[:, 0:4, :], t["mem"][:, 0:4, :]).then_inc(mem_in[0], 16)
            eng.dma_start(par[:, 0:cut], t["par"][:, 0:cut]).then_inc(par_in, 16)
            for n in range(1, 4):
                eng.dma_start(memx[:, 4 * n:4 * n + 4, :], t["mem"][:, 4 * n:4 * n + 4, :]).then_inc(mem_in[n], 16)
            eng.dma_start(pos[:, :], t["positions"]).then_inc(pos_in, 16)

            def slot(r, k, i):
                s = r.s0 + k
                if i is not None or s >= RAW:
                    eng.wait_ge(lows_a, val(s - RAW + 1, 4, i))
                    eng.wait_ge(lows_b, val(s - RAW + 1, 4, i))
                eng.dma_start(raw[:, s % RAW, 0:r.blocks * P],
                              t[r.array][val(r.a0 + k, 4, i), :, :]).then_inc(loaded[s % RAW], 16)
                if r.name == "mem_k" and k == 1:
                    eng.dma_start(x[:, :, :], t["x"]).then_inc(x_in, 16)
                if r.name == "mem_k" and k == 3:
                    eng.dma_start(par[:, cut:NPAR], t["par"][:, cut:NPAR]).then_inc(masks_in, 16)
                    eng.dma_start(wf[:, :], t["wf"]).then_inc(wf_in, 16)

            def between(name):
                if name == "end":
                    eng.wait_ge(stored, REGIONS[-1].t0 + REGIONS[-1].tiles)
                    eng.dma_start(t["out"], x[:, :, :]).then_inc(out_done, 16)
                    eng.wait_ge(out_done, 16)

            walk(eng, slot, between)

        @block.tensor
        def _(eng):
            def product(bank_, hi, lo, moving, start, stop):
                eng.matmul(bank_[:, :], hi, moving, start=start, stop=False)
                return eng.matmul(bank_[:, S:2 * S], lo, moving[:, 0:S], start=False, stop=stop)

            def product_natural(bank_, still, hi, lo, b, start, stop):
                xh, xl = still[:, b * P:(b + 1) * P], still[:, S + b * P:S + (b + 1) * P]
                eng.matmul(bank_[:, :], xh, hi, start=start, stop=False)
                eng.matmul(bank_[:, :], xl, hi, start=False, stop=False)
                return eng.matmul(bank_[:, :], xh, lo, start=False, stop=stop)

            def sum_over_features(out, tiles):
                for n, a in enumerate(tiles):
                    last = eng.matmul(out, ones, a, start=(n == 0), stop=(n == len(tiles) - 1))
                return last

            def slot(r, k, i):
                for step in steps_at(r, k, i):
                    do(*step)
                s = r.s0 + k
                pos_ = s % SPLIT

                def piece_ready(piece):
                    eng.wait_ge((lows_a, lows_b)[piece], val(s + 1, 4, i))

                def bank_free(tile, per):
                    if r.t0 + tile >= 2:
                        eng.wait_ge(stored, val(r.t0 + tile - 1, per, i))
                    return acc[(r.t0 + tile) % 2]

                def hl(b):
                    b += (8 - r.pieces[0]) * (b >= r.pieces[0])
                    return high[:, pos_, b * P:(b + 1) * P], low[:, pos_, b * P:(b + 1) * P]

                if r.kind == "tile":
                    a = bank_free(k, 4)
                    for b in range(KT):
                        if b % 8 == 0:
                            piece_ready(b // 8)
                        if k == 0 and mix_split(r.name) is not None and b % 4 == 0:
                            n = mix_split(r.name)
                            eng.wait_ge(mix_l, 4 * n + MIX_ORDER[n].index(b // 4) + 1)
                        if k == 0 and norms_before(r.name):
                            wait_split(eng, norms_before(r.name)[0], b)
                        last = product(a, *hl(b), in_mix(r)[:, b, :], b == 0, b == KT - 1)
                        if b % 8 == 7:
                            last.then_inc(products, 1)
                elif r.kind == "down":
                    half = k % 2
                    eng.wait_ge(hidden_done, r.hidden0 + HALF * (half + 1))
                    a = bank_free(k // 2, 2) if not half else acc[(r.t0 + k // 2) % 2]
                    for b in range(HALF):
                        if b in (0, r.pieces[0]):
                            piece_ready(int(b > 0))
                        last = product(a, *hl(b), hidden[:, HALF * half + b, :], half == 0 and b == 0,
                                       half == 1 and b == HALF - 1)
                        if b in (r.pieces[0] - 1, HALF - 1):
                            last.then_inc(products, 1)
                elif r.kind in ("uq", "uk"):
                    eng.wait_ge(lat_ready, r.layer + 1)
                    per, src = (KQ, 0) if r.kind == "uq" else (KKV, KQ)
                    for m in range(r.groups):
                        a = bank_free(k * r.groups + m, 0)
                        for b in range(per):
                            if m * per + b in (0, r.pieces[0]):
                                piece_ready(int(m * per + b > 0))
                            last = product(a, *hl(m * per + b), lats[:, src + b, :], b == 0, b == per - 1)
                        last.then_inc(products, 1)
                elif r.kind == "pool":
                    piece_ready(0)
                    piece_ready(1)
                    for g in range(GROUPS):
                        a = bank_free(g, 0)
                        eng.wait_ge(pool_ready, GROUPS * r.layer + g + 1)
                        product(a, *hl(g), pooled[:, g, :], True, True).then_inc(products, 1)
                elif r.kind == "uv":
                    piece_ready(0)
                    piece_ready(1)
                    for b in range(TB):
                        a = bank_free(TB * k + b, 0)
                        for c in range(KKV):
                            w = slice(c * 8 * P, c * 8 * P + 512)
                            last = product_natural(a, lats[:, KQ + c, :], high[:, pos_, w], low[:, pos_, w], b,
                                                   c == 0, c == KKV - 1)
                        last.then_inc(products, 1)
                else:
                    for piece in range(2):
                        piece_ready(piece)
                        for b in range(TB):
                            tile = TB * (k // 4) + b
                            a = bank_free(tile, 0) if k % 4 == 0 and piece == 0 else acc[(r.t0 + tile) % 2]
                            for c in range(2 * piece, 2 * piece + 2):
                                w = slice(c * 512, (c + 1) * 512)
                                kt = 4 * (k % 4) + c
                                if k < 4 and b == 0 and norms_before(r.name):
                                    wait_split(eng, norms_before(r.name)[0], kt)
                                last = product_natural(a, xs[:, kt, :], high[:, pos_, w], low[:, pos_, w], b,
                                                       kt == 0, kt == KT - 1)
                        last.then_inc(products, 1)

            def do(kind, *a):
                if kind == "shift":
                    n = LAYER_NORMS.index(a[0])
                    eng.wait_ge(first_in, n + 1)
                    eng.matmul(sums[:, 0:S], ones, moment[:, 0:S], start=True, stop=True).then_inc(first_sum, 1)
                elif kind == "factor_sum":
                    total_squares(a[0])
                elif kind == "lat_scale":
                    eng.wait_ge(lat_sq_done, a[0] + 1)
                    sum_over_features(sums[:, 0:S], [lat_sq[:, n, :] for n in range(KQ)])
                    sum_over_features(sums[:, S:2 * S], [lat_sq[:, n, :] for n in range(KQ, KQ + KKV)])\
                        .then_inc(lat_sums, 1)
                elif kind == "headnorm":
                    p = a[0]
                    eng.wait_ge(pair_sq, p + 1)
                    if p:
                        eng.wait_ge(pair_var, p)
                    if p == 0:
                        eng.wait_ge(shifted_by, 1)
                    if p == 2:
                        eng.wait_ge(decay_done, FOX)
                    eng.matmul(sums[:, :], ones, scale_a[:, :], start=True, stop=True).then_inc(pair_sum, 1)
                elif kind == "forget":
                    for kt in (KT - 2, KT - 1):
                        wait_split(eng, "mix", kt)
                    eng.wait_ge(wf_split, 1)
                    eng.wait_ge(masks_in, 16)
                    for kt in range(KT):
                        eng.matmul(sums[0:FOX, :], wfh[:, kt, :], xs[:, kt, :], start=(kt == 0), stop=False)
                        last = eng.matmul(sums[0:FOX, S:2 * S], wfl[:, kt, :], xs[:, kt, 0:S], start=False,
                                          stop=(kt == KT - 1))
                    last.then_inc(logits, 1)
                elif kind == "forget_turn":
                    eng.wait_ge(logit_rows, 1)
                    for b in range(TB):
                        last = eng.transpose(sums[:, 8 * b:8 * b + FOX], up[0:FOX, b * P:(b + 1) * P], ident[0:FOX, 0:FOX])
                    last.then_inc(logits, 1)
                elif kind == "decay":
                    h = a[0]
                    eng.wait_ge(logf, 1)
                    if h == 0:
                        for b in range(TB):
                            for c in range(TB):
                                last = eng.matmul(sums[:, 8 * b:8 * b + FOX], upto[:, c, b * P:(b + 1) * P],
                                                  fz[:, 0, c, :], start=(c == 0), stop=(c == TB - 1))
                        last.then_inc(cum_sum, 1)
                        eng.wait_ge(cum_done, 1)
                    else:
                        eng.wait_ge(decay_done, h)
                    for c in range(TB):
                        last = eng.matmul(sums[:, 0:S], lf_rows[:, h, c, :], upto[:, c, :],
                                          start=(c == 0), stop=(c == TB - 1))
                    last.then_inc(decay_sum, 1)
                elif kind == "scores":
                    n = a[0]
                    what, h, qk, _, _ = head_spec(n)
                    if n >= 2:
                        eng.wait_ge(shifted, TB * (n - 1))
                    if what == "mla":
                        layer = n // HEADS
                        eng.wait_ge(stored, REG[f"in_b{layer}"].t0)
                        eng.wait_ge(roped, 2 * layer + 2)
                    else:
                        eng.wait_ge(stored, REG["heads"].t0)
                        p = {"mem": h // 2, "swa": 3 + h // 2, "fox": 7 + 2 * (h // 2)}[what]
                        eng.wait_ge(pair_done, 2 + p + 1)
                    for b in range(TB):
                        for m, (qc, kc) in enumerate(qk):
                            w = keys_seen(what, b)
                            last = eng.matmul(score[n % 2][:, b, 0:w], qc[:, b * P:(b + 1) * P], kc[:, 0:w],
                                              start=(m == 0), stop=(m == len(qk) - 1))
                    last.then_inc(scores_done, 1)
                elif kind == "turn":
                    n = a[0]
                    eng.wait_ge(probs, 2 * n + 2)
                    if n:
                        eng.wait_ge(turned_s, n)
                    for b, c in blocks_seen(head_spec(n)[0]):
                        last = eng.transpose(turn_ps[:, c, b * P:(b + 1) * P], prob[:, n % 2, b, c * P:(c + 1) * P], ident)
                    last.then_inc(turns, 1)
                elif kind == "mixv":
                    n = a[0]
                    what, h, _, v, _ = head_spec(n)
                    eng.wait_ge(turned_s, n + 1)
                    if n >= 2:
                        eng.wait_ge(head_out, n - 1)
                    if what == "fox" and h >= 2:
                        eng.wait_ge(stored, REG["mixout"].t0)
                    o_ = 0 if what == "mem" else P
                    out_, pr = head_ps[n % 2], turned[:, n % TURNED, :, :]
                    eng.matmul(out_[:, 0:S], v[0], pr[:, 0, :], start=True, stop=False)
                    eng.matmul(out_[:, o_:S], v[1], pr[:, 1, o_:S], start=False, stop=True).then_inc(mixed, 1)

            def total_squares(name):
                eng.wait_ge(moments_in, N_OF[name])
                run = late_moment if name == "mix" else moment
                o_ = 0 if name in LAYER_NORMS else S
                eng.matmul(sums[:, o_:2 * S], ones, run[:, o_:2 * S], start=True, stop=True).then_inc(sumsq, 1)

            def norm(name):
                if name == "mem":
                    for kt in range(KT):
                        if kt % 4 == 0:
                            eng.wait_ge(squares, kt // 4 + 1)
                        last = eng.matmul(sums[:, S:2 * S], ones, square[:, kt, :], start=(kt == 0), stop=(kt == KT - 1))
                    last.then_inc(sumsq, 1)
                elif name != "ffn2":
                    if name == "emb":
                        eng.wait_ge(pair_var, 2)
                    total_squares(name)

            def between(name):
                if name == "mem_k":
                    eng.wait_ge(par_in, 16)
                for step in after_steps(name):
                    do(*step)
                for n in norms_before(name):
                    norm(n)

            walk(eng, slot, between)

        @block.scalar
        def _(eng):
            def split_high(piece, r, k, i):
                s = r.s0 + k
                n, at_ = r.pieces[piece], piece * r.pieces[0] * P
                eng.wait_ge(loaded[s % RAW], val(16 * (s // RAW + 1), 16, i))
                wait_slot_free(eng, r, k, i, piece)
                eng.activation(high[:, s % SPLIT, piece * 8 * P:(8 * piece + n) * P],
                               raw[:, s % RAW, at_:at_ + n * P], ACT.Copy).then_inc(highs, 1)

            def slot(r, k, i):
                nxt = following(r, k, i)
                if nxt:
                    split_high(1, *nxt)
                for step in steps_at(r, k, i):
                    do(*step)
                nxt = nxt and following(*nxt)
                early = {"tile": 0, "down": 0, "natural": 0, "uq": 1, "uk": 4, "pool": 2}.get(r.kind, -1)
                for nth, (tile, per, prod_, pper) in enumerate(tiles_done(r, k, i) + [(None,) * 4]):
                    if nxt and nth == early:
                        split_high(0, *nxt)
                    if tile is None:
                        break
                    T = r.t0 + tile
                    eng.wait_ge(products, val(prod_, pper, i))
                    if r.kind in ("natural", "uv"):
                        eng.activation(natural_dest(r, tile)[:, 0:S], acc[T % 2][:, 0:S], ACT.Copy)\
                            .then_inc(low_ready, 1)
                        continue
                    if T >= 2:
                        eng.wait_ge(stored, val(T - 1, per, i))
                    eng.activation(lowsum[:, T % 2, :], acc[T % 2][:, S:2 * S], ACT.Copy,
                                   scale=0.5 if r.kind == "down" else 1.0).then_inc(low_ready, 1)
                    if r.name[:2] == "up" and k % 2 == 0:
                        pair = r.pair0 + k // 2
                        eng.wait_ge(stored, val(T + 1, per, i))
                        if i is not None or pair:
                            eng.wait_ge(hidden_done, val(pair, 2, i))
                        eng.activation(silu_g[:, :], gate[:, :], ACT.Silu).then_inc(silu_done, 1)
                if nxt and early < 0:
                    split_high(0, *nxt)

            def take_root(name):
                eng.activation(dummy[:, :], ones[:, 0:1], ACT.Sqrt)
                eng.wait_ge(variance, N_OF[name] + 1)
                eng.activation(scale_b[:, 0:S], scale_a[:, 0:S], ACT.Sqrt).then_inc(root, 1)

            def do(kind, *a):
                if kind == "factor":
                    take_root(a[0])
                elif kind == "gain":
                    name, kt = a
                    eng.wait_ge(stored, REG["mixout"].t0 + kt + 1)
                    if kt == 0:
                        eng.wait_ge(products, REG["mixout"].g0)
                    eng.activation(xs[:, kt, 0:S], x[:, kt, :], ACT.Copy, scale=p_("ffn2_g", kt)).then_inc(split_h, 1)
                elif kind == "lat_square":
                    eng.wait_ge(stored, REG[f"in_a{a[0]}"].t0 + KQ + KKV)
                    eng.activation(lat_sq[:, :, :], lat[:, 0:KQ + KKV, :], ACT.Square).then_inc(lat_sq_done, 1)
                elif kind == "lat_scale":
                    eng.wait_ge(lat_var, a[0] + 1)
                    eng.activation(scale_b[:, :], scale_a[:, :], ACT.Sqrt).then_inc(lat_root, 1)
                elif kind == "silu":
                    n, dest = a
                    eng.wait_ge(stored, gate_stored(n))
                    if n:
                        eng.wait_ge(gated, n)
                    eng.activation(up[:, :], mix[:, dest, :], ACT.Exp, scale=-1.0).then_inc(gate_exp, 1)
                elif kind == "square":
                    p = a[0]
                    eng.wait_ge(stored, pair_stored(p))
                    if p:
                        eng.wait_ge(pair_done, p)
                    eng.activation(scale_a[:, :], flat(pair_of(p)[0]), ACT.Square).then_inc(pair_sq, 1)
                elif kind == "headnorm":
                    p = a[0]
                    eng.wait_ge(pair_var, p + 1)
                    eng.activation(scale_a[:, :], scale_b[:, :], ACT.Ln).then_inc(pair_ln, 1)
                    eng.wait_ge(pair_ln, p + 1)
                    eng.activation(scale_a[:, :], scale_a[:, :], ACT.Exp, scale=-0.5).then_inc(pair_exp, 1)
                elif kind == "forget_turn":
                    eng.wait_ge(logit_in, 1)
                    eng.activation(fz[:, 2, :, :], fz[:, 1, :, :], ACT.Exp).then_inc(soft_exp, 1)
                    eng.wait_ge(soft_exp, 1)
                    eng.activation(fz[:, 3, :, :], fz[:, 2, :, :], ACT.Ln, bias=1.0).then_inc(soft_ln, 1)
                elif kind == "exps":
                    n = a[0]
                    what, h, _, _, _ = head_spec(n)
                    eng.wait_ge(negmax, TB * (n + 1))
                    for b in range(TB):
                        pr = prob[:, n % 2, b, 0:keys_seen(what, b)]
                        eng.activation(pr, pr, ACT.Exp,
                                       bias=stat[:, n % 2, b:b + 1], accum_out=stat[:, n % 2, 2 + b:3 + b])\
                            .then_inc(exps, 1)
                    if what == "swa":
                        eng.activation(stat[:, n % 2, 4:6], stat[:, n % 2, 0:2], ACT.Exp, bias=p_("sinks", h))\
                            .then_inc(sink_exp, 1)
                elif kind == "turn":
                    n = a[0]
                    eng.wait_ge(turns, n + 1)
                    if n >= TURNED:
                        eng.wait_ge(mixed, n - TURNED + 1)
                    out_ = turned[:, n % TURNED, :, :]
                    if head_spec(n)[0] == "mem":
                        eng.activation(flat(out_), flat(turn_ps[:, :, :]), ACT.Copy).then_inc(turned_s, 1)
                    else:
                        eng.activation(out_[:, 0, :], turn_ps[:, 0, :], ACT.Copy)
                        eng.activation(out_[:, 1, P:S], turn_ps[:, 1, P:S], ACT.Copy).then_inc(turned_s, 1)
                elif kind == "mix_split":
                    layer, c = a
                    at_ = MIX_ORDER[layer].index(c)
                    if layer == DEPTH:
                        eng.wait_ge(head_out, MLA_ALL + FOX + SWA + MEM)
                    elif c == 2:
                        eng.wait_ge(mix_final, 2 * layer + 1)
                        eng.wait_ge(scores_done, HEADS * (layer + 1))
                        eng.wait_ge(products, REG[f"in_c{layer}"].g0)
                    elif c == 3:
                        eng.wait_ge(mix_final, 2 * layer + 2)
                    else:
                        eng.wait_ge(head_out, HEADS * (layer + 1))
                    eng.activation(mixs[:, 4 * c:4 * c + 4, 0:S], mix[:, 4 * c:4 * c + 4, :], ACT.Copy).then_inc(mix_h, 1)

            def norm(name):
                if name == "ffn2":
                    do("gain", name, KT - 1)
                    return
                if name == "mem":
                    for n in range(4):
                        eng.wait_ge(mem_in[n], 16)
                        eng.activation(square[:, 4 * n:4 * n + 4, :], memx[:, 4 * n:4 * n + 4, :], ACT.Square)\
                            .then_inc(squares, 1)
                take_root(name)
                if name in LAYER_NORMS:
                    o_ = KT if name == "ln1" else 0
                    g, b = ("emb_g", "emb_b") if name == "emb" else ("ln_g", "ln_b")
                    for n, (lo, hi) in enumerate(CUTS):
                        eng.wait_ge(normed_t, NORMED_T[name] + n + 1)
                        for kt in range(lo, hi):
                            gain, bias = p_(g, o_ + kt), p_(b, o_ + kt)
                            ins = eng.activation(x[:, kt, :], normed[:, kt, :], ACT.Identity, bias=bias, scale=gain)
                            if name != "ln1":
                                eng.activation(xs[:, kt, 0:S], normed[:, kt, :], ACT.Identity, bias=bias, scale=gain)\
                                    .then_inc(split_h, 1)
                                continue
                            ins.then_inc(embedded, 1)
                            eng.wait_ge(embedded, kt + 1)
                            eng.activation(xs[:, kt, 0:S], x[:, kt, :], ACT.Copy, scale=p_("ffn1_g", kt))\
                                .then_inc(split_h, 1)
                            eng.activation(square[:, kt, :], x[:, kt, :], ACT.Square).then_inc(ffn_squares, 1)
                else:
                    for kt in range(KT):
                        eng.wait_ge(normed_t, NORMED_T[name] + kt + 1)
                        eng.activation(xs[:, kt, 0:S], normed[:, kt, :], ACT.Copy).then_inc(split_h, 1)

            def between(name):
                if name == "mem_k":
                    eng.wait_ge(par_in, 16)
                    split_high(0, REG[name], 0, None)
                    split_high(1, REG[name], 0, None)
                    split_high(0, REG[name], 1, None)
                    eng.wait_ge(angles, 1)
                    eng.activation(sin[:, :], ang[:, 0, :], ACT.Sin)
                    eng.activation(cos[:, :], ang[:, 1, :], ACT.Sin).then_inc(tables, 1)
                for step in after_steps(name):
                    do(*step)
                if mix_split(name) is not None:
                    n = mix_split(name)
                    for c in MIX_ORDER[n] if n == DEPTH else MIX_ORDER[n][3:]:
                        do("mix_split", n, c)
                for n in norms_before(name):
                    norm(n)

            walk(eng, slot, between)

        @block.vector
        def _(eng):
            chain = Chain(eng, dve_order)
            step_ = chain.step

            def split_low(r, k, i):
                s = r.s0 + k
                w = slice(8 * P, (8 + r.pieces[1]) * P)
                eng.wait_ge(highs, val(2 * s + 2, 8, i))
                eng.tensor_tensor(low[:, s % SPLIT, w], raw[:, s % RAW, r.pieces[0] * P:r.blocks * P], high[:, s % SPLIT, w].bitcast(F32),
                                  ALU.subtract).then_inc(lows_b, 1)

            def slot(r, k, i):
                nxt = following(r, k, i)
                if nxt:
                    split_low(*nxt)
                for step in steps_at(r, k, i):
                    do(*step)
                for tile, per, prod_, pper in tiles_done(r, k, i):
                    store(r, k, i, tile, per)

            def store(r, k, i, tile, per):
                T = r.t0 + tile
                first, second = acc[T % 2][:, 0:S], lowsum[:, T % 2, :]
                eng.wait_ge(low_ready, val(T + 1, per, i))

                def done(ins, and_wait=False):
                    ins.then_inc(stored, 1)
                    if and_wait:
                        eng.wait_ge(stored, val(T + 1, per, i))

                if r.kind in ("natural", "uv"):
                    done(eng.tensor_copy(natural_dest(r, tile)[:, S:2 * S], acc[T % 2][:, S:2 * S]))
                elif r.name[:2] == "up":
                    out_ = gate if k % 2 == 0 else up
                    step_(eng.tensor_tensor(out_[:, :], first, second, ALU.add))
                    done(eng.tensor_tensor(out_[:, :], out_[:, :], factor[:, :], ALU.mult), True)
                    if k % 2 == 0:
                        return
                    hid = val(k // 2, 2, i)
                    eng.wait_ge(silu_done, val(r.pair0 + k // 2 + 1, 2, i))
                    step_(eng.tensor_tensor(hidden[:, hid, 0:S], silu_g[:, :], up[:, :], ALU.mult))
                    step_(eng.tensor_tensor(prod[:, :], silu_g[:, :], up[:, :], ALU.mult))
                    eng.tensor_tensor(hidden[:, hid, S:2 * S], prod[:, :], hidden[:, hid, 0:S].bitcast(F32),
                                      ALU.subtract).then_inc(hidden_done, 1)
                    eng.wait_ge(hidden_done, val(r.pair0 + k // 2 + 1, 2, i))
                elif r.kind == "down":
                    xt = x[:, val(tile, per, i), :]
                    step_(eng.scalar_tensor_tensor(out=xt, in0=first, scalar=0.5, in1=xt, op0=ALU.mult, op1=ALU.add))
                    done(eng.tensor_tensor(xt, xt, second, ALU.add), r.name == "down11")
                    if r.name == "down11":
                        add_squares("mix", late_moment, late_moment[:, 0:S], xt, i is None and tile == KT - 1)
                elif r.name[:3] == "out":
                    xt = x[:, tile, :]
                    step_(eng.scalar_tensor_tensor(out=xt, in0=xt, scalar=ALPHA, in1=first, op0=ALU.mult, op1=ALU.add))
                    done(eng.scalar_tensor_tensor(out=xt, in0=second, scalar=p_("b_out", KT * r.layer + tile), in1=xt,
                                                  op0=ALU.add, op1=ALU.add))
                elif r.name == "mixout":
                    xt = x[:, tile, :]
                    step_(eng.tensor_tensor(xt, first, xt, ALU.add))
                    done(eng.tensor_tensor(xt, xt, second, ALU.add), True)
                    add_squares("ffn2", moment, moment_sq[:, :], xt, tile == KT - 1)
                elif r.kind == "pool":
                    done(eng.tensor_tensor(gate[:, :], first, second, ALU.add), True)
                    ins = eng.scalar_tensor_tensor(out=mix[:, 8 + tile, :], in0=gate[:, :],
                                                   scalar=p_("pool_s", GROUPS * r.layer + tile),
                                                   in1=mix[:, 8 + tile, :], op0=ALU.mult, op1=ALU.mult)
                    final(ins, 2 * r.layer + 1 if tile == GROUPS - 1 else None)
                elif r.name[:4] == "in_c" and tile % 4 == 3:
                    done(eng.tensor_tensor(branch[:, 2, :], first, second, ALU.add), True)
                    g = tile // 4
                    ins = eng.tensor_tensor(mix[:, 12 + g, :], mix[:, 12 + g, :], branch[:, 2, :], ALU.mult)
                    final(ins, 2 * r.layer + 2 if g == GROUPS - 1 else None)
                else:
                    done(eng.tensor_tensor(tile_dest(r, tile), first, second, ALU.add))

            def final(ins, count):
                if count:
                    ins.then_inc(mix_final, 1)
                    eng.wait_ge(mix_final, count)
                else:
                    step_(ins)

            def added(name, ins, last):
                if last:
                    ins.then_inc(moments_in, 1)
                    eng.wait_ge(moments_in, N_OF[name])
                else:
                    step_(ins)

            def add_squares(name, run, tmp, xt, last):
                step_(eng.tensor_tensor(tmp, xt, xt, ALU.mult))
                added(name, eng.tensor_tensor(run[:, S:2 * S], run[:, S:2 * S], tmp, ALU.add), last)

            def tile_there(name, kt):
                if name == "emb":
                    eng.wait_ge(x_in, 16)
                else:
                    eng.wait_ge(stored, input_region(name).t0 + kt + 1)

            def moments(name, tiles):
                for kt in tiles:
                    tile_there(name, kt)
                    e = normed[:, kt, :]
                    step_(eng.tensor_tensor(e, x[:, kt, :], shift[:, :], ALU.add))
                    step_(eng.tensor_tensor(moment[:, 0:S], moment[:, 0:S], e, ALU.add))
                    add_squares(name, moment, moment_sq[:, :], e, kt == KT - 1)

            def variance_of(name):
                c = N_OF[name]
                eng.wait_ge(sumsq, c + 1)
                eps = LN_EPS if name in LAYER_NORMS else RMS_EPS
                ins = eng.tensor_scalar(scale_a[:, 0:S], sums[:, S:2 * S], 1.0 / D, eps, ALU.mult, ALU.add)
                if name in LAYER_NORMS:
                    step_(ins)
                    step_(eng.tensor_scalar(mean[:, :], sums[:, 0:S], 1.0 / D, None, ALU.mult))
                    step_(eng.tensor_tensor(moment_sq[:, :], mean[:, :], mean[:, :], ALU.mult))
                    ins = eng.tensor_tensor(scale_a[:, 0:S], scale_a[:, 0:S], moment_sq[:, :], ALU.subtract)
                ins.then_inc(variance, 1)
                eng.wait_ge(root, c + 1)

            def split_low_of(name, kt, gain=None):
                if low_count(name, kt)[0] != "v":
                    return
                eng.wait_ge(split_h, high_count(name, kt))
                hi = xs[:, kt, 0:S].bitcast(F32)
                if gain:
                    ins = eng.scalar_tensor_tensor(out=xs[:, kt, S:2 * S], in0=x[:, kt, :], scalar=p_(gain, kt), in1=hi,
                                                   op0=ALU.mult, op1=ALU.subtract)
                else:
                    ins = eng.tensor_tensor(xs[:, kt, S:2 * S], normed[:, kt, :], hi, ALU.subtract)
                ins.then_inc(split_l["v"], 1)

            def rotate(x1, x2, c, s_, tmp, out1, out2, last):
                step_(eng.tensor_tensor(tmp[0], x1, c, ALU.mult))
                step_(eng.tensor_tensor(tmp[1], x2, s_, ALU.mult))
                step_(eng.tensor_tensor(tmp[2], x2, c, ALU.mult))
                step_(eng.tensor_tensor(tmp[3], x1, s_, ALU.mult))
                step_(eng.tensor_tensor(out1, tmp[0], tmp[1], ALU.subtract))
                eng.tensor_tensor(out2, tmp[2], tmp[3], ALU.add).then_inc(roped, 1)
                eng.wait_ge(roped, last)

            def do(kind, *a):
                if kind == "first_sum":
                    name, n = a[0], LAYER_NORMS.index(a[0])
                    tile_there(name, SHIFT_TILES - 1)
                    if name == "emb":
                        eng.wait_ge(split_l["g"], low_count("mem", KT - 2)[1])
                    for kt in range(1, SHIFT_TILES):
                        ins = eng.tensor_tensor(moment[:, 0:S], x[:, kt, :], x[:, 0, :] if kt == 1 else moment[:, 0:S], ALU.add)
                        if kt < SHIFT_TILES - 1:
                            step_(ins)
                    ins.then_inc(first_in, 1)
                elif kind == "shift":
                    n = LAYER_NORMS.index(a[0])
                    eng.wait_ge(first_sum, n + 1)
                    eng.tensor_scalar(shift[:, :], sums[:, 0:S], -1.0 / (SHIFT_TILES * P), None, ALU.mult)\
                        .then_inc(shifted_by, 1)
                    eng.wait_ge(shifted_by, n + 1)
                    step_(eng.memset(moment[:, :], 0.0))
                elif kind == "moments":
                    moments(a[0], a[1:])
                elif kind == "gain":
                    split_low_of(a[0], a[1], "ffn2_g")
                elif kind == "factor":
                    variance_of(a[0])
                    step_(eng.reciprocal(factor[:, :], scale_b[:, 0:S]))
                elif kind == "lat_scale":
                    layer = a[0]
                    eng.wait_ge(lat_sums, layer + 1)
                    step_(eng.tensor_scalar(scale_a[:, 0:S], sums[:, 0:S], 1.0 / QLAT, RMS_EPS, ALU.mult, ALU.add))
                    eng.tensor_scalar(scale_a[:, S:2 * S], sums[:, S:2 * S], 1.0 / KVLAT, RMS_EPS, ALU.mult, ALU.add)\
                        .then_inc(lat_var, 1)
                    eng.wait_ge(lat_root, layer + 1)
                    step_(eng.reciprocal(scale_a[:, :], scale_b[:, :]))
                    for n in range(KQ + KKV):
                        g, o_ = (p_("q_g", KQ * layer + n), 0) if n < KQ else (p_("kv_g", KKV * layer + n - KQ), S)
                        step_(eng.scalar_tensor_tensor(out=lat[:, n, :], in0=lat[:, n, :], scalar=g,
                                                       in1=scale_a[:, o_:o_ + S], op0=ALU.mult, op1=ALU.mult))
                elif kind == "lat_split":
                    n = KQ + KKV
                    step_(eng.tensor_copy(lats[:, :, 0:S], lat[:, 0:n, :]))
                    eng.tensor_tensor(lats[:, :, S:2 * S], lat[:, 0:n, :], lats[:, :, 0:S].bitcast(F32), ALU.subtract)\
                        .then_inc(lat_ready, 1)
                elif kind == "rope_k":
                    layer = a[0]
                    eng.wait_ge(tables, 1)
                    eng.wait_ge(stored, REG[f"in_a{layer}"].t0 + 8)
                    rotate(lat[:, 6, :], lat[:, 7, :], cos[:, :], sin[:, :], [rope_u[:, n, :] for n in range(4)],
                           kr[:, 0, :], kr[:, 1, :], 2 * layer + 1)
                elif kind == "rope_q":
                    layer = a[0]
                    wide = [tt[:, :].unsqueeze(1).to_broadcast([P, 2, S]) for tt in (cos, sin)]
                    eng.wait_ge(stored, REG[f"uk{layer}"].t0)
                    rotate(q[:, 8:10, :], q[:, 10:12, :], *wide, [rope_t[:, n, :, :] for n in range(4)],
                           q[:, 8:10, :], q[:, 10:12, :], 2 * layer + 2)
                elif kind == "silu":
                    n, dest = a
                    eng.wait_ge(gate_exp, n + 1)
                    step_(eng.tensor_scalar(prod[:, :], up[:, :], 1.0, None, ALU.add))
                    step_(eng.reciprocal(gate[:, :], prod[:, :]))
                    eng.tensor_tensor(mix[:, dest, :], mix[:, dest, :], gate[:, :], ALU.mult).then_inc(gated, 1)
                    eng.wait_ge(gated, n + 1)
                elif kind == "conv":
                    layer, g = a

                    def tap(w):
                        return p_("conv", (3 * layer + w) * GROUPS + g)

                    eng.wait_ge(stored, REG[f"in_c{layer}"].t0 + 4 * g + 3)
                    u, y = silu_g[:, :], scale_c[:, 0:S]
                    step_(eng.tensor_tensor(u, branch[:, 0, :], branch[:, 1, :], ALU.mult))
                    step_(eng.tensor_scalar(y, u, tap(2), None, ALU.mult))
                    for back in (1, 2):
                        step_(eng.scalar_tensor_tensor(out=y[:, back:S], in0=u[:, 0:S - back], scalar=tap(2 - back),
                                                       in1=y[:, back:S], op0=ALU.mult, op1=ALU.add))
                    step_(eng.tensor_tensor(mix[:, 12 + g, :], mix[:, 12 + g, :], y, ALU.mult))
                elif kind == "pool":
                    layer, g = a
                    w = WINDOWS[g]
                    src = branch[:, 3, :]
                    eng.wait_ge(stored, REG[f"in_b{layer}"].t0 + 2 * g + 1)
                    halves = [scale_b[:, 0:S], scale_b[:, S:2 * S]]
                    cur, back, n = src, 1, 0
                    while back < w:
                        nxt = halves[n % 2]
                        step_(eng.tensor_tensor(nxt[:, back:S], cur[:, back:S], cur[:, 0:S - back], ALU.add))
                        step_(eng.tensor_copy(nxt[:, 0:back], cur[:, 0:back]))
                        cur, back, n = nxt, back * 2, n + 1
                    y = halves[n % 2]
                    step_(eng.scalar_tensor_tensor(out=y[:, w:S], in0=cur[:, w:S], scalar=1.0 / w, in1=src[:, w:S],
                                                   op0=ALU.mult, op1=ALU.subtract))
                    step_(eng.tensor_tensor(y[:, 0:w], cur[:, 0:w], p_("count", 0, w), ALU.mult))
                    step_(eng.tensor_tensor(y[:, 0:w], y[:, 0:w], src[:, 0:w], ALU.subtract))
                    step_(eng.tensor_copy(pooled[:, g, 0:S], y))
                    eng.tensor_tensor(pooled[:, g, S:2 * S], y, pooled[:, g, 0:S].bitcast(F32), ALU.subtract)\
                        .then_inc(pool_ready, 1)
                    eng.wait_ge(pool_ready, GROUPS * layer + g + 1)
                elif kind == "headnorm":
                    p = a[0]
                    pair, gain = pair_of(p)
                    eng.wait_ge(pair_sum, p + 1)
                    eng.tensor_scalar(scale_b[:, :], sums[:, :], 1.0 / P, RMS_EPS, ALU.mult, ALU.add)\
                        .then_inc(pair_var, 1)
                    eng.wait_ge(pair_exp, p + 1)
                    step_(eng.scalar_tensor_tensor(out=scale_c[:, :], in0=scale_a[:, :], scalar=-0.5, in1=scale_a[:, :],
                                                   op0=ALU.mult, op1=ALU.mult))
                    step_(eng.tensor_tensor(scale_c[:, :], scale_c[:, :], scale_b[:, :], ALU.mult))
                    step_(eng.scalar_tensor_tensor(out=scale_c[:, :], in0=scale_c[:, :], scalar=1.5, in1=scale_a[:, :],
                                                   op0=ALU.add, op1=ALU.mult))
                    eng.scalar_tensor_tensor(out=flat(pair), in0=flat(pair), scalar=p_(gain), in1=scale_c[:, :],
                                             op0=ALU.mult, op1=ALU.mult).then_inc(pair_done, 1)
                    eng.wait_ge(pair_done, p + 1)
                elif kind == "forget":
                    eng.wait_ge(logits, 1)
                    step_(eng.tensor_copy(prod[0:FOX, :], sums[0:FOX, S:2 * S]))
                    eng.tensor_tensor(up[0:FOX, :], sums[0:FOX, 0:S], prod[0:FOX, :], ALU.add).then_inc(logit_rows, 1)
                elif kind == "forget_turn":
                    eng.wait_ge(logits, 2)
                    for b in range(TB):
                        step_(eng.tensor_tensor(fz[:, 0, b, :], sums[:, 8 * b:8 * b + FOX], p_("forget", 0, FOX), ALU.add))
                    step_(eng.tensor_scalar(fz[:, 1, :, :], fz[:, 0, :, :], -1.0, None, ALU.mult))
                    eng.tensor_tensor(fz[:, 1, :, :], fz[:, 1, :, :], fz[:, 0, :, :], ALU.min).then_inc(logit_in, 1)
                    eng.wait_ge(soft_ln, 1)
                    step_(eng.scalar_tensor_tensor(out=fz[:, 0, :, :], in0=fz[:, 0, :, :], scalar=0.0, in1=fz[:, 3, :, :],
                                                   op0=ALU.min, op1=ALU.subtract))
                    for h in range(FOX):
                        for b in range(TB):
                            ins = eng.tensor_scalar(lf_rows[:, h, b, :], ones, fz[:, 0, b, h:h + 1], -1.0,
                                                    ALU.mult, ALU.mult)
                    ins.then_inc(logf, 1)
                elif kind == "decay":
                    h = a[0]
                    if h == 0:
                        eng.wait_ge(cum_sum, 1)
                        for b in range(TB):
                            ins = eng.tensor_copy(cum[:, b, :], sums[:, 8 * b:8 * b + FOX])
                        ins.then_inc(cum_done, 1)
                    eng.wait_ge(decay_sum, h + 1)
                    eng.tensor_copy(decay[:, h, :], sums[:, 0:S]).then_inc(decay_done, 1)
                elif kind == "scores":
                    shifted_scores(a[0])
                elif kind == "exps":
                    softmax(a[0])
                elif kind == "mix_split":
                    layer, c = a
                    eng.wait_ge(mix_h, 4 * layer + MIX_ORDER[layer].index(c) + 1)
                    w = slice(4 * c, 4 * c + 4)
                    eng.tensor_tensor(mixs[:, w, S:2 * S], mix[:, w, :], mixs[:, w, 0:S].bitcast(F32), ALU.subtract)\
                        .then_inc(mix_l, 1)
                elif kind == "mixv":
                    n = a[0]
                    what, h, _, _, dest = head_spec(n)
                    eng.wait_ge(mixed, n + 1)
                    if what == "mla":
                        eng.tensor_tensor(mix[:, dest, :], head_ps[n % 2][:, 0:S], mix[:, dest, :], ALU.mult)\
                            .then_inc(head_out, 1)
                    else:
                        eng.tensor_copy(mix[:, dest, :], head_ps[n % 2][:, 0:S]).then_inc(head_out, 1)

            def shifted_scores(n):
                what, h, _, _, _ = head_spec(n)
                pr, sc = prob[:, n % 2, :, :], score[n % 2]
                eng.wait_ge(scores_done, n + 1)
                if n >= 2:
                    eng.wait_ge(turns, n - 1)
                if n == 0:
                    eng.wait_ge(masks_in, 16)
                if what == "fox":
                    eng.wait_ge(decay_done, FOX)
                    for b in range(TB):
                        w = keys_seen(what, b)
                        ins = eng.scalar_tensor_tensor(out=pr[:, b, 0:w], in0=sc[:, b, 0:w], scalar=cum[:, b, h:h + 1],
                                                       in1=decay[:, h, 0:w], op0=ALU.add, op1=ALU.add)
                    step_(ins)
                slope = float(np.float32(2.0 ** (-8.0 * (h + 1) / SWA)))
                for b in range(TB):
                    w = keys_seen(what, b)
                    to, from_ = pr[:, b, 0:w], sc[:, b, 0:w]
                    if what == "mla":
                        ins = eng.scalar_tensor_tensor(out=to, in0=from_, scalar=MLA_SCALE, in1=causal[:, b, 0:w],
                                                       op0=ALU.mult, op1=ALU.add)
                    elif what == "mem":
                        ins = eng.tensor_copy(to, from_)
                    elif what == "fox":
                        ins = eng.tensor_tensor(to, to, causal[:, b, 0:w], ALU.add)
                    else:
                        ins = eng.scalar_tensor_tensor(out=to, in0=dist[:, b, 0:w], scalar=-slope, in1=from_,
                                                       op0=ALU.mult, op1=ALU.add)
                    ins.then_inc(shifted, 1)
                eng.wait_ge(shifted, TB * (n + 1))
                for b in range(TB):
                    neg = stat[:, n % 2, b:b + 1]
                    ins = eng.tensor_reduce(neg, pr[:, b, 0:keys_seen(what, b)], AX.X, ALU.max, negate=True)
                    if what == "swa":
                        step_(ins)
                        ins = eng.tensor_scalar(neg, neg, neg_sink[:, h:h + 1], None, ALU.min)
                    ins.then_inc(negmax, 1)

            def softmax(n):
                what, h, _, _, _ = head_spec(n)
                pr = prob[:, n % 2, :, :]
                total, inv = stat[:, n % 2, 2:4], stat[:, n % 2, 6:8]
                eng.wait_ge(exps, TB * (n + 1))
                if what == "swa":
                    eng.wait_ge(sink_exp, h + 1)
                    step_(eng.tensor_tensor(total, total, stat[:, n % 2, 4:6], ALU.add))
                step_(eng.reciprocal(inv, total))
                for b in range(TB):
                    w = keys_seen(what, b)
                    eng.tensor_scalar(pr[:, b, 0:w], pr[:, b, 0:w], inv[:, b:b + 1], None, ALU.mult).then_inc(probs, 1)

            def norm(name):
                if name == "ffn2":
                    split_low_of(name, KT - 1, "ffn2_g")
                    return
                if name in ("ln0", "ln1"):
                    moments(name, [KT - 1])
                variance_of(name)
                inv = scale_a[:, 0:S]
                step_(eng.reciprocal(inv, scale_b[:, 0:S]))
                if name in LAYER_NORMS:
                    for n, (lo, hi) in enumerate(CUTS):
                        e = normed[:, lo:hi, :]
                        wide = [v.unsqueeze(1).to_broadcast([P, hi - lo, S]) for v in (mean[:, :], inv)]
                        step_(eng.tensor_tensor(e, e, wide[0], ALU.subtract))
                        eng.tensor_tensor(e, e, wide[1], ALU.mult).then_inc(normed_t, 1)
                        if name == "ln1" and n:
                            for kt in range(*CUTS[n - 1]):
                                split_low_of(name, kt, "ffn1_g")
                    if name == "ln1":
                        for kt in range(*CUTS[-1]):
                            split_low_of(name, kt, "ffn1_g")
                        eng.wait_ge(ffn_squares, KT)
                        step_(eng.tensor_tensor(moment[:, S:2 * S], square[:, 0, :], square[:, 1, :], ALU.add))
                        for kt in range(2, KT):
                            added("ffn1", eng.tensor_tensor(moment[:, S:2 * S], moment[:, S:2 * S], square[:, kt, :],
                                                            ALU.add), kt == KT - 1)
                    return
                gain, src = ("mem_g", memx) if name == "mem" else ("mix_g", x)
                for kt in range(KT):
                    eng.scalar_tensor_tensor(out=normed[:, kt, :], in0=src[:, kt, :], scalar=p_(gain, kt),
                                             in1=inv, op0=ALU.mult, op1=ALU.mult).then_inc(normed_t, 1)
                    if kt > 2:
                        split_low_of(name, kt - 3)
                for kt in range(KT - 3, KT):
                    split_low_of(name, kt)

            def rope_angles():
                eng.wait_ge(pos_in, 16)
                eng.wait_ge(par_in, 16)
                a0, a1, turns_, r, m = (ang[:, n, :] for n in range(5))
                step_(eng.tensor_copy(r, pos[:, :]))
                step_(eng.tensor_scalar(a0, r, p_("inv_freq"), None, ALU.mult))
                step_(eng.tensor_scalar(turns_, a0, INV_2PI, MAGIC, ALU.mult, ALU.add))
                step_(eng.tensor_scalar(turns_, turns_, -MAGIC, None, ALU.add))
                for part in (PI_A, PI_B, PI_C):
                    step_(eng.scalar_tensor_tensor(out=a0, in0=turns_, scalar=-part, in1=a0, op0=ALU.mult, op1=ALU.add))
                step_(eng.tensor_scalar(a1, a0, float(np.pi / 2), None, ALU.add))
                step_(eng.tensor_scalar(m, a1, PI_IN, -2 * float(np.pi), ALU.is_gt, ALU.mult))
                step_(eng.tensor_tensor(a1, a1, m, ALU.add))
                step_(eng.tensor_scalar(a0, a0, PI_IN, -PI_IN, ALU.min, ALU.max))
                eng.tensor_scalar(a1, a1, PI_IN, -PI_IN, ALU.min, ALU.max).then_inc(angles, 1)

            def between(name):
                if name == "mem_k":
                    split_low(REG[name], 0, None)
                    rope_angles()
                    for g in ("fox_q", "swa_q", "mem_q"):
                        step_(eng.tensor_scalar(p_(g), p_(g), HEAD_SCALE, None, ALU.mult))
                    step_(eng.tensor_scalar(neg_sink[:, :], p_("sinks", 0, SWA), -1.0, None, ALU.mult))
                if name == "in_a0":
                    eng.wait_ge(wf_in, 16)
                    flat_h = wfh[:, :, :].rearrange("p k f -> p (k f)")
                    step_(eng.tensor_copy(flat_h, wf[:, :]))
                    eng.tensor_tensor(wfl[:, :, :].rearrange("p k f -> p (k f)"), wf[:, :], flat_h.bitcast(F32),
                                      ALU.subtract).then_inc(wf_split, 1)
                for step in after_steps(name):
                    do(*step)
                if mix_split(name) is not None:
                    n = mix_split(name)
                    for c in MIX_ORDER[n] if n == DEPTH else MIX_ORDER[n][3:]:
                        do("mix_split", n, c)
                for n in norms_before(name):
                    norm(n)
                if name in ("down11", "mixout"):
                    step_(eng.memset((late_moment if name == "down11" else moment)[:, :], 0.0))

            walk(eng, slot, between, chain)

        @block.gpsimd
        def _(eng):
            def split_low(r, k, i):
                s = r.s0 + k
                w = slice(0, r.pieces[0] * P)
                eng.wait_ge(highs, val(2 * s + 1, 8, i))
                eng.tensor_tensor(low[:, s % SPLIT, w], raw[:, s % RAW, w], high[:, s % SPLIT, w].bitcast(F32),
                                  ALU.subtract).then_inc(lows_a, 1)

            def slot(r, k, i):
                nxt = following(r, k, i)
                if nxt:
                    split_low(*nxt)

            def between(name):
                if name == "mem_k":
                    split_low(REG[name], 0, None)
                for n in norms_before(name):
                    y = x if n in LAYER_NORMS else normed
                    for kt in range(KT):
                        who, _ = low_count(n, kt)
                        if who == "g":
                            eng.wait_ge(split_h, high_count(n, kt))
                            eng.tensor_tensor(xs[:, kt, S:2 * S], y[:, kt, :], xs[:, kt, 0:S].bitcast(F32),
                                              ALU.subtract).then_inc(split_l["g"], 1)

            walk(eng, slot, between)


class Chain:

    def __init__(self, eng, sem):
        self.eng, self.sem, self.n, self.i, self.per = eng, sem, 0, None, 0

    def enter(self, i, r):
        self.i, self.per, self.start = i, 8 if r.kind == "tile" else 6 if r.name == "down11" else 2, self.n

    def leave(self, runs, r):
        assert self.n - self.start == self.per, (r.name, self.n - self.start)
        self.n, self.i = self.start + runs * self.per, None

    def step(self, ins):
        ins.then_inc(self.sem, 1)
        self.n += 1
        self.eng.wait_ge(self.sem, self.n if self.i is None else self.i * self.per + self.n)


def _tiles(w, columns=None):
    w = w if columns is None else w[:, columns]
    k, n = w.shape
    return np.ascontiguousarray(w.reshape(k // P, P, n // P, P).transpose(2, 1, 0, 3)).reshape(n // P, P, k)


def _rows(w, per, width):
    k, n = w.shape
    a = w.reshape(k // P // per, per, P, n // width, width).transpose(3, 0, 2, 1, 4)
    return np.ascontiguousarray(a).reshape(-1, P, per * width)


def _cols(v):
    return np.asarray(v).reshape(-1, P).T


def _all(v):
    return np.broadcast_to(np.asarray(v).reshape(1, -1), (P, np.size(v)))


def layout(inp):
    a = {k: np.asarray(v) for k, v in inp.items()}
    arange = np.arange
    out = {}
    starts = dict(zip(("q", "kv", "kr", "g", "p", "gp", "ch", "cb", "cc", "gc"),
                      np.cumsum([0, QLAT, KVLAT, ROPE, 1024, 512, 512, 512, 512, 512])))
    half = ROPE // 2
    first = [arange(QLAT + KVLAT), starts["kr"] + arange(P) % half, starts["kr"] + half + arange(P) % half,
             starts["g"] + arange(1024)]
    rest = [starts[n] + g * P + arange(P) for names in (("p", "gp"), ("gc", "ch", "cc", "cb"))
            for g in range(GROUPS) for n in names]
    columns = np.concatenate(first + rest)
    out["w_in"] = np.concatenate([_tiles(a["w_in"][l], columns) for l in range(DEPTH)])
    per = P + ROPE
    nope = (arange(HEADS)[:, None] * per + arange(P)).ravel()
    x1 = (arange(HEADS)[:, None] * per + P + arange(half)).ravel()
    uq = [_tiles(a["w_uq"][l], np.concatenate([nope, x1, x1 + half])) for l in range(DEPTH)]
    out["w_uq"] = np.concatenate([u.reshape(4, 3, P, QLAT).transpose(0, 2, 1, 3).reshape(4, P, 3 * QLAT) for u in uq])
    kcols = (arange(HEADS)[:, None] * 2 * P + arange(P)).ravel()
    out["w_uk"] = np.stack([_tiles(a["w_ukv"][l], kcols).transpose(1, 0, 2).reshape(P, -1) for l in range(DEPTH)])
    out["w_uv"] = np.concatenate([_rows(a["w_ukv"][l][:, kcols + P], KKV, 512) for l in range(DEPTH)])
    out["w_pool"] = np.ascontiguousarray(a["w_pool"].transpose(0, 2, 1, 3)).reshape(DEPTH, P, GROUPS * P)
    out["w_out"] = np.concatenate([_tiles(a["w_out"][l]) for l in range(DEPTH)])
    for part in ("1", "2"):
        up = np.stack([_tiles(a[f"ffn{part}_{n}_2"][0]) for n in ("gate", "up")], 1)
        out["w_up" + part] = up.reshape(2 * FT, P, D)
        down = a[f"ffn{part}_down_2"][0].reshape(CHUNKS, 2, HALF, P, KT, P).transpose(0, 4, 1, 3, 2, 5)
        out["w_down" + part] = np.ascontiguousarray(down).reshape(CHUNKS * KT * 2, P, HALF * P)
    w = a["w_in_2"][0]
    cuts = np.cumsum([0, FOX * P, FOX * P, FOX * P, FOX, SWA * P, SWA_KV * P, SWA_KV * P, MEM * P])
    fq, fk, fv, fl, sq, sk, sv, mq = (arange(cuts[n], cuts[n + 1]) for n in range(8))
    out["w_nat"] = _rows(w[:, np.concatenate([sv, fv])], 4, 512)
    order = [mq, sk, sq]
    for n in range(FOX // 2):
        order += [fk[2 * P * n:2 * P * (n + 1)], fq[2 * P * n:2 * P * (n + 1)]]
    out["w_heads"] = _tiles(w, np.concatenate(order))
    out["wf"] = np.ascontiguousarray(w[:, fl].reshape(KT, P, FOX).transpose(1, 0, 2)).reshape(P, KT * FOX)
    out["w_mixout"] = _tiles(a["w_out_2"][0])
    out["w_memk"] = _tiles(a["w_mem_k_2"][0])
    out["w_memv"] = _rows(a["w_mem_v_2"][0], 4, 512)
    for name, src in (("x", "x"), ("mem", "mem_2")):
        out[name] = np.ascontiguousarray(a[src][0].T.reshape(KT, P, S).transpose(1, 0, 2))
    out["positions"] = np.ascontiguousarray(np.broadcast_to(a["positions"], (P, S)))
    tok = arange(S)
    upto = (tok[:, None] <= tok[None, :]).astype(np.float32).reshape(TB, P, S).transpose(1, 0, 2).reshape(P, -1)
    gap = tok[:, None] - tok[None, :]
    causal = np.where(gap >= 0, 0.0, NEG)
    far = np.where((gap >= 0) & (gap < SWA_WINDOW), gap, FAR)
    causal, far = (m.astype(np.float32).reshape(TB, P, S).transpose(1, 0, 2).reshape(P, -1) for m in (causal, far))
    inv_freq = np.float32(10000.0) ** (-(arange(P) % half).astype(np.float32) / np.float32(half))
    values = dict(
        emb_g=_cols(a["emb_ln_g"]), emb_b=_cols(a["emb_ln_b"]), ffn1_g=_cols(a["ffn1_norm_2"]),
        mix_g=_cols(a["mix_norm_2"]), mem_g=_cols(a["mem_norm_2"]), ffn2_g=_cols(a["ffn2_norm_2"]),
        ln_g=_cols(a["ln_g"]), ln_b=_cols(a["ln_b"]), b_out=_cols(a["b_out"]), q_g=_cols(a["q_norm_g"]),
        kv_g=_cols(a["kv_norm_g"]), pool_s=_cols(a["pool_scale"]), conv=_cols(a["conv_w"]),
        fox_q=_cols(a["fox_q_gain_2"]), fox_k=_cols(a["fox_k_gain_2"]), swa_q=_cols(a["swa_q_gain_2"]),
        swa_k=_cols(a["swa_k_gain_2"]), mem_q=_cols(a["mem_q_gain_2"]), mem_k=_cols(a["mem_k_gain_2"]),
        forget=_all(a["forget_bias_2"]), sinks=_all(a["swa_sinks_2"]),
        inv_freq=inv_freq.reshape(P, 1).astype(np.float32),
        count=_all(1 / np.arange(1, max(WINDOWS) + 1, dtype=np.float32)),
        ident=np.eye(P, dtype=np.float32), ones=np.ones((P, P), np.float32), upto=upto, causal=causal, dist=far)
    out["par"] = np.ascontiguousarray(np.concatenate([values[n] for n, _ in COLUMNS], 1))
    return out


def kernel(**inputs):
    import concourse.bacc as bacc
    from concourse.bass_utils import run_bass_kernel_spmd

    arrays = layout(inputs)
    nc = bacc.Bacc("TRN2", target_bir_lowering=False, num_devices=1, dynamic_dma_scratch_size=1024)
    t = {n: nc.dram_tensor(n + "_dram", v.shape, mybir.dt.from_np(v.dtype), kind="ExternalInput").ap()
         for n, v in arrays.items()}
    t["out"] = nc.dram_tensor("out_dram", (P, KT, S), F32, kind="ExternalOutput").ap()
    build(nc, t)
    r = run_bass_kernel_spmd(nc, [{n + "_dram": v for n, v in arrays.items()}], core_ids=[0])
    out = np.asarray(r.results[0]["out_dram"])
    return np.ascontiguousarray(out.transpose(2, 1, 0)).reshape(1, S, D)
```

```python
from contextlib import ExitStack

import numpy as np

import concourse.bass as bass
from concourse import mybir

F32 = mybir.dt.float32
F32R = mybir.dt.float32r
I32 = mybir.dt.int32
ALU = mybir.AluOpType
ACT = mybir.ActivationFunctionType
AX = mybir.AxisListType

P = 128
D = 2048
S = 256
KT = D // P
TB = S // P
DEPTH = 2
HEADS = 8
ROPE = 64
QLAT, KVLAT = 512, 256
KQ, KKV = QLAT // P, KVLAT // P
GROUPS = 4
WINDOWS = (2, 4, 8, 16)
FOX, SWA, SWA_KV, MEM = 6, 6, 2, 4
SWA_WINDOW = 128
FF = 5632
FT = FF // P
CHUNKS = 2
CT = FT // CHUNKS
HALF = CT // 2
LN_EPS, RMS_EPS = 1e-5, 1e-6
ALPHA = (2 * DEPTH) ** 0.25
MLA_SCALE = (128 + ROPE) ** -0.5
HEAD_SCALE = 128 ** -0.5
NEG = -1e30
FAR = 1e32
INV_2PI = float(1 / (2 * np.pi))
MAGIC = 1.5 * 2.0 ** 23
PI_A = 6.28125
PI_B = float(np.float32(np.round((2 * np.pi - PI_A) * 2 ** 20) / 2 ** 20))
PI_C = float(2 * np.pi - PI_A - PI_B)
PI_IN = float(np.nextafter(np.float32(np.pi), np.float32(0)))

COLUMNS, AT = [], {}


def _column(name, width):
    AT[name] = (sum(w for _, w in COLUMNS), width)
    COLUMNS.append((name, width))


for _name, _width in (
        ("emb_g", KT), ("emb_b", KT), ("ffn1_g", KT), ("mix_g", KT), ("mem_g", KT), ("ffn2_g", KT),
        ("ln_g", DEPTH * KT), ("ln_b", DEPTH * KT), ("b_out", DEPTH * KT),
        ("q_g", DEPTH * KQ), ("kv_g", DEPTH * KKV), ("pool_s", DEPTH * GROUPS), ("conv", DEPTH * 3 * GROUPS),
        ("fox_q", 1), ("fox_k", 1), ("swa_q", 1), ("swa_k", 1), ("mem_q", 1), ("mem_k", 1),
        ("forget", FOX), ("sinks", SWA), ("inv_freq", 1), ("rope_sign", 1), ("count", max(WINDOWS)),
        ("ident", P), ("ones", P), ("upto", TB * S), ("causal", TB * S), ("dist", TB * S)):
    _column(_name, _width)
NPAR = sum(w for _, w in COLUMNS)


class Region:
    def __init__(self, name, slabs, pieces, tiles, groups):
        self.name, self.n, self.pieces, self.tiles, self.groups = name, slabs, pieces, tiles, groups
        self.blocks = sum(pieces)


def plan():
    regions = [Region("mem_k", 4, (8, 8), 4, 2), Region("mem_v", 4, (8, 8), TB, 2)]
    for layer in range(DEPTH):
        regions += [
            Region(f"in_a{layer}", 16, (8, 8), 16, 2), Region(f"uq{layer}", 4, (4, 8), 12, 3),
            Region(f"uk{layer}", 1, (8, 8), 8, 8), Region(f"uv{layer}", 2, (4, 4), 2 * TB, 2),
            Region(f"in_b{layer}", 8, (8, 8), 8, 2), Region(f"pool{layer}", 1, (2, 2), 4, 4),
            Region(f"in_c{layer}", 16, (8, 8), 16, 2),
            Region(f"out{layer}", KT, (8, 8), KT, 2)]
    for part in (1, 2):
        if part == 2:
            regions += [Region("nat0", 4, (8, 8), TB, 2), Region("heads", 24, (8, 8), 24, 2),
                        Region("nat1", 4, (8, 8), TB, 2), Region("mixout", KT, (8, 8), KT, 2)]
        for c in range(CHUNKS):
            regions += [Region(f"up{part}{c}", 2 * CT, (8, 8), 2 * CT, 2),
                        Region(f"down{part}{c}", 2 * KT, (6, 5), KT, 2)]
    s = t = g = pairs = 0
    used = {}
    for r in regions:
        r.s0, r.t0, r.g0 = s, t, g
        s, t, g = s + r.n, t + r.tiles, g + r.n * r.groups
        r.kind = next((k for n, k in (("up", "tile"), ("down", "down"), ("uq", "uq"), ("uk", "uk"), ("uv", "uv"),
                                      ("pool", "pool"), ("mem_v", "natural"), ("nat", "natural"))
                       if r.name.startswith(n)), "tile")
        r.layer = int(r.name[-1]) if r.name[-1].isdigit() else 0
        r.array = {"in_": "w_in", "uq": "w_uq", "uk": "w_uk", "uv": "w_uv", "pool": "w_pool", "out": "w_out",
                   "mem_k": "w_memk", "mem_v": "w_memv", "nat": "w_nat", "heads": "w_heads", "mixout": "w_mixout",
                   "up1": "w_up1", "up2": "w_up2", "down1": "w_down1", "down2": "w_down2"}[
                       next(n for n in ("in_", "uq", "uk", "uv", "pool", "out", "mem_k", "mem_v", "nat", "heads",
                                        "mixout", "up1", "up2", "down1", "down2") if r.name.startswith(n))]
        r.a0 = used.get(r.array, 0)
        used[r.array] = r.a0 + r.n
        r.looped = r.name.startswith(("up", "down"))
        r.first = 4 if r.name in ("up10", "up20") else 0
        if r.looped:
            assert r.s0 % 4 == 0 and r.t0 % 2 == 0
        r.pair0 = pairs
        if r.name.startswith("up"):
            pairs += r.n // 2
        r.hidden0 = pairs - CT
    return regions


REGIONS = plan()
REG = {r.name: r for r in REGIONS}
ORDER = [r.name for r in REGIONS]
RAW = 4
TURNED = 4
SPLIT = 2


def region_of(s):
    return next(r for r in REGIONS if r.s0 <= s < r.s0 + r.n)


def released(s, piece):
    r = region_of(s)
    at = r.g0 + (s - r.s0) * r.groups
    if r.name[:2] == "uv" or piece == 1:
        return at + r.groups
    return at + {2: 1, 3: 1, 8: 4, 4: 2}[r.groups]


NORMS = ("mem", "emb", "ln0", "ln1", "ffn1", "mix", "ffn2")
N_OF = {n: i for i, n in enumerate(NORMS)}
LAYER_NORMS = ("emb", "ln0", "ln1")
SHIFT_TILES = 4
CUTS = ((0, 1), (1, 4), (4, 8), (8, 12), (12, 16))
FILLS = {"mem": "gv", "emb": "gg", "ln0": "gg", "ln1": "vv", "mix": "gv", "ffn2": "vv"}
NORMED_T = {}
_n = 0
for _name in NORMS:
    NORMED_T[_name] = _n
    _n += {"mem": KT, "mix": KT}.get(_name, len(CUTS) if _name in LAYER_NORMS else 0)


def high_count(name, kt):
    return KT * list(FILLS).index(name) + kt + 1


def low_count(name, kt):
    who, n = FILLS[name][kt % 2], 0
    for other, engines in FILLS.items():
        for k in range(KT if other != name else kt + 1):
            n += engines[k % 2] == who
        if other == name:
            return who, n


MEM_STEPS = {("mem_k", 0): [("first_sum", "emb")], ("mem_k", 1): [("shift", "emb"), ("moments", "emb", 0, 2)],
             ("mem_k", 2): [("moments", "emb", 2, 5)], ("mem_k", 3): [("moments", "emb", 5, 7)],
             ("mem_v", 0): [("moments", "emb", 7, 10)], ("mem_v", 1): [("moments", "emb", 10, 12)],
             ("mem_v", 2): [("moments", "emb", 12, 15)], ("mem_v", 3): [("moments", "emb", 15, KT)]}
TOGETHER = ("in_a0", "in_a1")


def head_steps(put, n, slot, last):
    put(slot, "scores", n)
    put(slot + 1, "exps", n)
    put(slot + 2, "turn", n)
    put(last, "mixv", n)


MLA_ALL = DEPTH * HEADS
SWA0, FOX0 = 4, 10
PAIRS = ["mem_q", "mem_q", "swa_k", "swa_q", "swa_q", "swa_q", "fox_k", "fox_q", "fox_k", "fox_q", "fox_k", "fox_q"]
MIX_ORDER = [(2, 0, 1, 3)] * DEPTH + [(0, 1, 2, 3)]


def layer_steps(layer):
    steps = {}

    def put(slot, *step):
        for name, first in (("in_a", 0), ("uq", 16), ("uk", 20), ("uv", 21), ("in_b", 23), ("pool", 31),
                            ("in_c", 32), ("out", 48)):
            r = REG[f"{name}{layer}"]
            if first <= slot < first + r.n:
                steps.setdefault((r.name, slot - first), []).append(step)

    if layer == 0:
        put(2, "tables")
        for p in range(2):
            put(4 + 2 * p, "square", p)
            put(5 + 2 * p, "headnorm", p)
    put(8, "lat_square", layer)
    put(9, "lat_scale", layer)
    put(10, "lat_split", layer)
    put(11, "rope_k", layer)
    put(23, "rope_q", layer)
    put(13, "silu", layer, 0, 4)
    put(17, "silu", layer, 4, 8)
    for h, slot in enumerate((24, 26, 28, 32, 34, 36, 38, 40)):
        head_steps(put, layer * HEADS + h, slot, slot + 3)
    for g in range(GROUPS):
        put(24 + 2 * g, "pool", layer, g)
        put(25 + 2 * g, "silu", layer, 8 + g, 9 + g)
        put(33 + 4 * g, "silu", layer, 12 + g, 13 + g)
        put(35 + 4 * g, "conv", layer, g)
    for slot, c in zip((44, 45, 46), MIX_ORDER[layer]):
        put(slot, "mix_split", layer, c)
    ln = f"ln{layer}"
    put(48 + 4, "first_sum", ln)
    put(48 + 5, "shift", ln)
    for k, lo, hi in [(5, 0, 2), (6, 2, 4), (7, 4, 6), (8, 6, 8)] + [(k, k - 1, k) for k in range(9, KT)]:
        put(48 + k, "moments", ln, lo, hi)
    return steps


def mix_steps():
    steps = {}

    def put(slot, *step):
        where = (("nat0", slot) if slot < 4 else ("heads", slot - 4) if slot < 28 else ("nat1", slot - 28)
                 if slot < 32 else ("after", slot - 32))
        steps.setdefault(where, []).append(step)

    put(1, "forget")
    put(2, "forget_turn")
    for h in range(FOX):
        put(4 + h // 2, "decay", h)
    for n, slot in enumerate((8, 9, 10, 12, 14, 15, 16, 17, 18, 20, 22, 24, 26, 28, 30, 30)):
        head_steps(put, MLA_ALL + n, slot, slot + 3 if n < FOX0 + 2 else max(32, slot + 3))
    for p in range(len(PAIRS)):
        put(6 + 2 * p, "square", 2 + p)
        put(7 + 2 * p, "headnorm", 2 + p)
    return steps


def ffn_steps():
    steps = {}
    for k in range(1, KT):
        steps[("mixout", k)] = [("gain", "ffn2", k - 1)]
    for part in (1, 2):
        steps[(f"up{part}0", 0)] = [("factor", f"ffn{part}")]
        steps[(f"up{part}0", 1)] = [("factor_sum", f"ffn{part}")]
    return steps


def in_order(steps):
    rank = {"mixv": 0, "turn": 1, "silu": 2, "exps": 2, "shift": 2, "square": 3, "headnorm": 3, "scores": 5}
    return {k: sorted(v, key=lambda x: rank.get(x[0], 4)) for k, v in steps.items()}


STEPS = dict(MEM_STEPS)
for _l in range(DEPTH):
    STEPS.update(layer_steps(_l))
STEPS.update(mix_steps())
STEPS.update(ffn_steps())
STEPS = in_order(STEPS)
AFTER = max(k[1] for k in STEPS if k[0] == "after") + 1


def build(nc, t):
    with ExitStack() as ctx:
        cursor = [(nc.sbuf_base + 31) // 32 * 32]

        def at(name, shape, dt, offset=None):
            size = int(np.prod(shape[1:])) * 4
            if offset is None:
                offset = cursor[0]
                cursor[0] += (size + 31) // 32 * 32
            return nc.alloc_sbuf_tensor_at(name, shape, dt, offset=offset)

        raw = at("raw", [P, RAW, 16 * P], F32)
        high = at("high", [P, SPLIT, 16 * P], F32R)
        low = at("low", [P, SPLIT, 16 * P], F32R)
        xs = at("xs", [P, KT, 2 * S], F32R)
        x = at("x", [P, KT, S], F32)
        memk = at("memk", [P, MEM, S], F32)
        memv = at("memv", [P, TB, MEM * P], F32)
        work = cursor[0]
        cursor[0] += 63488
        KB = 1024
        memx = at("memx", [P, KT, S], F32, work)
        square = at("square", [P, KT, S], F32, work + 16 * KB)
        mixs = at("mixs", [P, KT, 2 * S], F32R, work)
        moment = at("moment", [P, 2 * S], F32, work + 32 * KB)
        moment_sq = at("moment_sq", [P, 3, S], F32, work + 34 * KB)
        shift = at("shift", [P, S], F32, work + 37 * KB)
        factor = at("factor", [P, S], F32, work + 44 * KB)
        late_moment = at("late_moment", [P, 2 * S], F32, work + 46 * KB)
        normed = at("normed", [P, KT, S], F32, work + 46 * KB)
        hidden = at("hidden", [P, CT, 2 * S], F32R, work)
        lat = at("lat", [P, 8, S], F32, work)
        v_mla = at("v_mla", [P, TB, HEADS * P], F32, work)
        lats = at("lats", [P, KQ + KKV, 2 * S], F32R, work + 8 * KB)
        pooled = at("pooled", [P, GROUPS, 2 * S], F32R, work + 8 * KB)
        rope_b = at("rope_b", [P, HEADS // 2, S], F32, work + 8 * KB)
        branch = at("branch", [P, 4, S], F32, work + 32 * KB)
        q = at("q", [P, 12, S], F32, work + 20 * KB)
        lat_sq = at("lat_sq", [P, 6, S], F32, work + 24 * KB)
        kn = at("kn", [P, HEADS, S], F32, work + 36 * KB)
        kr = at("kr", [P, 2, S], F32, work + 44 * KB)
        mix = at("mix", [P, KT, S], F32, work + 46 * KB)
        feat = at("feat", [P, 24, S], F32, work)
        v_nat = at("v_nat", [P, TB, (FOX + SWA_KV) * P], F32, work + 24 * KB)
        decay = at("decay", [P, FOX, S], F32, work + 32 * KB)
        lf_rows = at("lf_rows", [P, FOX, TB, P], F32, work + 38 * KB)
        lowsum = at("lowsum", [P, 2, S], F32)
        gate = at("gate", [P, S], F32)
        silu_g = at("silu_g", [P, S], F32)
        up = at("up", [P, S], F32)
        prod = at("prod", [P, S], F32)
        prob = at("prob", [P, 2, TB, S], F32)
        turned = at("turned", [P, TURNED, TB, S], F32)
        scale_a = at("scale_a", [P, 2 * S], F32)
        square_h = at("square_h", [P, 2 * S], F32R)
        square_l = at("square_l", [P, 2 * S], F32R)
        ones_r = at("ones_r", [P, P], F32R)
        scale_b = at("scale_b", [P, 2 * S], F32)
        mean = at("mean", [P, S], F32, work + 45 * KB)
        dummy = at("dummy", [P, 1], F32)
        cos = at("cos", [P, S], F32)
        sin = at("sin", [P, S], F32)
        par = at("par", [P, NPAR], F32)
        stat = at("stat", [P, 2, 8], F32)
        wf = at("wf", [P, KT * FOX], F32)
        wfh = at("wfh", [P, KT, FOX], F32R)
        wfl = at("wfl", [P, KT, FOX], F32R)
        fz = at("fz", [P, 4, TB, FOX], F32)
        cum = at("cum", [P, TB, FOX], F32)
        neg_sink = at("neg_sink", [P, SWA], F32)
        scale_c = at("scale_c", [P, 2 * S], F32)
        pos = at("pos", [P, S], I32, work + 38 * KB)
        ang = at("ang", [P, 5, S], F32, work + 39 * KB)
        assert cursor[0] <= nc.sbuf_usable_end, cursor[0] - nc.sbuf_usable_end

        def bank(name, shape):
            return ctx.enter_context(nc.psum_tensor(name, shape, F32))

        acc = [bank(f"acc{i}", [P, 2 * S]) for i in range(2)]
        score = [bank(f"score{i}", [P, TB, S]) for i in range(2)]
        turn_ps = bank("turn_ps", [P, TB, S])
        head_ps = [bank(f"head_ps{i}", [P, 2 * S]) for i in range(2)]
        sums = bank("sums", [P, 2 * S])

        def sem(name):
            return ctx.enter_context(nc.semaphore(name))

        loaded = [sem(f"loaded{i}") for i in range(RAW)]
        highs = sem("highs")
        lows_a = sem("lows_a")
        lows_b = sem("lows_b")
        products = sem("products")
        low_ready = sem("low_ready")
        stored = sem("stored")
        dve_order = sem("dve_order")
        par_in, masks_in, x_in, pos_in, wf_in = (sem(n) for n in ("par_in", "masks_in", "x_in", "pos_in", "wf_in"))
        mem_in = [sem(f"mem_in{n}") for n in range(4)]
        out_done = sem("out_done")
        first_in = sem("first_in")
        first_sum = sem("first_sum")
        shifted_by = sem("shifted_by")
        sum_in = sem("sum_in")
        mean_sum = sem("mean_sum")
        moments_in = sem("moments_in")
        squares = sem("squares")
        squared = sem("squared")
        sumsq = sem("sumsq")
        variance, root = sem("variance"), sem("root")
        normed_t = sem("normed_t")
        embedded = sem("embedded")
        embedded_v = sem("embedded_v")
        split_h = sem("split_h")
        split_l = {"g": sem("split_l_g"), "v": sem("split_l_v")}
        angles, tables = sem("angles"), sem("tables")
        silu_done = sem("silu_done")
        hidden_done = sem("hidden_done")
        lat_sq_done, lat_sums, lat_var, lat_root, lat_ready = (
            sem(n) for n in ("lat_sq_done", "lat_sums", "lat_var", "lat_root", "lat_ready"))
        swapped = sem("swapped")
        roped = sem("roped")
        gated = sem("gated")
        pool_ready = sem("pool_ready")
        scores_done = sem("scores_done")
        shifted = sem("shifted")
        negmax = sem("negmax")
        exps = sem("exps")
        sink_exp = sem("sink_exp")
        probs = sem("probs")
        turns = sem("turns")
        turned_s = sem("turned_s")
        mixed = sem("mixed")
        head_out = sem("head_out")
        pair_sq, pair_low, pair_sum, pair_var, pair_ln, pair_exp, pair_done = (
            sem(n) for n in ("pair_sq", "pair_low", "pair_sum", "pair_var", "pair_ln", "pair_exp", "pair_done"))
        wf_split, logits, logit_rows, logit_in, soft_exp, soft_ln, logf, cum_sum, cum_done, decay_sum, decay_done = (
            sem(n) for n in ("wf_split", "logits", "logit_rows", "logit_in", "soft_exp", "soft_ln", "logf", "cum_sum",
                             "cum_done", "decay_sum", "decay_done"))
        mix_final = sem("mix_final")
        mix_h, mix_l = sem("mix_h"), sem("mix_l")

        def p_(name, i=0, n=1):
            o, w = AT[name]
            assert i + n <= w
            return par[:, o + i:o + i + n]

        ident = p_("ident", 0, P)
        ones = p_("ones", 0, P)

        def blocks_of(name):
            return p_(name, 0, TB * S).rearrange("p (b s) -> p b s", b=TB)

        upto, causal, dist = blocks_of("upto"), blocks_of("causal"), blocks_of("dist")

        def walk(eng, slot, between, chain=None):
            for name in ORDER:
                r = REG[name]
                between(name)
                if r.looped:
                    first = r.first
                    for k in range(first):
                        slot(r, k, None)
                    runs = (r.n - first) // 4 - 1
                    with eng.Fori(0, runs) as i:
                        if chain:
                            chain.enter(i, r)
                        for k in range(first, first + 4):
                            slot(r, k, i)
                        if chain:
                            chain.leave(runs, r)
                    for k in range(first + 4 * runs, r.n):
                        slot(r, k, None)
                else:
                    for k in range(r.n):
                        slot(r, k, None)
            between("end")

        def val(base, per, i):
            return base if i is None else i * per + base

        def following(r, k, i):
            if i is not None or k + 1 < r.n:
                return r, k + 1, i
            at_ = ORDER.index(r.name) + 1
            return (REG[ORDER[at_]], 0, None) if at_ < len(ORDER) else None

        def free_after(r, k, i, piece):
            if i is not None:
                return val(r.g0 + (k - 2) * r.groups + piece + 1, 4 * r.groups, i)
            s = r.s0 + k - SPLIT
            return released(s, piece) if s >= 0 else None

        def wait_slot_free(eng, r, k, i, piece):
            v = free_after(r, k, i, piece)
            if v is not None:
                eng.wait_ge(products, v)

        def steps_at(r, k, i):
            return STEPS.get((r.name, k), []) if i is None else []

        def after_steps(name):
            return [x for k in range(AFTER) for x in STEPS.get(("after", k), [])] if name == "mixout" else []

        def norms_before(name):
            return {"mem_k": ["mem"], "in_a0": ["emb"], "in_a1": ["ln0"], "up10": ["ln1"],
                    "nat0": ["mix"], "up20": ["ffn2"]}.get(name, [])

        def wait_split(eng, name, kt):
            who, n = low_count(name, kt)
            eng.wait_ge(split_l[who], n)

        def input_region(ln):
            return REG["out" + ln[2:]] if ln != "emb" else None

        def in_mix(r):
            return mixs if r.name[:3] == "out" or r.name == "mixout" else xs

        def mix_split(name):
            return {"out0": 0, "out1": 1, "mixout": 2}.get(name)

        def tiles_done(r, k, i):
            if r.kind == "tile":
                return [(k, 4, r.g0 + 2 * k + 2, 8)]
            if r.kind == "down":
                return [(k // 2, 2, r.g0 + 2 * k + 2, 8)] if k % 2 else []
            at_ = r.g0 + r.groups * k
            if r.kind == "uq":
                return [(3 * k + m, 0, at_ + 1 + m, 0) for m in range(3)]
            if r.kind in ("uk", "pool"):
                return [(m, 0, at_ + 1 + m, 0) for m in range(r.groups)]
            if r.kind == "uv":
                return [(TB * k + m, 0, at_ + 1 + m, 0) for m in range(TB)]
            return [(TB * (k // 4) + m, 0, at_ + 2, 0) for m in range(TB)] if k % 4 == 3 else []

        def natural_dest(r, tile):
            dest = {"mem_v": memv, "nat0": v_nat, "nat1": v_nat}.get(r.name, v_mla)
            c = tile // TB if r.name != "nat1" else 1
            return dest[:, tile % TB, 512 * c:512 * (c + 1)]

        def tile_dest(r, tile):
            if r.name == "mem_k":
                return memk[:, tile, :]
            if r.name[:4] == "in_a":
                return lat[:, tile, :] if tile < 8 else mix[:, tile - 8, :]
            if r.kind == "uq":
                return q[:, tile, :]
            if r.kind == "uk":
                return kn[:, tile, :]
            if r.name[:4] == "in_b":
                return branch[:, 3, :] if tile % 2 == 0 else mix[:, 8 + tile // 2, :]
            if r.name[:4] == "in_c":
                g, e = tile // 4, tile % 4
                return mix[:, 12 + g, :] if e == 0 else branch[:, e - 1, :]
            assert r.name == "heads"
            return feat[:, tile, :]

        def head_spec(n):
            if n < MLA_ALL:
                h = n % HEADS
                a = slice(ROPE * (h // 4), ROPE * (h // 4) + ROPE)
                qk = [(q[:, h, :], kn[:, h, :]), (q[a, HEADS + h % 4, :], kr[a, 0, :])]
                return "mla", h, qk, [v_mla[:, b, h * P:(h + 1) * P] for b in range(TB)], h
            m = n - MLA_ALL
            if m < SWA0:
                return "mem", m, [(feat[:, m, :], memk[:, m, :])], [
                    memv[:, b, m * P:(m + 1) * P] for b in range(TB)], FOX + SWA + m
            if m < FOX0:
                h = m - SWA0
                kv = h // (SWA // SWA_KV)
                return "swa", h, [(feat[:, MEM + SWA_KV + h, :], feat[:, MEM + kv, :])], [
                    v_nat[:, b, kv * P:(kv + 1) * P] for b in range(TB)], FOX + h
            h = m - FOX0
            k_at = MEM + SWA_KV + SWA + 4 * (h // 2) + h % 2
            return "fox", h, [(feat[:, k_at + 2, :], feat[:, k_at, :])], [
                v_nat[:, b, (SWA_KV + h) * P:(SWA_KV + h + 1) * P] for b in range(TB)], h

        def keys_seen(kind, b):
            return S if kind == "mem" else (b + 1) * P

        def blocks_seen(kind):
            return [(b, c) for b in range(TB) for c in range(TB) if kind == "mem" or c <= b]

        def pair_of(p):
            if p < 2:
                return memk[:, 2 * p:2 * p + 2, :], "mem_k"
            return feat[:, 2 * (p - 2):2 * (p - 2) + 2, :], PAIRS[p - 2]

        def pair_stored(p):
            return REG["mem_k"].t0 + 2 * p + 2 if p < 2 else REG["heads"].t0 + 2 * (p - 2) + 2

        def flat(a):
            return a.rearrange("p b s -> p (b s)")

        def gate_stored(layer, tile):
            if tile < 8:
                return REG[f"in_a{layer}"].t0 + 8 + tile + 1
            if tile < 12:
                return REG[f"in_b{layer}"].t0 + 2 * (tile - 8) + 2
            return REG[f"in_c{layer}"].t0 + 4 * (tile - 12) + 1

        def gates_done(layer, tile):
            return 10 * layer + (tile // 4 + 1 if tile < 8 else tile - 5)

        block = ctx.enter_context(nc.Block())

        @block.sync
        def _(eng):
            cut = AT["upto"][0]
            eng.dma_start(memx[:, 0:4, :], t["mem"][:, 0:4, :]).then_inc(mem_in[0], 16)
            eng.dma_start(par[:, 0:cut], t["par"][:, 0:cut]).then_inc(par_in, 16)
            for n in range(1, 4):
                eng.dma_start(memx[:, 4 * n:4 * n + 4, :], t["mem"][:, 4 * n:4 * n + 4, :]).then_inc(mem_in[n], 16)
            eng.dma_start(pos[:, :], t["positions"]).then_inc(pos_in, 16)

            def slot(r, k, i):
                s = r.s0 + k
                if i is not None or s >= RAW:
                    eng.wait_ge(lows_a, val(s - RAW + 1, 4, i))
                    eng.wait_ge(lows_b, val(s - RAW + 1, 4, i))
                eng.dma_start(raw[:, s % RAW, 0:r.blocks * P],
                              t[r.array][val(r.a0 + k, 4, i), :, :]).then_inc(loaded[s % RAW], 16)
                if r.name[:4] == "in_b" and k == 1:
                    eng.wait_ge(stored, REG[f"uk{r.layer}"].t0)
                    for a in range(0, P, ROPE // 2):
                        b = a ^ (ROPE // 2)
                        eng.dma_start(rope_b[a:a + ROPE // 2, :, :], q[b:b + ROPE // 2, HEADS:, :]).then_inc(swapped, 16)
                if r.name == "mem_k" and k == 1:
                    eng.dma_start(x[:, :, :], t["x"]).then_inc(x_in, 16)
                if r.name == "mem_k" and k == 3:
                    eng.dma_start(par[:, cut:NPAR], t["par"][:, cut:NPAR]).then_inc(masks_in, 16)
                    eng.dma_start(wf[:, :], t["wf"]).then_inc(wf_in, 16)

            def between(name):
                if name == "end":
                    cuts = (0, 8, 12, 14, 15, KT)
                    for lo, hi in zip(cuts, cuts[1:]):
                        eng.wait_ge(stored, REGIONS[-1].t0 + hi)
                        eng.dma_start(t["out"][:, lo:hi, :], x[:, lo:hi, :]).then_inc(out_done, 16)
                    eng.wait_ge(out_done, 16 * (len(cuts) - 1))

            walk(eng, slot, between)

        @block.tensor
        def _(eng):
            def product(bank_, hi, lo, moving, start, stop):
                eng.matmul(bank_[:, :], hi, moving, start=start, stop=False)
                return eng.matmul(bank_[:, S:2 * S], lo, moving[:, 0:S], start=False, stop=stop)

            def product_natural(bank_, still, hi, lo, b, start, stop):
                xh, xl = still[:, b * P:(b + 1) * P], still[:, S + b * P:S + (b + 1) * P]
                eng.matmul(bank_[:, :], xh, hi, start=start, stop=False)
                eng.matmul(bank_[:, :], xl, hi, start=False, stop=False)
                return eng.matmul(bank_[:, :], xh, lo, start=False, stop=stop)

            def sum_over_features(out, tiles):
                for n, a in enumerate(tiles):
                    last = eng.matmul(out, ones, a, start=(n == 0), stop=(n == len(tiles) - 1))
                return last

            def slot(r, k, i):
                steps = steps_at(r, k, i)
                halfway = [x for x in steps if r.kind in ("tile", "natural") and (
                    x[0] in ("scores", "forget_turn") or x[0] == "decay" and x[1] % 2)]
                for step in steps:
                    if step not in halfway:
                        do(*step)
                s = r.s0 + k
                pos_ = s % SPLIT

                def piece_ready(piece):
                    eng.wait_ge((lows_a, lows_b)[piece], val(s + 1, 4, i))

                def bank_free(tile, per):
                    if r.t0 + tile >= 2:
                        eng.wait_ge(stored, val(r.t0 + tile - 1, per, i))
                    return acc[(r.t0 + tile) % 2]

                def hl(b):
                    b += (8 - r.pieces[0]) * (b >= r.pieces[0])
                    return high[:, pos_, b * P:(b + 1) * P], low[:, pos_, b * P:(b + 1) * P]

                if r.name in TOGETHER and k == 1:
                    return
                if r.name in TOGETHER and k == 0:
                    banks = bank_free(0, 4), bank_free(1, 4)
                    for b in range(KT):
                        at_ = slice(b * P, (b + 1) * P)
                        wait_split(eng, norms_before(r.name)[0], b)
                        if b % 8 == 0:
                            eng.wait_ge((lows_a, lows_b)[b // 8], s + 2)
                        for n in range(2):
                            last = product(banks[n], high[:, (s + n) % SPLIT, at_], low[:, (s + n) % SPLIT, at_],
                                           xs[:, b, :], b == 0, b == KT - 1)
                            if n:
                                if b == KT - 1:
                                    last.then_inc(products, 2)
                            elif b % 8 == 7:
                                last.then_inc(products, 1)
                elif r.kind == "tile":
                    a = bank_free(k, 4)
                    for b in range(KT):
                        if b == 8:
                            for step in halfway:
                                do(*step)
                        if b % 8 == 0:
                            piece_ready(b // 8)
                        if k == 0 and mix_split(r.name) is not None and b % 4 == 0:
                            n = mix_split(r.name)
                            eng.wait_ge(mix_l, 4 * n + MIX_ORDER[n].index(b // 4) + 1)
                        if k == 0 and norms_before(r.name):
                            wait_split(eng, norms_before(r.name)[0], b)
                        last = product(a, *hl(b), in_mix(r)[:, b, :], b == 0, b == KT - 1)
                        if b % 8 == 7:
                            last.then_inc(products, 1)
                elif r.kind == "down":
                    half = k % 2
                    eng.wait_ge(hidden_done, r.hidden0 + HALF * (half + 1))
                    a = bank_free(k // 2, 2) if not half else acc[(r.t0 + k // 2) % 2]
                    for b in range(HALF):
                        if b in (0, r.pieces[0]):
                            piece_ready(int(b > 0))
                        last = product(a, *hl(b), hidden[:, HALF * half + b, :], half == 0 and b == 0,
                                       half == 1 and b == HALF - 1)
                        if b in (r.pieces[0] - 1, HALF - 1):
                            last.then_inc(products, 1)
                elif r.kind in ("uq", "uk"):
                    eng.wait_ge(lat_ready, r.layer + 1)
                    per, src = (KQ, 0) if r.kind == "uq" else (KKV, KQ)
                    for m in range(r.groups):
                        a = bank_free(k * r.groups + m, 0)
                        for b in range(per):
                            if m * per + b in (0, r.pieces[0]):
                                piece_ready(int(m * per + b > 0))
                            last = product(a, *hl(m * per + b), lats[:, src + b, :], b == 0, b == per - 1)
                        last.then_inc(products, 1)
                elif r.kind == "pool":
                    piece_ready(0)
                    piece_ready(1)
                    for g in range(GROUPS):
                        a = bank_free(g, 0)
                        eng.wait_ge(pool_ready, GROUPS * r.layer + g + 1)
                        product(a, *hl(g), pooled[:, g, :], True, True).then_inc(products, 1)
                elif r.kind == "uv":
                    piece_ready(0)
                    piece_ready(1)
                    for b in range(TB):
                        a = bank_free(TB * k + b, 0)
                        for c in range(KKV):
                            w = slice(c * 8 * P, c * 8 * P + 512)
                            last = product_natural(a, lats[:, KQ + c, :], high[:, pos_, w], low[:, pos_, w], b,
                                                   c == 0, c == KKV - 1)
                        last.then_inc(products, 1)
                else:
                    for piece in range(2):
                        for step in halfway if piece else []:
                            do(*step)
                        piece_ready(piece)
                        for b in range(TB):
                            tile = TB * (k // 4) + b
                            a = bank_free(tile, 0) if k % 4 == 0 and piece == 0 else acc[(r.t0 + tile) % 2]
                            for c in range(2 * piece, 2 * piece + 2):
                                w = slice(c * 512, (c + 1) * 512)
                                kt = 4 * (k % 4) + c
                                if k < 4 and b == 0 and norms_before(r.name):
                                    wait_split(eng, norms_before(r.name)[0], kt)
                                last = product_natural(a, xs[:, kt, :], high[:, pos_, w], low[:, pos_, w], b,
                                                       kt == 0, kt == KT - 1)
                        last.then_inc(products, 1)

            def do(kind, *a):
                if kind == "shift":
                    n = LAYER_NORMS.index(a[0])
                    eng.wait_ge(first_in, n + 1)
                    eng.matmul(sums[:, 0:S], ones, moment[:, 0:S], start=True, stop=True).then_inc(first_sum, 1)
                elif kind == "factor_sum":
                    total_squares(a[0])
                elif kind == "lat_scale":
                    eng.wait_ge(lat_sq_done, a[0] + 1)
                    sum_over_features(sums[:, 0:S], [lat_sq[:, n, :] for n in range(KQ)])
                    sum_over_features(sums[:, S:2 * S], [lat_sq[:, n, :] for n in range(KQ, KQ + KKV)])\
                        .then_inc(lat_sums, 1)
                elif kind == "headnorm":
                    p = a[0]
                    eng.wait_ge(pair_low, p + 1)
                    if p:
                        eng.wait_ge(pair_var, p)
                    if p == 2:
                        eng.wait_ge(decay_done, FOX)
                    eng.matmul(sums[:, :], ones_r[:, :], square_h[:, :], start=True, stop=False)
                    eng.matmul(sums[:, :], ones_r[:, :], square_l[:, :], start=False, stop=True).then_inc(pair_sum, 1)
                elif kind == "forget":
                    for kt in (KT - 2, KT - 1):
                        wait_split(eng, "mix", kt)
                    eng.wait_ge(wf_split, 1)
                    eng.wait_ge(masks_in, 16)
                    for kt in range(KT):
                        eng.matmul(sums[0:FOX, :], wfh[:, kt, :], xs[:, kt, :], start=(kt == 0), stop=False)
                        last = eng.matmul(sums[0:FOX, S:2 * S], wfl[:, kt, :], xs[:, kt, 0:S], start=False,
                                          stop=(kt == KT - 1))
                    last.then_inc(logits, 1)
                elif kind == "forget_turn":
                    eng.wait_ge(logit_rows, 1)
                    for b in range(TB):
                        last = eng.transpose(sums[:, 8 * b:8 * b + FOX], up[0:FOX, b * P:(b + 1) * P], ident[0:FOX, 0:FOX])
                    last.then_inc(logits, 1)
                elif kind == "decay":
                    h = a[0]
                    eng.wait_ge(logf, 1)
                    if h == 0:
                        for b in range(TB):
                            for c in range(TB):
                                last = eng.matmul(sums[:, 8 * b:8 * b + FOX], upto[:, c, b * P:(b + 1) * P],
                                                  fz[:, 0, c, :], start=(c == 0), stop=(c == TB - 1))
                        last.then_inc(cum_sum, 1)
                        eng.wait_ge(cum_done, 1)
                    else:
                        eng.wait_ge(decay_done, h)
                    for c in range(TB):
                        last = eng.matmul(sums[:, 0:S], lf_rows[:, h, c, :], upto[:, c, :],
                                          start=(c == 0), stop=(c == TB - 1))
                    last.then_inc(decay_sum, 1)
                elif kind == "scores":
                    n = a[0]
                    what, h, qk, _, _ = head_spec(n)
                    if n >= 2:
                        eng.wait_ge(shifted, TB * (n - 1))
                    if what == "mla":
                        layer = n // HEADS
                        eng.wait_ge(stored, REG[f"in_b{layer}"].t0)
                        eng.wait_ge(roped, 2 * layer + 2)
                    else:
                        eng.wait_ge(stored, REG["heads"].t0)
                        p = {"mem": h // 2, "swa": 3 + h // 2, "fox": 7 + 2 * (h // 2)}[what]
                        eng.wait_ge(pair_done, 2 + p + 1)
                    for b in range(TB):
                        for m, (qc, kc) in enumerate(qk):
                            w = keys_seen(what, b)
                            last = eng.matmul(score[n % 2][:, b, 0:w], qc[:, b * P:(b + 1) * P], kc[:, 0:w],
                                              start=(m == 0), stop=(m == len(qk) - 1))
                    last.then_inc(scores_done, 1)
                elif kind == "turn":
                    n = a[0]
                    eng.wait_ge(probs, 2 * n + 2)
                    if n:
                        eng.wait_ge(turned_s, n)
                    for b, c in blocks_seen(head_spec(n)[0]):
                        last = eng.transpose(turn_ps[:, c, b * P:(b + 1) * P], prob[:, n % 2, b, c * P:(c + 1) * P], ident)
                    last.then_inc(turns, 1)
                elif kind == "mixv":
                    n = a[0]
                    what, h, _, v, _ = head_spec(n)
                    eng.wait_ge(turned_s, n + 1)
                    if n >= 2:
                        eng.wait_ge(head_out, n - 1)
                    if what == "fox" and h >= 2:
                        eng.wait_ge(stored, REG["mixout"].t0)
                    o_ = 0 if what == "mem" else P
                    out_, pr = head_ps[n % 2], turned[:, n % TURNED, :, :]
                    eng.matmul(out_[:, 0:S], v[0], pr[:, 0, :], start=True, stop=False)
                    eng.matmul(out_[:, o_:S], v[1], pr[:, 1, o_:S], start=False, stop=True).then_inc(mixed, 1)

            def total_squares(name):
                eng.wait_ge(moments_in, N_OF[name])
                run = late_moment if name == "mix" else moment
                eng.matmul(sums[:, S:2 * S], ones, run[:, S:2 * S], start=True, stop=True).then_inc(sumsq, 1)

            def norm(name):
                if name == "mem":
                    for kt in range(KT):
                        if kt % 4 == 0:
                            eng.wait_ge(squares, kt // 4 + 1)
                        last = eng.matmul(sums[:, S:2 * S], ones, square[:, kt, :], start=(kt == 0), stop=(kt == KT - 1))
                    last.then_inc(sumsq, 1)
                elif name != "ffn2":
                    if name in LAYER_NORMS:
                        eng.wait_ge(sum_in, LAYER_NORMS.index(name) + 1)
                        eng.matmul(turn_ps[:, 0, :], ones, moment[:, 0:S], start=True, stop=True).then_inc(mean_sum, 1)
                    total_squares(name)

            def between(name):
                if name == "mem_k":
                    eng.wait_ge(par_in, 16)
                for step in after_steps(name):
                    do(*step)
                for n in norms_before(name):
                    norm(n)

            walk(eng, slot, between)

        @block.scalar
        def _(eng):
            def split_high(piece, r, k, i):
                s = r.s0 + k
                n, at_ = r.pieces[piece], piece * r.pieces[0] * P
                eng.wait_ge(loaded[s % RAW], val(16 * (s // RAW + 1), 16, i))
                wait_slot_free(eng, r, k, i, piece)
                eng.activation(high[:, s % SPLIT, piece * 8 * P:(8 * piece + n) * P],
                               raw[:, s % RAW, at_:at_ + n * P], ACT.Copy).then_inc(highs, 1)

            def slot(r, k, i):
                nxt = following(r, k, i)
                if nxt and not (k == 0 and norms_before(r.name) and r.name != "up20"):
                    split_high(1, *nxt)
                for step in steps_at(r, k, i):
                    do(*step)
                nxt = nxt and following(*nxt)
                early = {"tile": 0, "down": 0, "natural": 0, "uq": 1, "uk": 4, "pool": 2}.get(r.kind, -1)
                for nth, (tile, per, prod_, pper) in enumerate(tiles_done(r, k, i) + [(None,) * 4]):
                    if nxt and nth == early:
                        split_high(0, *nxt)
                    if tile is None:
                        break
                    T = r.t0 + tile
                    eng.wait_ge(products, val(prod_, pper, i))
                    if r.kind in ("natural", "uv"):
                        eng.activation(natural_dest(r, tile)[:, 0:S], acc[T % 2][:, 0:S], ACT.Copy)\
                            .then_inc(low_ready, 1)
                        continue
                    if T >= 2:
                        eng.wait_ge(stored, val(T - 1, per, i))
                    eng.activation(lowsum[:, T % 2, :], acc[T % 2][:, S:2 * S], ACT.Copy,
                                   scale=0.5 if r.kind == "down" else 1.0).then_inc(low_ready, 1)
                    if r.name[:2] == "up" and k % 2 == 0:
                        pair = r.pair0 + k // 2
                        eng.wait_ge(stored, val(T + 1, per, i))
                        if i is not None or pair:
                            eng.wait_ge(hidden_done, val(pair, 2, i))
                        eng.activation(silu_g[:, :], gate[:, :], ACT.Silu).then_inc(silu_done, 1)
                if nxt and early < 0:
                    split_high(0, *nxt)

            def take_root(name, r=None):
                eng.activation(dummy[:, :], ones[:, 0:1], ACT.Sqrt)
                if r and r.name in TOGETHER:
                    split_high(1, r, 1, None)
                eng.wait_ge(variance, N_OF[name] + 1)
                eng.activation(scale_b[:, 0:S], scale_a[:, 0:S], ACT.Sqrt).then_inc(root, 1)

            def do(kind, *a):
                if kind == "factor":
                    take_root(a[0])
                elif kind == "tables":
                    eng.wait_ge(angles, 1)
                    eng.activation(sin[:, :], ang[:, 0, :], ACT.Sin)
                    eng.activation(cos[:, :], ang[:, 1, :], ACT.Sin).then_inc(tables, 1)
                elif kind == "gain":
                    name, kt = a
                    eng.wait_ge(stored, REG["mixout"].t0 + kt + 1)
                    if kt == 0:
                        eng.wait_ge(products, REG["mixout"].g0)
                    eng.activation(xs[:, kt, 0:S], x[:, kt, :], ACT.Copy, scale=p_("ffn2_g", kt)).then_inc(split_h, 1)
                elif kind == "lat_square":
                    eng.wait_ge(stored, REG[f"in_a{a[0]}"].t0 + KQ + KKV)
                    eng.activation(lat_sq[:, :, :], lat[:, 0:KQ + KKV, :], ACT.Square).then_inc(lat_sq_done, 1)
                elif kind == "lat_scale":
                    eng.wait_ge(lat_var, a[0] + 1)
                    eng.activation(scale_b[:, :], scale_a[:, :], ACT.Sqrt).then_inc(lat_root, 1)
                elif kind == "silu":
                    layer, lo, hi = a
                    eng.wait_ge(stored, gate_stored(layer, hi - 1))
                    eng.activation(mix[:, lo:hi, :], mix[:, lo:hi, :], ACT.Silu).then_inc(gated, 1)
                elif kind == "square":
                    p = a[0]
                    eng.wait_ge(stored, pair_stored(p))
                    if p:
                        eng.wait_ge(pair_done, p)
                    eng.activation(square_h[:, :], flat(pair_of(p)[0]), ACT.Square).then_inc(pair_sq, 1)
                elif kind == "headnorm":
                    p = a[0]
                    eng.wait_ge(pair_var, p + 1)
                    eng.activation(scale_a[:, :], scale_b[:, :], ACT.Ln).then_inc(pair_ln, 1)
                    eng.wait_ge(pair_ln, p + 1)
                    eng.activation(scale_a[:, :], scale_a[:, :], ACT.Exp, scale=-0.5).then_inc(pair_exp, 1)
                elif kind == "forget_turn":
                    eng.wait_ge(logit_in, 1)
                    eng.activation(fz[:, 2, :, :], fz[:, 1, :, :], ACT.Exp).then_inc(soft_exp, 1)
                    eng.wait_ge(soft_exp, 1)
                    eng.activation(fz[:, 3, :, :], fz[:, 2, :, :], ACT.Ln, bias=1.0).then_inc(soft_ln, 1)
                elif kind == "exps":
                    n = a[0]
                    what, h, _, _, _ = head_spec(n)
                    eng.wait_ge(negmax, TB * (n + 1))
                    for b in range(TB):
                        pr = prob[:, n % 2, b, 0:keys_seen(what, b)]
                        eng.activation(pr, pr, ACT.Exp,
                                       bias=stat[:, n % 2, b:b + 1], accum_out=stat[:, n % 2, 2 + b:3 + b])\
                            .then_inc(exps, 1)
                    if what == "swa":
                        eng.activation(stat[:, n % 2, 4:6], stat[:, n % 2, 0:2], ACT.Exp, bias=p_("sinks", h))\
                            .then_inc(sink_exp, 1)
                elif kind == "turn":
                    n = a[0]
                    eng.wait_ge(turns, n + 1)
                    if n >= TURNED:
                        eng.wait_ge(mixed, n - TURNED + 1)
                    out_ = turned[:, n % TURNED, :, :]
                    if head_spec(n)[0] == "mem":
                        eng.activation(flat(out_), flat(turn_ps[:, :, :]), ACT.Copy).then_inc(turned_s, 1)
                    else:
                        eng.activation(out_[:, 0, :], turn_ps[:, 0, :], ACT.Copy)
                        eng.activation(out_[:, 1, P:S], turn_ps[:, 1, P:S], ACT.Copy).then_inc(turned_s, 1)
                elif kind == "mix_split":
                    layer, c = a
                    at_ = MIX_ORDER[layer].index(c)
                    if layer == DEPTH:
                        eng.wait_ge(head_out, MLA_ALL + FOX + SWA + MEM)
                    elif c == 2:
                        eng.wait_ge(mix_final, 2 * layer + 1)
                        eng.wait_ge(scores_done, HEADS * (layer + 1))
                        eng.wait_ge(products, REG[f"in_c{layer}"].g0)
                    elif c == 3:
                        eng.wait_ge(mix_final, 2 * layer + 2)
                    else:
                        eng.wait_ge(head_out, HEADS * (layer + 1))
                    eng.activation(mixs[:, 4 * c:4 * c + 4, 0:S], mix[:, 4 * c:4 * c + 4, :], ACT.Copy).then_inc(mix_h, 1)

            def norm(name):
                if name == "ffn2":
                    do("gain", name, KT - 1)
                    return
                r = REG[next(n for n in ORDER if norms_before(n) == [name])]
                if name == "mem":
                    for n in range(4):
                        eng.wait_ge(mem_in[n], 16)
                        eng.activation(square[:, 4 * n:4 * n + 4, :], memx[:, 4 * n:4 * n + 4, :], ACT.Square)\
                            .then_inc(squares, 1)
                    eng.wait_ge(par_in, 16)
                    split_high(0, REG["mem_k"], 0, None)
                    split_high(1, REG["mem_k"], 0, None)
                take_root(name, r)
                if name == "mem":
                    split_high(0, r, 1, None)
                if r.name not in TOGETHER:
                    split_high(1, r, 1, None)
                if name in LAYER_NORMS:
                    o_ = KT if name == "ln1" else 0
                    g, b = ("emb_g", "emb_b") if name == "emb" else ("ln_g", "ln_b")
                    for n, (lo, hi) in enumerate(CUTS):
                        eng.wait_ge(normed_t, NORMED_T[name] + n + 1)
                        for kt in range(lo, hi):
                            gain, bias = p_(g, o_ + kt), p_(b, o_ + kt)
                            if name == "ln1" or kt % 2 == 0:
                                ins = eng.activation(x[:, kt, :], normed[:, kt, :], ACT.Identity, bias=bias, scale=gain)
                            if name != "ln1":
                                eng.activation(xs[:, kt, 0:S], normed[:, kt, :], ACT.Identity, bias=bias, scale=gain)\
                                    .then_inc(split_h, 1)
                                continue
                            ins.then_inc(embedded, 1)
                            eng.wait_ge(embedded, kt + 1)
                            eng.activation(xs[:, kt, 0:S], x[:, kt, :], ACT.Copy, scale=p_("ffn1_g", kt))\
                                .then_inc(split_h, 1)
                else:
                    for kt in range(KT):
                        eng.wait_ge(normed_t, NORMED_T[name] + kt + 1)
                        eng.activation(xs[:, kt, 0:S], normed[:, kt, :], ACT.Copy).then_inc(split_h, 1)
            def between(name):
                for step in after_steps(name):
                    do(*step)
                if mix_split(name) is not None:
                    n = mix_split(name)
                    for c in MIX_ORDER[n] if n == DEPTH else MIX_ORDER[n][3:]:
                        do("mix_split", n, c)
                for n in norms_before(name):
                    norm(n)

            walk(eng, slot, between)

        @block.vector
        def _(eng):
            chain = Chain(eng, dve_order)
            step_ = chain.step

            def split_low(r, k, i):
                s = r.s0 + k
                w = slice(8 * P, (8 + r.pieces[1]) * P)
                eng.wait_ge(highs, val(2 * s + 2, 8, i))
                eng.tensor_tensor(low[:, s % SPLIT, w], raw[:, s % RAW, r.pieces[0] * P:r.blocks * P],
                                  high[:, s % SPLIT, w].bitcast(F32), ALU.subtract).then_inc(lows_b, 1)

            def slot(r, k, i):
                nxt = following(r, k, i)
                if nxt and not (k == 0 and r.name in TOGETHER):
                    split_low(*nxt)
                for step in steps_at(r, k, i):
                    do(*step)
                for tile, per, prod_, pper in tiles_done(r, k, i):
                    store(r, k, i, tile, per)

            def store(r, k, i, tile, per):
                T = r.t0 + tile
                first, second = acc[T % 2][:, 0:S], lowsum[:, T % 2, :]
                eng.wait_ge(low_ready, val(T + 1, per, i))

                def done(ins, and_wait=False):
                    ins.then_inc(stored, 1)
                    if and_wait:
                        eng.wait_ge(stored, val(T + 1, per, i))

                if r.kind in ("natural", "uv"):
                    done(eng.tensor_copy(natural_dest(r, tile)[:, S:2 * S], acc[T % 2][:, S:2 * S]))
                elif r.name[:2] == "up":
                    out_ = gate if k % 2 == 0 else up
                    step_(eng.tensor_tensor(out_[:, :], first, second, ALU.add))
                    done(eng.tensor_tensor(out_[:, :], out_[:, :], factor[:, :], ALU.mult), True)
                    if k % 2 == 0:
                        return
                    hid = val(k // 2, 2, i)
                    eng.wait_ge(silu_done, val(r.pair0 + k // 2 + 1, 2, i))
                    step_(eng.tensor_tensor(hidden[:, hid, 0:S], silu_g[:, :], up[:, :], ALU.mult))
                    step_(eng.tensor_tensor(prod[:, :], silu_g[:, :], up[:, :], ALU.mult))
                    eng.tensor_tensor(hidden[:, hid, S:2 * S], prod[:, :], hidden[:, hid, 0:S].bitcast(F32),
                                      ALU.subtract).then_inc(hidden_done, 1)
                    eng.wait_ge(hidden_done, val(r.pair0 + k // 2 + 1, 2, i))
                elif r.kind == "down":
                    xt = x[:, val(tile, per, i), :]
                    step_(eng.scalar_tensor_tensor(out=xt, in0=first, scalar=0.5, in1=xt, op0=ALU.mult, op1=ALU.add))
                    done(eng.tensor_tensor(xt, xt, second, ALU.add), r.name == "down11")
                    if r.name == "down11":
                        add_squares("mix", late_moment, late_moment[:, 0:S], xt, i is None and tile == KT - 1)
                elif r.name[:3] == "out":
                    xt = x[:, tile, :]
                    step_(eng.scalar_tensor_tensor(out=xt, in0=xt, scalar=ALPHA, in1=first, op0=ALU.mult, op1=ALU.add))
                    done(eng.scalar_tensor_tensor(out=xt, in0=second, scalar=p_("b_out", KT * r.layer + tile), in1=xt,
                                                  op0=ALU.add, op1=ALU.add))
                elif r.name == "mixout":
                    xt = x[:, tile, :]
                    step_(eng.tensor_tensor(xt, first, xt, ALU.add))
                    done(eng.tensor_tensor(xt, xt, second, ALU.add), True)
                    add_squares("ffn2", moment, moment_sq[:, 0, :], xt, tile == KT - 1)
                elif r.kind == "pool":
                    done(eng.tensor_tensor(gate[:, :], first, second, ALU.add), True)
                    eng.wait_ge(gated, gates_done(r.layer, 8 + tile))
                    ins = eng.scalar_tensor_tensor(out=mix[:, 8 + tile, :], in0=gate[:, :],
                                                   scalar=p_("pool_s", GROUPS * r.layer + tile),
                                                   in1=mix[:, 8 + tile, :], op0=ALU.mult, op1=ALU.mult)
                    final(ins, 2 * r.layer + 1 if tile == GROUPS - 1 else None)
                elif r.name[:4] == "in_c" and tile % 4 == 3:
                    done(eng.tensor_tensor(branch[:, 2, :], first, second, ALU.add), True)
                    g = tile // 4
                    ins = eng.tensor_tensor(mix[:, 12 + g, :], mix[:, 12 + g, :], branch[:, 2, :], ALU.mult)
                    final(ins, 2 * r.layer + 2 if g == GROUPS - 1 else None)
                else:
                    done(eng.tensor_tensor(tile_dest(r, tile), first, second, ALU.add))

            def final(ins, count):
                if count:
                    ins.then_inc(mix_final, 1)
                    eng.wait_ge(mix_final, count)
                else:
                    step_(ins)

            def added(name, ins, last):
                if last:
                    ins.then_inc(moments_in, 1)
                    eng.wait_ge(moments_in, N_OF[name])
                else:
                    step_(ins)

            def add_squares(name, run, tmp, xt, last):
                step_(eng.tensor_tensor(tmp, xt, xt, ALU.mult))
                added(name, eng.tensor_tensor(run[:, S:2 * S], run[:, S:2 * S], tmp, ALU.add), last)

            def tile_there(name, kt):
                if name == "emb":
                    eng.wait_ge(x_in, 16)
                else:
                    eng.wait_ge(stored, input_region(name).t0 + kt + 1)

            def moments(name, lo, hi):
                tile_there(name, hi - 1)
                e = normed[:, lo:hi, :]
                wide = shift[:, :].unsqueeze(1).to_broadcast([P, hi - lo, S])
                step_(eng.tensor_tensor(e, x[:, lo:hi, :], wide, ALU.add))
                for kt in range(lo, hi):
                    ins = eng.tensor_tensor(moment[:, 0:S], moment[:, 0:S], normed[:, kt, :], ALU.add)
                    if kt == KT - 1:
                        ins.then_inc(sum_in, 1)
                        eng.wait_ge(sum_in, LAYER_NORMS.index(name) + 1)
                    else:
                        step_(ins)
                step_(eng.tensor_tensor(moment_sq[:, 0:hi - lo, :], e, e, ALU.mult))
                for kt in range(lo, hi):
                    run = moment[:, S:2 * S]
                    added(name, eng.tensor_tensor(run, run, moment_sq[:, kt - lo, :], ALU.add), kt == KT - 1)

            def variance_of(name):
                c = N_OF[name]
                if name in ("emb", "ln0"):
                    split_low(REG[TOGETHER[LAYER_NORMS.index(name)]], 1, None)
                if name in LAYER_NORMS:
                    eng.wait_ge(mean_sum, LAYER_NORMS.index(name) + 1)
                    rest = scale_c[:, 0:S]
                    step_(eng.tensor_scalar(mean[:, :], turn_ps[:, 0, :], 1.0 / D, None, ALU.mult))
                    step_(eng.scalar_tensor_tensor(out=rest, in0=mean[:, :], scalar=-1.0, in1=mean[:, :], op0=ALU.mult,
                                                   op1=ALU.mult))
                    step_(eng.tensor_scalar(rest, rest, LN_EPS, None, ALU.add))
                eng.wait_ge(sumsq, c + 1)
                if name in LAYER_NORMS:
                    ins = eng.scalar_tensor_tensor(out=scale_a[:, 0:S], in0=sums[:, S:2 * S], scalar=1.0 / D, in1=rest,
                                                   op0=ALU.mult, op1=ALU.add)
                else:
                    ins = eng.tensor_scalar(scale_a[:, 0:S], sums[:, S:2 * S], 1.0 / D, RMS_EPS, ALU.mult, ALU.add)
                ins.then_inc(variance, 1)
                eng.wait_ge(root, c + 1)

            def split_low_of(name, kt, gain=None):
                if low_count(name, kt)[0] != "v":
                    return
                eng.wait_ge(split_h, high_count(name, kt))
                hi = xs[:, kt, 0:S].bitcast(F32)
                if gain:
                    ins = eng.scalar_tensor_tensor(out=xs[:, kt, S:2 * S], in0=x[:, kt, :], scalar=p_(gain, kt), in1=hi,
                                                   op0=ALU.mult, op1=ALU.subtract)
                else:
                    ins = eng.tensor_tensor(xs[:, kt, S:2 * S], normed[:, kt, :], hi, ALU.subtract)
                ins.then_inc(split_l["v"], 1)

            def rotate(a, b, c, s_, out, out_b, count):
                step_(eng.tensor_tensor(out, a, c, ALU.mult))
                step_(eng.tensor_tensor(out_b, b, s_, ALU.mult))
                eng.tensor_tensor(out, out, out_b, ALU.add).then_inc(roped, 1)
                eng.wait_ge(roped, count)

            def do(kind, *a):
                if kind == "first_sum":
                    name, n = a[0], LAYER_NORMS.index(a[0])
                    tile_there(name, SHIFT_TILES - 1)
                    if name == "emb":
                        eng.wait_ge(split_l["g"], low_count("mem", KT - 2)[1])
                    for kt in range(1, SHIFT_TILES):
                        before = x[:, 0, :] if kt == 1 else moment[:, 0:S]
                        ins = eng.tensor_tensor(moment[:, 0:S], x[:, kt, :], before, ALU.add)
                        if kt < SHIFT_TILES - 1:
                            step_(ins)
                    ins.then_inc(first_in, 1)
                elif kind == "shift":
                    n = LAYER_NORMS.index(a[0])
                    eng.wait_ge(first_sum, n + 1)
                    eng.tensor_scalar(shift[:, :], sums[:, 0:S], -1.0 / (SHIFT_TILES * P), None, ALU.mult)\
                        .then_inc(shifted_by, 1)
                    eng.wait_ge(shifted_by, n + 1)
                    step_(eng.memset(moment[:, :], 0.0))
                elif kind == "moments":
                    moments(*a)
                elif kind == "tables":
                    rope_angles()
                elif kind == "gain":
                    split_low_of(a[0], a[1], "ffn2_g")
                elif kind == "factor":
                    variance_of(a[0])
                    step_(eng.reciprocal(factor[:, :], scale_b[:, 0:S]))
                elif kind == "lat_scale":
                    layer = a[0]
                    eng.wait_ge(lat_sums, layer + 1)
                    step_(eng.tensor_scalar(scale_a[:, 0:S], sums[:, 0:S], 1.0 / QLAT, RMS_EPS, ALU.mult, ALU.add))
                    eng.tensor_scalar(scale_a[:, S:2 * S], sums[:, S:2 * S], 1.0 / KVLAT, RMS_EPS, ALU.mult, ALU.add)\
                        .then_inc(lat_var, 1)
                    eng.wait_ge(lat_root, layer + 1)
                    step_(eng.reciprocal(scale_a[:, :], scale_b[:, :]))
                    for n in range(KQ + KKV):
                        g, o_ = (p_("q_g", KQ * layer + n), 0) if n < KQ else (p_("kv_g", KKV * layer + n - KQ), S)
                        step_(eng.scalar_tensor_tensor(out=lat[:, n, :], in0=lat[:, n, :], scalar=g,
                                                       in1=scale_a[:, o_:o_ + S], op0=ALU.mult, op1=ALU.mult))
                elif kind == "lat_split":
                    n = KQ + KKV
                    step_(eng.tensor_copy(lats[:, :, 0:S], lat[:, 0:n, :]))
                    eng.tensor_tensor(lats[:, :, S:2 * S], lat[:, 0:n, :], lats[:, :, 0:S].bitcast(F32), ALU.subtract)\
                        .then_inc(lat_ready, 1)
                elif kind == "rope_k":
                    layer = a[0]
                    eng.wait_ge(tables, 1)
                    eng.wait_ge(stored, REG[f"in_a{layer}"].t0 + 8)
                    rotate(lat[:, 6, :], lat[:, 7, :], cos[:, :], sin[:, :], kr[:, 0, :], kr[:, 1, :], 2 * layer + 1)
                elif kind == "rope_q":
                    layer = a[0]
                    wide = [v[:, :].unsqueeze(1).to_broadcast([P, HEADS // 2, S]) for v in (cos, sin)]
                    eng.wait_ge(swapped, 64 * (layer + 1))
                    rotate(q[:, HEADS:, :], rope_b[:, :, :], *wide, q[:, HEADS:, :], rope_b[:, :, :], 2 * layer + 2)
                elif kind == "conv":
                    layer, g = a

                    def tap(w):
                        return p_("conv", (3 * layer + w) * GROUPS + g)

                    eng.wait_ge(stored, REG[f"in_c{layer}"].t0 + 4 * g + 3)
                    u, y = silu_g[:, :], scale_c[:, 0:S]
                    step_(eng.tensor_tensor(u, branch[:, 0, :], branch[:, 1, :], ALU.mult))
                    step_(eng.tensor_scalar(y, u, tap(2), None, ALU.mult))
                    for back in (1, 2):
                        step_(eng.scalar_tensor_tensor(out=y[:, back:S], in0=u[:, 0:S - back], scalar=tap(2 - back),
                                                       in1=y[:, back:S], op0=ALU.mult, op1=ALU.add))
                    eng.wait_ge(gated, gates_done(layer, 12 + g))
                    step_(eng.tensor_tensor(mix[:, 12 + g, :], mix[:, 12 + g, :], y, ALU.mult))
                elif kind == "pool":
                    layer, g = a
                    w = WINDOWS[g]
                    src = branch[:, 3, :]
                    eng.wait_ge(stored, REG[f"in_b{layer}"].t0 + 2 * g + 1)
                    halves = [scale_b[:, 0:S], scale_b[:, S:2 * S]]
                    cur, back, n = src, 1, 0
                    while back < w:
                        nxt = halves[n % 2]
                        step_(eng.tensor_tensor(nxt[:, back:S], cur[:, back:S], cur[:, 0:S - back], ALU.add))
                        step_(eng.tensor_copy(nxt[:, 0:back], cur[:, 0:back]))
                        cur, back, n = nxt, back * 2, n + 1
                    y = halves[n % 2]
                    step_(eng.scalar_tensor_tensor(out=y[:, w:S], in0=cur[:, w:S], scalar=1.0 / w, in1=src[:, w:S],
                                                   op0=ALU.mult, op1=ALU.subtract))
                    step_(eng.tensor_tensor(y[:, 0:w], cur[:, 0:w], p_("count", 0, w), ALU.mult))
                    step_(eng.tensor_tensor(y[:, 0:w], y[:, 0:w], src[:, 0:w], ALU.subtract))
                    step_(eng.tensor_copy(pooled[:, g, 0:S], y))
                    eng.tensor_tensor(pooled[:, g, S:2 * S], y, pooled[:, g, 0:S].bitcast(F32), ALU.subtract)\
                        .then_inc(pool_ready, 1)
                    eng.wait_ge(pool_ready, GROUPS * layer + g + 1)
                elif kind == "square":
                    p = a[0]
                    pair = flat(pair_of(p)[0])
                    eng.wait_ge(stored, pair_stored(p))
                    step_(eng.tensor_tensor(scale_b[:, :], pair, pair, ALU.mult))
                    eng.wait_ge(pair_sq, p + 1)
                    eng.tensor_tensor(square_l[:, :], scale_b[:, :], square_h[:, :].bitcast(F32), ALU.subtract)\
                        .then_inc(pair_low, 1)
                elif kind == "headnorm":
                    p = a[0]
                    pair, gain = pair_of(p)
                    eng.wait_ge(pair_sum, p + 1)
                    eng.tensor_scalar(scale_b[:, :], sums[:, :], 1.0 / P, RMS_EPS, ALU.mult, ALU.add)\
                        .then_inc(pair_var, 1)
                    eng.wait_ge(pair_exp, p + 1)
                    step_(eng.scalar_tensor_tensor(out=scale_c[:, :], in0=scale_a[:, :], scalar=-0.5, in1=scale_a[:, :],
                                                   op0=ALU.mult, op1=ALU.mult))
                    step_(eng.tensor_tensor(scale_c[:, :], scale_c[:, :], scale_b[:, :], ALU.mult))
                    step_(eng.scalar_tensor_tensor(out=scale_c[:, :], in0=scale_c[:, :], scalar=1.5, in1=scale_a[:, :],
                                                   op0=ALU.add, op1=ALU.mult))
                    eng.scalar_tensor_tensor(out=flat(pair), in0=flat(pair), scalar=p_(gain), in1=scale_c[:, :],
                                             op0=ALU.mult, op1=ALU.mult).then_inc(pair_done, 1)
                    eng.wait_ge(pair_done, p + 1)
                elif kind == "forget":
                    eng.wait_ge(logits, 1)
                    step_(eng.tensor_copy(prod[0:FOX, :], sums[0:FOX, S:2 * S]))
                    eng.tensor_tensor(up[0:FOX, :], sums[0:FOX, 0:S], prod[0:FOX, :], ALU.add).then_inc(logit_rows, 1)
                elif kind == "forget_turn":
                    eng.wait_ge(logits, 2)
                    for b in range(TB):
                        step_(eng.tensor_tensor(fz[:, 0, b, :], sums[:, 8 * b:8 * b + FOX], p_("forget", 0, FOX), ALU.add))
                    step_(eng.tensor_scalar(fz[:, 1, :, :], fz[:, 0, :, :], -1.0, None, ALU.mult))
                    eng.tensor_tensor(fz[:, 1, :, :], fz[:, 1, :, :], fz[:, 0, :, :], ALU.min).then_inc(logit_in, 1)
                    eng.wait_ge(soft_ln, 1)
                    step_(eng.scalar_tensor_tensor(out=fz[:, 0, :, :], in0=fz[:, 0, :, :], scalar=0.0, in1=fz[:, 3, :, :],
                                                   op0=ALU.min, op1=ALU.subtract))
                    for h in range(FOX):
                        for b in range(TB):
                            ins = eng.tensor_scalar(lf_rows[:, h, b, :], ones, fz[:, 0, b, h:h + 1], -1.0,
                                                    ALU.mult, ALU.mult)
                    ins.then_inc(logf, 1)
                elif kind == "decay":
                    h = a[0]
                    if h == 0:
                        eng.wait_ge(cum_sum, 1)
                        for b in range(TB):
                            ins = eng.tensor_copy(cum[:, b, :], sums[:, 8 * b:8 * b + FOX])
                        ins.then_inc(cum_done, 1)
                    eng.wait_ge(decay_sum, h + 1)
                    eng.tensor_copy(decay[:, h, :], sums[:, 0:S]).then_inc(decay_done, 1)
                elif kind == "scores":
                    shifted_scores(a[0])
                elif kind == "exps":
                    softmax(a[0])
                elif kind == "mix_split":
                    layer, c = a
                    eng.wait_ge(mix_h, 4 * layer + MIX_ORDER[layer].index(c) + 1)
                    w = slice(4 * c, 4 * c + 4)
                    eng.tensor_tensor(mixs[:, w, S:2 * S], mix[:, w, :], mixs[:, w, 0:S].bitcast(F32), ALU.subtract)\
                        .then_inc(mix_l, 1)
                elif kind == "mixv":
                    n = a[0]
                    what, h, _, _, dest = head_spec(n)
                    eng.wait_ge(mixed, n + 1)
                    if what == "mla":
                        eng.wait_ge(gated, gates_done(n // HEADS, dest))
                        eng.tensor_tensor(mix[:, dest, :], head_ps[n % 2][:, 0:S], mix[:, dest, :], ALU.mult)\
                            .then_inc(head_out, 1)
                    else:
                        eng.tensor_copy(mix[:, dest, :], head_ps[n % 2][:, 0:S]).then_inc(head_out, 1)

            def shifted_scores(n):
                what, h, _, _, _ = head_spec(n)
                pr, sc = prob[:, n % 2, :, :], score[n % 2]
                eng.wait_ge(scores_done, n + 1)
                if n >= 2:
                    eng.wait_ge(turns, n - 1)
                if n == 0:
                    eng.wait_ge(masks_in, 16)
                if what == "fox":
                    eng.wait_ge(decay_done, FOX)
                    for b in range(TB):
                        w = keys_seen(what, b)
                        ins = eng.scalar_tensor_tensor(out=pr[:, b, 0:w], in0=sc[:, b, 0:w], scalar=cum[:, b, h:h + 1],
                                                       in1=decay[:, h, 0:w], op0=ALU.add, op1=ALU.add)
                    step_(ins)
                slope = float(np.float32(2.0 ** (-8.0 * (h + 1) / SWA)))
                for b in range(TB):
                    w = keys_seen(what, b)
                    to, from_ = pr[:, b, 0:w], sc[:, b, 0:w]
                    if what == "mla":
                        ins = eng.scalar_tensor_tensor(out=to, in0=from_, scalar=MLA_SCALE, in1=causal[:, b, 0:w],
                                                       op0=ALU.mult, op1=ALU.add)
                    elif what == "mem":
                        ins = eng.tensor_copy(to, from_)
                    elif what == "fox":
                        ins = eng.tensor_tensor(to, to, causal[:, b, 0:w], ALU.add)
                    else:
                        ins = eng.scalar_tensor_tensor(out=to, in0=dist[:, b, 0:w], scalar=-slope, in1=from_,
                                                       op0=ALU.mult, op1=ALU.add)
                    ins.then_inc(shifted, 1)
                eng.wait_ge(shifted, TB * (n + 1))
                for b in range(TB):
                    neg = stat[:, n % 2, b:b + 1]
                    ins = eng.tensor_reduce(neg, pr[:, b, 0:keys_seen(what, b)], AX.X, ALU.max, negate=True)
                    if what == "swa":
                        step_(ins)
                        ins = eng.tensor_scalar(neg, neg, neg_sink[:, h:h + 1], None, ALU.min)
                    ins.then_inc(negmax, 1)

            def softmax(n):
                what, h, _, _, _ = head_spec(n)
                pr = prob[:, n % 2, :, :]
                total, inv = stat[:, n % 2, 2:4], stat[:, n % 2, 6:8]
                eng.wait_ge(exps, TB * (n + 1))
                if what == "swa":
                    eng.wait_ge(sink_exp, h + 1)
                    step_(eng.tensor_tensor(total, total, stat[:, n % 2, 4:6], ALU.add))
                step_(eng.reciprocal(inv, total))
                for b in range(TB):
                    w = keys_seen(what, b)
                    eng.tensor_scalar(pr[:, b, 0:w], pr[:, b, 0:w], inv[:, b:b + 1], None, ALU.mult).then_inc(probs, 1)

            def low_and_squares(n):
                for kt in range(*CUTS[n]):
                    split_low_of("ln1", kt, "ffn1_g")
                if n > 1:
                    lo, hi = CUTS[n]
                    eng.wait_ge(squared, hi)
                    step_(eng.tensor_tensor(square[:, 0:4, :], square[:, 0:4, :], square[:, lo:hi, :], ALU.add))

            def norm(name):
                if name == "ffn2":
                    split_low_of(name, KT - 1, "ffn2_g")
                    return
                if name in ("ln0", "ln1"):
                    moments(name, KT - 1, KT)
                if name == "mem":
                    split_low(REG["mem_k"], 0, None)
                variance_of(name)
                inv = scale_a[:, 0:S]
                step_(eng.reciprocal(inv, scale_b[:, 0:S]))
                if name in LAYER_NORMS:
                    for n, (lo, hi) in enumerate(CUTS):
                        e = normed[:, lo:hi, :]
                        wide = [v.unsqueeze(1).to_broadcast([P, hi - lo, S]) for v in (mean[:, :], inv)]
                        step_(eng.tensor_tensor(e, e, wide[0], ALU.subtract))
                        eng.tensor_tensor(e, e, wide[1], ALU.mult).then_inc(normed_t, 1)
                        if name == "ln1" and n:
                            low_and_squares(n - 1)
                        for kt in range(lo, hi) if name != "ln1" else []:
                            if kt % 2:
                                eng.wait_ge(normed_t, NORMED_T[name] + n + 1)
                                g, b = ("emb_g", "emb_b") if name == "emb" else ("ln_g", "ln_b")
                                eng.tensor_scalar(x[:, kt, :], normed[:, kt, :], p_(g, kt), p_(b, kt), ALU.mult, ALU.add)\
                                    .then_inc(embedded_v, 1)
                    if name == "ln1":
                        low_and_squares(len(CUTS) - 1)
                        fold = square[:, 0:2, :]
                        step_(eng.tensor_tensor(fold, fold, square[:, 2:4, :], ALU.add))
                        added("ffn1", eng.tensor_tensor(moment[:, S:2 * S], square[:, 0, :], square[:, 1, :], ALU.add), True)
                    return
                gain, src = ("mem_g", memx) if name == "mem" else ("mix_g", x)
                for kt in range(KT):
                    eng.scalar_tensor_tensor(out=normed[:, kt, :], in0=src[:, kt, :], scalar=p_(gain, kt),
                                             in1=inv, op0=ALU.mult, op1=ALU.mult).then_inc(normed_t, 1)
                    if kt > 2:
                        split_low_of(name, kt - 3)
                for kt in range(KT - 3, KT):
                    split_low_of(name, kt)

            def rope_angles():
                eng.wait_ge(pos_in, 16)
                eng.wait_ge(par_in, 16)
                a0, a1, turns_, r, m = (ang[:, n, :] for n in range(5))
                step_(eng.tensor_copy(r, pos[:, :]))
                step_(eng.tensor_scalar(a0, r, p_("inv_freq"), None, ALU.mult))
                step_(eng.tensor_scalar(turns_, a0, INV_2PI, MAGIC, ALU.mult, ALU.add))
                step_(eng.tensor_scalar(turns_, turns_, -MAGIC, None, ALU.add))
                for part in (PI_A, PI_B, PI_C):
                    step_(eng.scalar_tensor_tensor(out=a0, in0=turns_, scalar=-part, in1=a0, op0=ALU.mult, op1=ALU.add))
                step_(eng.tensor_scalar(a1, a0, float(np.pi / 2), None, ALU.add))
                step_(eng.tensor_scalar(m, a1, PI_IN, -2 * float(np.pi), ALU.is_gt, ALU.mult))
                step_(eng.tensor_tensor(a1, a1, m, ALU.add))
                step_(eng.tensor_scalar(a0, a0, PI_IN, -PI_IN, ALU.min, ALU.max))
                step_(eng.tensor_scalar(a0, a0, p_("rope_sign"), None, ALU.mult))
                eng.tensor_scalar(a1, a1, PI_IN, -PI_IN, ALU.min, ALU.max).then_inc(angles, 1)

            def between(name):
                if name == "mem_k":
                    eng.wait_ge(par_in, 16)
                    step_(eng.tensor_copy(ones_r[:, :], ones))
                    for g in ("fox_q", "swa_q", "mem_q"):
                        step_(eng.tensor_scalar(p_(g), p_(g), HEAD_SCALE, None, ALU.mult))
                    step_(eng.tensor_scalar(neg_sink[:, :], p_("sinks", 0, SWA), -1.0, None, ALU.mult))
                if name == "in_a0":
                    eng.wait_ge(wf_in, 16)
                    flat_h = wfh[:, :, :].rearrange("p k f -> p (k f)")
                    step_(eng.tensor_copy(flat_h, wf[:, :]))
                    eng.tensor_tensor(wfl[:, :, :].rearrange("p k f -> p (k f)"), wf[:, :], flat_h.bitcast(F32),
                                      ALU.subtract).then_inc(wf_split, 1)
                for step in after_steps(name):
                    do(*step)
                if mix_split(name) is not None:
                    n = mix_split(name)
                    for c in MIX_ORDER[n] if n == DEPTH else MIX_ORDER[n][3:]:
                        do("mix_split", n, c)
                for n in norms_before(name):
                    norm(n)
                if name in ("down11", "mixout"):
                    step_(eng.memset((late_moment if name == "down11" else moment)[:, :], 0.0))

            walk(eng, slot, between, chain)

        @block.gpsimd
        def _(eng):
            def split_low(r, k, i):
                s = r.s0 + k
                w = slice(0, r.pieces[0] * P)
                eng.wait_ge(highs, val(2 * s + 1, 8, i))
                eng.tensor_tensor(low[:, s % SPLIT, w], raw[:, s % RAW, w], high[:, s % SPLIT, w].bitcast(F32),
                                  ALU.subtract).then_inc(lows_a, 1)

            def slot(r, k, i):
                nxt = following(r, k, i)
                if nxt and not (k == 0 and norms_before(r.name)):
                    split_low(*nxt)

            def between(name):
                if name == "mem_k":
                    split_low(REG[name], 0, None)
                if norms_before(name):
                    split_low(REG[name], 1, None)
                for n in norms_before(name):
                    y = x if n in LAYER_NORMS else normed
                    for kt in range(KT):
                        who, _ = low_count(n, kt)
                        if n == "ln1":
                            eng.wait_ge(embedded, kt + 1)
                            eng.tensor_tensor(square[:, kt, :], x[:, kt, :], x[:, kt, :], ALU.mult).then_inc(squared, 1)
                        if who == "g":
                            eng.wait_ge(split_h, high_count(n, kt))
                            if n in LAYER_NORMS and kt % 2:
                                eng.wait_ge(embedded_v, KT // 2 * LAYER_NORMS.index(n) + kt // 2 + 1)
                            eng.tensor_tensor(xs[:, kt, S:2 * S], y[:, kt, :], xs[:, kt, 0:S].bitcast(F32),
                                              ALU.subtract).then_inc(split_l["g"], 1)

            walk(eng, slot, between)


class Chain:

    def __init__(self, eng, sem):
        self.eng, self.sem, self.n, self.i, self.per = eng, sem, 0, None, 0

    def enter(self, i, r):
        self.i, self.per, self.start = i, 8 if r.kind == "tile" else 6 if r.name == "down11" else 2, self.n

    def leave(self, runs, r):
        assert self.n - self.start == self.per, (r.name, self.n - self.start)
        self.n, self.i = self.start + runs * self.per, None

    def step(self, ins):
        ins.then_inc(self.sem, 1)
        self.n += 1
        self.eng.wait_ge(self.sem, self.n if self.i is None else self.i * self.per + self.n)


def _tiles(w, columns=None):
    w = w if columns is None else w[:, columns]
    k, n = w.shape
    return np.ascontiguousarray(w.reshape(k // P, P, n // P, P).transpose(2, 1, 0, 3)).reshape(n // P, P, k)


def _rows(w, per, width):
    k, n = w.shape
    a = w.reshape(k // P // per, per, P, n // width, width).transpose(3, 0, 2, 1, 4)
    return np.ascontiguousarray(a).reshape(-1, P, per * width)


def _cols(v):
    return np.asarray(v).reshape(-1, P).T


def _all(v):
    return np.broadcast_to(np.asarray(v).reshape(1, -1), (P, np.size(v)))


def layout(inp):
    a = {k: np.asarray(v) for k, v in inp.items()}
    arange = np.arange
    out = {}
    starts = dict(zip(("q", "kv", "kr", "g", "p", "gp", "ch", "cb", "cc", "gc"),
                      np.cumsum([0, QLAT, KVLAT, ROPE, 1024, 512, 512, 512, 512, 512])))
    half = ROPE // 2
    first = [arange(QLAT + KVLAT), starts["kr"] + arange(P) % ROPE, starts["kr"] + (arange(P) + half) % ROPE,
             starts["g"] + arange(1024)]
    rest = [starts[n] + g * P + arange(P) for names in (("p", "gp"), ("gc", "ch", "cc", "cb"))
            for g in range(GROUPS) for n in names]
    columns = np.concatenate(first + rest)
    out["w_in"] = np.concatenate([_tiles(a["w_in"][l], columns) for l in range(DEPTH)])
    per = P + ROPE
    nope = (arange(HEADS)[:, None] * per + arange(P)).ravel()
    rope = [(h + HEADS // 2 * (arange(P) // ROPE)) * per + P + arange(P) % ROPE for h in range(HEADS // 2)]
    uq = [_tiles(a["w_uq"][l], np.concatenate([nope] + rope)) for l in range(DEPTH)]
    out["w_uq"] = np.concatenate([u.reshape(4, 3, P, QLAT).transpose(0, 2, 1, 3).reshape(4, P, 3 * QLAT) for u in uq])
    kcols = (arange(HEADS)[:, None] * 2 * P + arange(P)).ravel()
    out["w_uk"] = np.stack([_tiles(a["w_ukv"][l], kcols).transpose(1, 0, 2).reshape(P, -1) for l in range(DEPTH)])
    out["w_uv"] = np.concatenate([_rows(a["w_ukv"][l][:, kcols + P], KKV, 512) for l in range(DEPTH)])
    out["w_pool"] = np.ascontiguousarray(a["w_pool"].transpose(0, 2, 1, 3)).reshape(DEPTH, P, GROUPS * P)
    out["w_out"] = np.concatenate([_tiles(a["w_out"][l]) for l in range(DEPTH)])
    for part in ("1", "2"):
        up = np.stack([_tiles(a[f"ffn{part}_{n}_2"][0]) for n in ("gate", "up")], 1)
        out["w_up" + part] = up.reshape(2 * FT, P, D)
        down = a[f"ffn{part}_down_2"][0].reshape(CHUNKS, 2, HALF, P, KT, P).transpose(0, 4, 1, 3, 2, 5)
        out["w_down" + part] = np.ascontiguousarray(down).reshape(CHUNKS * KT * 2, P, HALF * P)
    w = a["w_in_2"][0]
    cuts = np.cumsum([0, FOX * P, FOX * P, FOX * P, FOX, SWA * P, SWA_KV * P, SWA_KV * P, MEM * P])
    fq, fk, fv, fl, sq, sk, sv, mq = (arange(cuts[n], cuts[n + 1]) for n in range(8))
    out["w_nat"] = _rows(w[:, np.concatenate([sv, fv])], 4, 512)
    order = [mq, sk, sq]
    for n in range(FOX // 2):
        order += [fk[2 * P * n:2 * P * (n + 1)], fq[2 * P * n:2 * P * (n + 1)]]
    out["w_heads"] = _tiles(w, np.concatenate(order))
    out["wf"] = np.ascontiguousarray(w[:, fl].reshape(KT, P, FOX).transpose(1, 0, 2)).reshape(P, KT * FOX)
    out["w_mixout"] = _tiles(a["w_out_2"][0])
    out["w_memk"] = _tiles(a["w_mem_k_2"][0])
    out["w_memv"] = _rows(a["w_mem_v_2"][0], 4, 512)
    for name, src in (("x", "x"), ("mem", "mem_2")):
        out[name] = np.ascontiguousarray(a[src][0].T.reshape(KT, P, S).transpose(1, 0, 2))
    out["positions"] = np.ascontiguousarray(np.broadcast_to(a["positions"], (P, S)))
    tok = arange(S)
    upto = (tok[:, None] <= tok[None, :]).astype(np.float32).reshape(TB, P, S).transpose(1, 0, 2).reshape(P, -1)
    gap = tok[:, None] - tok[None, :]
    causal = np.where(gap >= 0, 0.0, NEG)
    far = np.where((gap >= 0) & (gap < SWA_WINDOW), gap, FAR)
    causal, far = (m.astype(np.float32).reshape(TB, P, S).transpose(1, 0, 2).reshape(P, -1) for m in (causal, far))
    inv_freq = np.float32(10000.0) ** (-(arange(P) % half).astype(np.float32) / np.float32(half))
    values = dict(
        emb_g=_cols(a["emb_ln_g"]), emb_b=_cols(a["emb_ln_b"]), ffn1_g=_cols(a["ffn1_norm_2"]),
        mix_g=_cols(a["mix_norm_2"]), mem_g=_cols(a["mem_norm_2"]), ffn2_g=_cols(a["ffn2_norm_2"]),
        ln_g=_cols(a["ln_g"]), ln_b=_cols(a["ln_b"]), b_out=_cols(a["b_out"]), q_g=_cols(a["q_norm_g"]),
        kv_g=_cols(a["kv_norm_g"]), pool_s=_cols(a["pool_scale"]), conv=_cols(a["conv_w"]),
        fox_q=_cols(a["fox_q_gain_2"]), fox_k=_cols(a["fox_k_gain_2"]), swa_q=_cols(a["swa_q_gain_2"]),
        swa_k=_cols(a["swa_k_gain_2"]), mem_q=_cols(a["mem_q_gain_2"]), mem_k=_cols(a["mem_k_gain_2"]),
        forget=_all(a["forget_bias_2"]), sinks=_all(a["swa_sinks_2"]),
        rope_sign=np.where(arange(P) % ROPE < half, -1, 1).astype(np.float32).reshape(P, 1),
        inv_freq=inv_freq.reshape(P, 1).astype(np.float32),
        count=_all(1 / np.arange(1, max(WINDOWS) + 1, dtype=np.float32)),
        ident=np.eye(P, dtype=np.float32), ones=np.ones((P, P), np.float32), upto=upto, causal=causal, dist=far)
    out["par"] = np.ascontiguousarray(np.concatenate([values[n] for n, _ in COLUMNS], 1))
    return out


def kernel(**inputs):
    import concourse.bacc as bacc
    from concourse.bass_utils import run_bass_kernel_spmd

    arrays = layout(inputs)
    nc = bacc.Bacc("TRN2", target_bir_lowering=False, num_devices=1, dynamic_dma_scratch_size=1024)
    t = {n: nc.dram_tensor(n + "_dram", v.shape, mybir.dt.from_np(v.dtype), kind="ExternalInput").ap()
         for n, v in arrays.items()}
    t["out"] = nc.dram_tensor("out_dram", (P, KT, S), F32, kind="ExternalOutput").ap()
    build(nc, t)
    r = run_bass_kernel_spmd(nc, [{n + "_dram": v for n, v in arrays.items()}], core_ids=[0])
    out = np.asarray(r.results[0]["out_dram"])
    return np.ascontiguousarray(out.transpose(2, 1, 0)).reshape(1, S, D)
```
